# Optimizing a Trainium2 kernel written in Bass

```python
import math
import jax, jax.numpy as jnp
from jax import lax
import numpy as np

D_MODEL = 2048
BATCH = 1
SEQ = 256
DEPTH = 2

CHUNK = 64
Q_BLOCK = 128
EPS = 1e-6

SB_HEADS = 4
SB_HEAD_DIM = 128
SB_WIDTH = SB_HEADS * SB_HEAD_DIM

MLA_HEADS = 8
MLA_NOPE = 128
MLA_ROPE = 64
MLA_QK = MLA_NOPE + MLA_ROPE
MLA_V = 128
MLA_WIDTH = MLA_HEADS * MLA_V
Q_LORA = 512
KV_LORA = 512
ROPE_THETA = 10000.0

RW_HEADS = 8
RW_HEAD_DIM = 64
RW_WIDTH = RW_HEADS * RW_HEAD_DIM
DECAY_LORA = 64
ICL_LORA = 64
RW_GN_EPS = 64e-5
RW_SHIFT_WIDTH = 3 * RW_WIDTH + DECAY_LORA + ICL_LORA

N_BRANCH = 3
SB_COLS = 4 * SB_WIDTH
MLA_COLS = Q_LORA + KV_LORA + MLA_ROPE + MLA_WIDTH
RW_COLS = RW_SHIFT_WIDTH + RW_WIDTH
GATE_COLS = N_BRANCH * D_MODEL
N_IN = SB_COLS + MLA_COLS + RW_COLS + GATE_COLS

kernel_name = "hybrid_sb_mla_rwkv7_gated_merge"

def rms_norm(x, g, eps=EPS):
    xf = x.astype(jnp.float32)
    y = xf * lax.rsqrt(jnp.mean(xf * xf, axis=-1, keepdims=True) + eps)
    return (y * g.astype(jnp.float32)).astype(x.dtype)

def split_cols(t, sizes):
    out, start = [], 0
    for n in sizes:
        out.append(t[..., start:start + n])
        start += n
    return out

def rope(x, pos):
    half = x.shape[-1] // 2
    freqs = ROPE_THETA ** (-jnp.arange(half, dtype=jnp.float32) / half)
    ang = pos.astype(jnp.float32)[:, None] * freqs[None, :]
    cos = jnp.cos(ang)[None, :, None, :]
    sin = jnp.sin(ang)[None, :, None, :]
    x1, x2 = x[..., :half], x[..., half:]
    return jnp.concatenate([x1 * cos - x2 * sin, x1 * sin + x2 * cos], axis=-1).astype(x.dtype)

def stick_breaking_attention(q, k, v):
    S, Dh = q.shape[1], q.shape[-1]
    scale = Dh ** -0.5
    outs = []
    for i in range(S // Q_BLOCK):
        q0, q1 = i * Q_BLOCK, (i + 1) * Q_BLOCK
        z = jnp.einsum('bqhd,bkhd->bhqk', q[:, q0:q1], k[:, :q1]).astype(jnp.float32) * scale
        t_pos = q0 + jnp.arange(Q_BLOCK)
        s_pos = jnp.arange(q1)
        causal = s_pos[None, :] < t_pos[:, None]
        log_beta = jax.nn.log_sigmoid(z)
        log_fail = jnp.where(causal, log_beta - z, 0.0)
        between = lax.cumsum(log_fail, axis=3, reverse=True) - log_fail
        w = jnp.where(causal, jnp.exp(log_beta + between), 0.0)
        outs.append(jnp.einsum('bhqk,bkhd->bqhd', w.astype(v.dtype), v[:, :q1]))
    return jnp.concatenate(outs, axis=1)

def chunk_causal_softmax_attention(q, k, v):
    S, Dh = q.shape[1], q.shape[-1]
    scale = Dh ** -0.5
    outs = []
    for i in range(S // Q_BLOCK):
        q0, q1 = i * Q_BLOCK, (i + 1) * Q_BLOCK
        s = jnp.einsum('bqhd,bkhd->bhqk', q[:, q0:q1], k[:, :q1]).astype(jnp.float32) * scale
        t_chunk = (q0 + jnp.arange(Q_BLOCK)) // CHUNK
        s_chunk = jnp.arange(q1) // CHUNK
        mask = s_chunk[None, :] <= t_chunk[:, None]
        p = jax.nn.softmax(jnp.where(mask, s, -jnp.inf), axis=-1)
        outs.append(jnp.einsum('bhqk,bkhd->bqhd', p.astype(v.dtype), v[:, :q1]))
    return jnp.concatenate(outs, axis=1)

def rwkv7_scan(r, decay, k, v, a_vec, b_vec):
    B, S, H, N = r.shape

    def step(state, inp):
        r_t, w_t, k_t, v_t, a_t, b_t = inp
        sa = jnp.einsum('bhij,bhj->bhi', state, a_t)
        state = (state * w_t[:, :, None, :] + sa[..., None] * b_t[:, :, None, :]
                 + v_t[..., None] * k_t[:, :, None, :])
        return state, jnp.einsum('bhij,bhj->bhi', state, r_t)

    xs = tuple(jnp.moveaxis(t, 1, 0) for t in (r, decay, k, v, a_vec, b_vec))
    state0 = jnp.zeros((B, H, N, N), jnp.float32)
    _, out = lax.scan(step, state0, xs)
    return jnp.moveaxis(out, 0, 1)

def rwkv7_mixer(r, k, v, w_down, a_down, w0, w_up, a0, a_up, k_k, k_a, r_k, gn_g, gn_b):
    B, S, _ = r.shape
    dt = r.dtype
    f32 = jnp.float32
    heads = lambda t: t.astype(f32).reshape(B, S, RW_HEADS, RW_HEAD_DIM)
    w_log = -jax.nn.softplus(-(w0 + jnp.tanh(w_down) @ w_up).astype(f32)) - 0.5
    decay = jnp.exp(-jnp.exp(w_log))
    a = jax.nn.sigmoid((a0 + a_down @ a_up).astype(f32))
    kk = heads(k * k_k)
    kk = kk / jnp.maximum(jnp.sqrt(jnp.sum(kk * kk, axis=-1, keepdims=True)), 1e-12)
    k_mod = k.astype(f32) * (1.0 + (a - 1.0) * k_a.astype(f32))
    rh, kh, vh, ah = heads(r), heads(k_mod), heads(v), heads(a)
    o = rwkv7_scan(rh, heads(decay), kh, vh, -kk, kk * ah)
    mu = jnp.mean(o, axis=-1, keepdims=True)
    var = jnp.mean(jnp.square(o - mu), axis=-1, keepdims=True)
    o = ((o - mu) * lax.rsqrt(var + RW_GN_EPS)).reshape(B, S, RW_WIDTH)
    o = o * gn_g.astype(f32) + gn_b.astype(f32)
    bonus = jnp.sum(rh * kh * r_k.astype(f32), axis=-1, keepdims=True) * vh
    return (o + bonus.reshape(B, S, RW_WIDTH)).astype(dt)

def setup_inputs(seed: int = 0) -> dict:
    key = jax.random.key(seed)
    ks = iter(jax.random.split(key, 32))
    L = DEPTH
    nrm = lambda shape, scale: jax.random.normal(next(ks), shape, jnp.float32) * scale
    gain = lambda shape: 1.0 + 0.1 * jax.random.normal(next(ks), shape, jnp.float32)
    return {
        "x": nrm((BATCH, SEQ, D_MODEL), 1.0),
        "norm_g": gain((L, D_MODEL)),
        "w_in": nrm((L, D_MODEL, N_IN), D_MODEL ** -0.5),
        "mla_q_norm_g": gain((L, Q_LORA)),
        "mla_kv_norm_g": gain((L, KV_LORA)),
        "mla_w_uq": nrm((L, Q_LORA, MLA_HEADS * MLA_QK), Q_LORA ** -0.5),
        "mla_w_ukv": nrm((L, KV_LORA, MLA_HEADS * (MLA_NOPE + MLA_V)), KV_LORA ** -0.5),
        "mla_qn_g": gain((L, MLA_QK)),
        "mla_kn_g": gain((L, MLA_QK)),
        "rw_mu": jax.random.uniform(next(ks), (L, RW_SHIFT_WIDTH), jnp.float32),
        "rw_w0": jax.random.uniform(next(ks), (L, RW_WIDTH), jnp.float32, minval=-6.0, maxval=-1.0),
        "rw_w_up": nrm((L, DECAY_LORA, RW_WIDTH), 0.5 * DECAY_LORA ** -0.5),
        "rw_a0": nrm((L, RW_WIDTH), 0.5),
        "rw_a_up": nrm((L, ICL_LORA, RW_WIDTH), ICL_LORA ** -0.5),
        "rw_k_k": 0.85 + 0.05 * jax.random.normal(next(ks), (L, RW_WIDTH), jnp.float32),
        "rw_k_a": 1.0 + 0.05 * jax.random.normal(next(ks), (L, RW_WIDTH), jnp.float32),
        "rw_r_k": nrm((L, RW_HEADS, RW_HEAD_DIM), 0.1),
        "rw_gn_g": gain((L, RW_WIDTH)),
        "rw_gn_b": nrm((L, RW_WIDTH), 0.02),
        "w_br_sb": nrm((L, SB_WIDTH, D_MODEL), SB_WIDTH ** -0.5),
        "w_br_mla": nrm((L, MLA_WIDTH, D_MODEL), MLA_WIDTH ** -0.5),
        "w_br_rw": nrm((L, RW_WIDTH, D_MODEL), RW_WIDTH ** -0.5),
        "w_out": nrm((L, D_MODEL, D_MODEL), D_MODEL ** -0.5),
    }

def reference(x, norm_g, w_in, mla_q_norm_g, mla_kv_norm_g, mla_w_uq, mla_w_ukv, mla_qn_g, mla_kn_g,
              rw_mu, rw_w0, rw_w_up, rw_a0, rw_a_up, rw_k_k, rw_k_a, rw_r_k, rw_gn_g, rw_gn_b,
              w_br_sb, w_br_mla, w_br_rw, w_out):
    B, S, _ = x.shape
    pos = jnp.arange(S)
    for l in range(DEPTH):
        h = rms_norm(x, norm_g[l])
        p = h @ w_in[l]
        p_sb, p_mla, p_rw, p_gate = split_cols(p, (SB_COLS, MLA_COLS, RW_COLS, GATE_COLS))

        sq, sk, sv, sg = split_cols(p_sb, (SB_WIDTH,) * 4)
        sbh = lambda t: t.reshape(B, S, SB_HEADS, SB_HEAD_DIM)
        y_sb = stick_breaking_attention(sbh(sq), sbh(sk), sbh(sv)).reshape(B, S, SB_WIDTH)
        y_sb = y_sb * jax.nn.silu(sg)

        c_q, c_kv, k_rope, mg = split_cols(p_mla, (Q_LORA, KV_LORA, MLA_ROPE, MLA_WIDTH))
        q = (rms_norm(c_q, mla_q_norm_g[l]) @ mla_w_uq[l]).reshape(B, S, MLA_HEADS, MLA_QK)
        kv = (rms_norm(c_kv, mla_kv_norm_g[l]) @ mla_w_ukv[l]).reshape(B, S, MLA_HEADS, MLA_NOPE + MLA_V)
        k_nope, v_m = kv[..., :MLA_NOPE], kv[..., MLA_NOPE:]
        k = jnp.concatenate(
            [k_nope, jnp.broadcast_to(k_rope[:, :, None, :], (B, S, MLA_HEADS, MLA_ROPE))], axis=-1)
        q = rms_norm(q, mla_qn_g[l])
        k = rms_norm(k, mla_kn_g[l])
        q = jnp.concatenate([q[..., :MLA_NOPE], rope(q[..., MLA_NOPE:], pos)], axis=-1)
        k = jnp.concatenate([k[..., :MLA_NOPE], rope(k[..., MLA_NOPE:], pos)], axis=-1)
        y_mla = chunk_causal_softmax_attention(q, k, v_m).reshape(B, S, MLA_WIDTH)
        y_mla = y_mla * jax.nn.silu(mg)

        rw_main, rg = split_cols(p_rw, (RW_SHIFT_WIDTH, RW_WIDTH))
        prev = jnp.pad(rw_main, ((0, 0), (1, 0), (0, 0)))[:, :-1]
        rw_main = rw_main + rw_mu[l] * (prev - rw_main)
        rr, rk, rv, wd, ad = split_cols(rw_main, (RW_WIDTH,) * 3 + (DECAY_LORA, ICL_LORA))
        y_rw = rwkv7_mixer(rr, rk, rv, wd, ad, rw_w0[l], rw_w_up[l], rw_a0[l], rw_a_up[l],
                           rw_k_k[l], rw_k_a[l], rw_r_k[l], rw_gn_g[l], rw_gn_b[l])
        y_rw = y_rw * jax.nn.silu(rg)

        g_sb, g_mla, g_rw = split_cols(jax.nn.sigmoid(p_gate), (D_MODEL,) * N_BRANCH)
        merged = (g_sb * (y_sb @ w_br_sb[l]) + g_mla * (y_mla @ w_br_mla[l])
                  + g_rw * (y_rw @ w_br_rw[l]))
        x = x + merged @ w_out[l]
    return x


_drawn_inputs = setup_inputs


def setup_inputs(seed=0):
    import zlib

    import numpy as np

    out = dict(_drawn_inputs(seed))
    spreads = {}
    factors = {'mla_q_norm_g': 8.0,
     'mla_kv_norm_g': 6.614,
     'mla_qn_g': 8.0,
     'mla_kn_g': 8.0,
     'rw_w_up': 5.262,
     'rw_k_k': 3.286,
     'rw_gn_b': 6.425}
    for name, (base, spread) in spreads.items():
        noise = np.random.default_rng([zlib.crc32(name.encode()), seed]).standard_normal(out[name].shape)
        drawn = base * np.exp(spread * noise) if base else spread * noise
        out[name] = __import__('jax').numpy.asarray(drawn.astype(out[name].dtype))
    for name, factor in factors.items():
        out[name] = (out[name] * factor).astype(out[name].dtype)
    return out
```

```python
import numpy as np
import concourse.bass as bass
from concourse import mybir
from contextlib import ExitStack

F32 = mybir.dt.float32
U32 = mybir.dt.uint32
ALU = mybir.AluOpType
ACT = mybir.ActivationFunctionType
X = mybir.AxisListType.X

DEPTH, SEQ, DM = 2, 256, 2048
P = 128
HALVES = SEQ // P
KD = DM // P
SBH, MLH, RWH = 4, 8, 8
NOPE, ROPE, VD = 128, 64, 128
QK = NOPE + ROPE
LORA = 512
RWW = 512
EPS = 1e-6
C_SB = 0
C_CQ = 2048
C_CKV = C_CQ + LORA
C_KR = C_CKV + LORA
C_MG = C_KR + ROPE
C_RW = C_MG + MLH * VD
C_WD = C_RW + 3 * RWW
C_RG = C_WD + 128
C_GATE = C_RG + RWW
N_IN = C_GATE + 3 * DM
DECAY = float(np.exp(-0.5))
MID = P // 2 - 1
LEVELS = 6
KC = 2
RING = 4
ARENA = 35200
SB_SCALE = 128.0 ** -0.5
ML_SCALE = QK ** -0.5
MASKED = -1e30

K_ID, K_INC, K_EXC, K_NTRI, K_NONE, K_RWM, K_LEV = 0, 128, 256, 384, 512, 640, 1152
K_COS = K_LEV + (LEVELS + 1) * 128
K_SIN = K_COS + 64
K_COL = K_SIN + 64
K_LATE = K_COL + 2
K_EARLY = K_LATE + P
K_END = K_EARLY + P


def constants():
    c = np.zeros((P, K_END), np.float32)
    i = np.arange(P)
    row, col = i[:, None], i[None, :]
    c[:, K_ID:K_ID + P] = row == col
    past_mid = (row <= MID).astype(np.float32)
    c[:, K_INC:K_INC + P] = -DECAY * ((row <= col).astype(np.float32) - past_mid)
    c[:, K_EXC:K_EXC + P] = -DECAY * ((row < col).astype(np.float32) - past_mid)
    c[:, K_NTRI:K_NTRI + P] = -(row >= col).astype(np.float32)
    c[:, K_NONE:K_NONE + P] = -1.0
    strict, incl = (row < col), (row <= col)
    c[:, K_RWM:K_RWM + 512] = np.concatenate([strict, incl, strict, incl], 1)
    for n in range(LEVELS + 1):
        b = 2 ** n
        c[:, K_LEV + n * P:K_LEV + (n + 1) * P] = (row // (2 * b) == col // (2 * b)) & (row // b < col // b)
    half = ROPE // 2
    freqs = (np.float32(10000.0) ** (-np.arange(half, dtype=np.float32) / np.float32(half))).astype(np.float32)
    ang = np.arange(SEQ, dtype=np.float32)[:, None] * freqs[None, :]
    for h in range(HALVES):
        c[:, K_COS + h * half:K_COS + (h + 1) * half] = np.cos(ang[h * P:(h + 1) * P])
        c[:, K_SIN + h * half:K_SIN + (h + 1) * half] = np.sin(ang[h * P:(h + 1) * P])
    c[:, K_COL] = -DECAY * (i > MID)
    c[:, K_COL + 1] = -DECAY * (i <= MID)
    c[:, K_LATE + 64:K_LATE + P] = 1.0
    c[:, K_EARLY:K_EARLY + 64] = MASKED
    return c


def groups():
    def wide(name, c0):
        return [(name, "w_in", c0, 512, KD)]

    def pair(p):
        return [(f"uq{p}", "uq", p * 2 * QK, 2 * QK, 4), (f"ukv{p}", "ukv", p * 512, 512, 4)]

    gates = [wide(f"gate{n}", C_GATE + n * 512)[0] for n in range(12)]
    g = [("wk", "w_in", C_KR, 192, KD)]
    g += wide("rr", C_RW) + wide("rk", C_RW + 512) + wide("rv", C_RW + 1024)
    g += wide("cq", C_CQ) + wide("ckv", C_CKV)
    g += gates[:9] + pair(0) + pair(1) + wide("sq", C_SB) + wide("sk", C_SB + 512) + pair(2)
    g += wide("sv", C_SB + 1024) + pair(3) + gates[9:]
    g += wide("rg", C_RG) + wide("sg", C_SB + 1536) + wide("mg0", C_MG) + wide("mg1", C_MG + 512)
    for j in range(4):
        g += [(f"bs{j}", "bs", j * 512, 512, 4), (f"bm{j}", "bm", j * 512, 512, 8), (f"br{j}", "br", j * 512, 512, 4)]
    g += [(f"o{j}", "w_out", j * 512, 512, KD) for j in range(4)]
    return g


GROUPS = groups()
CHUNKS = [(gi, c) for gi, g in enumerate(GROUPS) for c in range(g[4] // KC)]
GI = {g[0]: i for i, g in enumerate(GROUPS)}
END = {g[0]: sum(x[4] // KC for x in GROUPS[:i + 1]) for i, g in enumerate(GROUPS)}

AT_LORA = END["rv"] + 2
AT_Z = AT_LORA + 4
AT_LATENTS = END["ckv"] + 2
AT_DECAY = AT_LATENTS + 4
AT_PAIRS = AT_DECAY + 3
RW_BEATS, ML_BEATS, SB_BEATS = 21, 9, 4
BEATS = 4 * RW_BEATS + 4 * ML_BEATS + SBH * SB_BEATS


def beat_at(n):
    return AT_PAIRS + n * (END["gate11"] - AT_PAIRS) // BEATS


RW_PE, RW_ACT, RW_DVE = 21, 12, 11


def program(nc, x, norm_g, w_in, mla_q_norm_g, mla_kv_norm_g, mla_w_uq, mla_w_ukv, mla_qn_g, mla_kn_g,
            rw_mu, rw_w0, rw_w_up, rw_a0, rw_a_up, rw_k_k, rw_k_a, rw_r_k, rw_gn_g, rw_gn_b,
            w_br_sb, w_br_mla, w_br_rw, w_out, consts, out, spill):
    weights = dict(w_in=w_in, uq=mla_w_uq, ukv=mla_w_ukv, bs=w_br_sb, bm=w_br_mla, br=w_br_rw, w_out=w_out)
    with ExitStack() as ctx:
        def sb(name, shape):
            return ctx.enter_context(nc.sbuf_tensor(name, shape, F32))

        sems = []

        def sem(name):
            s = ctx.enter_context(nc.semaphore(name))
            sems.append(s)
            return s

        con = sb("con", [P, K_END])
        xy = sb("xy", [P, HALVES, DM])
        ht = sb("ht", [P, KD, SEQ])
        ring = sb("ring", [P, RING, KC, 512])
        small = sb("small", [P, 160])
        gev = sb("gev", [P, 2, HALVES, 512])
        arena = sb("arena", [P, ARENA])
        used = [0]

        def take(n):
            a = arena[:, used[0]:used[0] + n]
            used[0] += n
            assert used[0] <= ARENA, used[0]
            return a

        def halved(n):
            return take(n).rearrange("p (h c) -> p h c", h=HALVES)

        def units(n, u):
            return take(n).rearrange("p (u c) -> p u c", u=u)

        R = halved(3072)
        PV = halved(3072)
        S1, SIG, AA = (PV[:, :, n * 512:(n + 1) * 512] for n in range(3))
        WK = halved(384)
        PW = halved(256)
        MU = take(1664)
        ROWS = take(5 * 512)
        KK, S2 = halved(1024), halved(1024)
        LW, LA = take(512), take(512)
        WT, AT = take(256), take(256)
        TT = units(1024, 2)
        AM = units(2048, 4)
        LM = units(512, 4)
        TB = units(1024, 4)
        XB = units(512, 4)
        YU = take(256)
        ST = take(128)
        CQ, CKV = halved(1024), halved(1024)
        CTQ, CTK = units(1024, 4), units(1024, 4)
        QS = take(768)
        MQ = take(1536).rearrange("p (b h n c) -> p b h n c", b=2, h=2, n=2)
        MKV = take(2048).rearrange("p (b h n c) -> p b h n c", b=2, h=2, n=2)
        KR = halved(128)
        KRH = take(256).rearrange("p (h n c) -> p h n c", h=2, n=2)
        GR = take(128)
        QKN, QKR = take(512), take(512)
        PP, PT = take(384), take(384)
        SQKV = halved(3072)
        S3 = SQKV[:, :, 0:512]
        QKT = take(512)
        AZ, LF = take(384), take(384)
        LG = LF
        used[0] = 0
        MT = units(4096, KD)
        GT = take(3072).rearrange("p (n h c) -> p n h c", n=3, h=2)
        MJ = take(2048).rearrange("p (n h c) -> p n h c", n=2, h=2)
        MG = halved(1024)

        cell = [0]

        def cells(n):
            cell[0] += n
            return small[:, cell[0] - n:cell[0]]

        ng, cqg, ckg, gq, gk, gg = cells(16), cells(4), cells(4), cells(1), cells(1), cells(1)
        ss, rs = cells(2), cells(2)
        kss, bon, mean, var = cells(16), cells(16), cells(16), cells(16)
        scv, css, qss, nss, krs = cells(4), cells(4), cells(4), cells(4), cells(2)
        mx, nb, den, rden = cells(2), cells(2), cells(2), cells(2)
        eps, eps_gn, bias_kk = cells(1), cells(1), cells(1)

        ident = con[:, K_ID:K_ID + P]
        level = [con[:, K_LEV + n * P:K_LEV + (n + 1) * P] for n in range(LEVELS + 1)]
        ntri, none = con[:, K_NTRI:K_NTRI + P], con[:, K_NONE:K_NONE + P]
        late, early = con[0:1, K_LATE:K_LATE + P], con[0:1, K_EARLY:K_EARLY + P]
        cosx = con[:, K_COS:K_COS + 64].rearrange("p (h c) -> p h c", h=2)
        sinx = con[:, K_SIN:K_SIN + 64].rearrange("p (h c) -> p h c", h=2)

        def psum(name):
            return ctx.enter_context(nc.psum_tensor(name, [P, 512], F32))

        D = [psum(f"D{i}") for i in range(4)]
        B = [psum(f"B{i}") for i in range(4)]

        def own(bank):
            return bank[:, 0:384].rearrange("p (a c) -> p a c", a=2)[:, :, 0:64]

        def as_pair(a):
            return a.rearrange("p (a c) -> p a c", a=2)

        full = [sem(f"ring_full{i}") for i in range(RING)]
        freed = sem("ring_freed")
        dense_mm = sem("dense_done")
        dense_ev = sem("dense_out")
        small_in, mu_in, rows_in, lora_in = sem("gains_in"), sem("mu_in"), sem("rows_in"), sem("lora_in")
        wk_shift = [sem(f"latents_shifted{i}") for i in range(2)]
        r_shift = [sem(f"rkv_shifted{i}") for i in range(6)]
        preset = sem("preset")
        act_seq, dve_seq = sem("act_order"), sem("dve_order")
        rstd = sem("rstd")
        normed = sem("normed")
        tr = sem("transposed")
        tr_a, tr_d = sem("transposed_out_act"), sem("transposed_out_dve")
        lora_dve, lora_pe, lora_act = sem("lora_mixed"), sem("lora_pe"), sem("lora_act")
        mixed = sem("rkv_mixed")
        kk_ss, kk_rs = sem("kk_squares"), sem("kk_rstd")
        ops_done = sem("rw_operands")
        cum_pe, cum_act = sem("decay_sums"), sem("decay_exps")
        cum_dve = sem("decayed")
        rw_pe, rw_act, rw_dve, rw_pool = sem("rw_pe"), sem("rw_act"), sem("rw_dve"), sem("rw_levels")
        gn_var, gn_rs = sem("gn_var"), sem("gn_rstd")
        lat_act, lat_dve, lat_pe, lat_gain, lat_out_a, lat_out_d = (sem("latents_" + n) for n in (
            "rstd", "normed", "transposed", "gain", "out_act", "out_dve"))
        ml_sq, ml_ss, ml_rs, ml_qk = (sem("ml_" + n) for n in ("squares", "sums", "rstd", "qk"))
        ml_pe, ml_act, ml_dve = sem("ml_pe"), sem("ml_act"), sem("ml_dve")
        sb_pe, sb_act, sb_dve, sb_pool = sem("sb_pe"), sem("sb_act"), sem("sb_dve"), sem("sb_pool")
        spilled = [sem(f"gates_spilled{i}") for i in range(2)]
        silu_sig, silu_dve = sem("silu_sigmoid"), sem("silu_gated")
        gate_in = [sem(f"gate_in{i}") for i in range(3)]
        gate_sig, gate_used = sem("gate_sigmoid"), sem("gate_used")
        merged, mt_pe, mt_act = sem("merged"), sem("merged_transposed"), sem("merged_out")
        x_in, x_new = sem("x_back"), sem("x_new")
        x_out = [sem(f"x_stored{i}") for i in range(4)]
        s_done = sem("engines_done")
        last_sem = sems[-1]
        s_go = ctx.enter_context(nc.semaphore("next_layer"))
        con_in = ctx.enter_context(nc.semaphore("constants_in"))
        x_first = ctx.enter_context(nc.semaphore("x_in"))
        x_copy = ctx.enter_context(nc.semaphore("x_to_out"))
        resumed = ctx.enter_context(nc.semaphore("resumed"))
        once = ctx.enter_context(nc.semaphore("set_once"))
        numbers = sorted(s.num for s in sems)
        assert numbers == list(range(numbers[0], numbers[-1] + 1))
        block = ctx.enter_context(nc.Block())

        def layer_end(eng, l):
            eng.drain().then_inc(s_done, 1)
            eng.wait_ge(s_go, l + 1)
            eng.sem_inc(resumed, 1)

        def filled(n):
            double = sum(1 for m in range(n % RING, min(n + 1, END["wk"]), RING))
            return 16 * (n // RING + 1 + double)

        @block.sync
        def _(sp):
            sp.dma_start(xy[:], x[0].rearrange("(h p) d -> p h d", p=P)).then_inc(x_first, 16)
            sp.dma_start(con[:], consts).then_inc(con_in, 16)
            with sp.Fori(0, DEPTH) as l:
                with nc.allow_non_contiguous_dma("gains as columns"):
                    for dst, src in ((ng, norm_g[l]), (cqg, mla_q_norm_g[l]), (ckg, mla_kv_norm_g[l]),
                                     (gq, mla_qn_g[l, 0:P]), (gk, mla_kn_g[l, 0:P])):
                        sp.dma_start(dst, src.rearrange("(k p) -> p k", p=P)).then_inc(small_in, 16)

                def row(dst, src, s):
                    sp.dma_start(dst, src.rearrange("(a n) -> a n", a=1).to_broadcast([P, dst.shape[-1]])
                                   ).then_inc(s, 16)

                for n, (gi, c) in enumerate(CHUNKS):
                    name, w, c0, cols, _ = GROUPS[gi]
                    slot = n % RING
                    if n == RING:
                        row(MU, rw_mu[l], mu_in)
                        row(GR[:, 0:64], mla_qn_g[l, P:QK], rows_in)
                        row(GR[:, 64:128], mla_kn_g[l, P:QK], rows_in)
                        for i, src in enumerate((rw_k_k[l], rw_k_a[l], rw_r_k[l].rearrange("h n -> (h n)"),
                                                 rw_gn_g[l], rw_gn_b[l])):
                            row(ROWS[:, i * 512:(i + 1) * 512], src, rows_in)
                        for dst, up, bias in ((LW, rw_w_up, rw_w0), (LA, rw_a_up, rw_a0)):
                            sp.dma_start(dst[0:64, :], up[l]).then_inc(lora_in, 16)
                            sp.dma_start(dst[64:65, :], bias[l].rearrange("(a n) -> a n", a=1)).then_inc(lora_in, 16)
                    if n >= RING:
                        sp.wait_ge(freed, n - RING + 1)
                    rows = slice(c * KC * P, (c + 1) * KC * P)
                    pieces = ((0, C_KR, ROPE), (ROPE, C_WD, 128)) if name == "wk" else ((0, c0, cols),)
                    for d0, s0, m in pieces:
                        sp.dma_start(ring[:, slot, :, d0:d0 + m],
                                     weights[w][l, rows, s0:s0 + m].rearrange("(k p) n -> p k n", p=P)
                                     ).then_inc(full[slot], 16)
                layer_end(sp, l)

        @block.gpsimd
        def _(pool):
            pool.dma_start(out[0], x[0]).then_inc(x_copy, 16)
            nc.gpsimd.memset(eps, EPS).then_inc(once, 1)
            pool.wait_ge(once, 1)
            nc.gpsimd.memset(eps_gn, 64e-5).then_inc(once, 1)
            pool.wait_ge(once, 2)
            nc.gpsimd.memset(bias_kk, float(10 * np.log(2.0))).then_inc(once, 1)
            pool.wait_ge(once, 3)
            pool.wait_ge(x_copy, 16)
            pool.wait_ge(con_in, 16)
            with pool.Fori(0, DEPTH) as l:
                for n, (t, value) in enumerate(((PV[0:1, 0, :], 0.0), (PW[0:1, 0, :], 0.0), (WT[64:65, :], 1.0),
                                                (AT[64:65, :], 1.0), (AM, 0.0), (ST, 0.0))):
                    nc.gpsimd.memset(t, value).then_inc(preset, 1)
                    pool.wait_ge(preset, n + 1)
                def shift(dst, src, s):
                    pool.dma_start(dst[1:P, :, :], src[0:P - 1, :, :]).then_inc(s[0], 16)
                    pool.dma_start(dst[0:1, 1, :], src[P - 1:P, 0, :]).then_inc(s[1], 16)

                pool.wait_ge(dense_ev, GI["wk"] + 1)
                shift(PW, WK[:, :, 64:192], wk_shift)
                for i in range(3):
                    pool.wait_ge(dense_ev, GI["rr"] + i + 1)
                    shift(PV[:, :, i * 512:(i + 1) * 512], R[:, :, i * 512:(i + 1) * 512], r_shift[2 * i:2 * i + 2])

                gate, beats = [0], [0]

                def dense_to(end):
                    while gate[0] < 12 and END[f"gate{gate[0]}"] <= end:
                        n = gate[0]
                        pool.wait_ge(dense_ev, GI[f"gate{n}"] + 1)
                        pool.dma_start(spill[n].rearrange("(h p) c -> p h c", p=P), gev[:, n % 2, :, :]
                                       ).then_inc(spilled[n % 2], 16)
                        gate[0] += 1

                def beat(count=1):
                    beats[0] += count
                    dense_to(beat_at(beats[0]))

                def rw_level(p, n):
                    nc.gpsimd.tensor_tensor(LM, AM[:, :, 0:P], level[n].unsqueeze(1).to_broadcast([P, 4, P]),
                                            ALU.mult).then_inc(rw_pool, 1)

                for p in range(4):
                    beat(2)
                    pool.wait_ge(rw_dve, RW_DVE * p + 2)
                    rw_level(p, 1)
                    beat()
                    for n in range(1, LEVELS + 1):
                        beat()
                        if n < LEVELS:
                            pool.wait_ge(rw_pe, RW_PE * p + 2 + 2 * n)
                            rw_level(p, n + 1)
                        beat()
                    beat(6)
                beat(4 * ML_BEATS)
                for h in range(SBH):
                    for k, buf in enumerate((LF, AZ)):
                        beat(2 - k)
                        pool.wait_ge(*((sb_dve, 2 * h + 1) if k == 0 else (sb_act, 3 * h + 3)))
                        for c0 in (0, 256):
                            part = buf[:, c0:c0 + P]
                            last = nc.gpsimd.affine_select(out=part, in_=part, compare_op=ALU.is_gt, fill=0.0, base=0,
                                                           pattern=[[1, P]], channel_multiplier=-1)
                        last.then_inc(sb_pool, 1)
                    beat()
                dense_to(END["gate11"])
                for i in range(2):
                    pool.wait_ge(spilled[i], 16 * 6)
                pool.wait_ge(silu_dve, 8)
                for n in range(12):
                    if n >= 3:
                        pool.wait_ge(gate_used, n - 2)
                    pool.dma_start(GT[:, n % 3, :, :], spill[n % 3 * 4 + n // 3].rearrange("(h p) c -> p h c", p=P)
                                   ).then_inc(gate_in[n % 3], 16)
                    if n == 2:
                        pool.wait_ge(tr, 16)
                        pool.dma_start(xy[:], out[0].rearrange("(h p) d -> p h d", p=P)).then_inc(x_in, 16)
                for j in range(4):
                    pool.wait_ge(x_new, j + 1)
                    pool.dma_start(out[0, :, j * 512:(j + 1) * 512].rearrange("(h p) d -> p h d", p=P),
                                   xy[:, :, j * 512:(j + 1) * 512]).then_inc(x_out[j], 16)
                for j in range(4):
                    pool.wait_ge(x_out[j], 16)
                pool.wait_ge(s_done, 4)
                pool.dma_reset(range(numbers[0], numbers[-1] + 1))
                pool.sem_clear(range(numbers[0], numbers[-1] + 1))
                pool.drain().then_inc(s_go, 1)

        @block.tensor
        def _(pe):
            at, beats = [0], [0]

            def mm(o, a, b, start, stop):
                return nc.tensor.matmul(o, a, b, start=start, stop=stop, skip_group_check=True)

            def stationary(name):
                return {"uq": CTQ, "ukv": CTK, "bs": ht[:, 0:4, :], "bm": ht[:, 4:12, :], "br": ht[:, 12:16, :],
                        "o": MT}.get(name.rstrip("0123456789"), ht)

            def dense_to(end):
                while at[0] < end:
                    n = at[0]
                    gi, c = CHUNKS[n]
                    name, _, _, cols, blocks = GROUPS[gi]
                    if c == 0 and gi >= 2:
                        pe.wait_ge(dense_ev, gi - 1)
                    if c == 0 and name == "uq0":
                        pe.wait_ge(lat_out_a, 2)
                        pe.wait_ge(lat_out_d, 2)
                    if c == 0 and name == "bs0":
                        pe.wait_ge(tr_a, 8)
                        pe.wait_ge(tr_d, 8)
                    if name == "o0" and c * KC % 4 == 0:
                        pe.wait_ge(mt_act, 2 * (c * KC // 4 + 1))
                    pe.wait_ge(full[n % RING], filled(n))
                    st = stationary(name)
                    for kk in range(KC):
                        for h in range(HALVES):
                            k = c * KC + kk
                            last = mm(D[gi % 2 * 2 + h][:, 0:cols], st[:, k, h * P:(h + 1) * P],
                                      ring[:, n % RING, kk, 0:cols], k == 0, k == blocks - 1)
                    last.then_inc(freed, 1)
                    at[0] += 1

            def beat():
                beats[0] += 1
                dense_to(beat_at(beats[0]))

            def transposes(base):
                for s in range(8):
                    if s >= 4:
                        pe.wait_ge((tr_a, tr_d)[s % 2], base + (s - 4) // 2 + 1)
                    for i in range(2):
                        for h in range(HALVES):
                            k = 2 * s + i
                            last = nc.tensor.transpose(B[s % 4][:, i * 256 + h * P:i * 256 + (h + 1) * P],
                                                       xy[:, h, k * P:(k + 1) * P], ident)
                    last.then_inc(tr, 1)

            def rw_pair(p):
                e, d0, a0 = RW_PE * p, RW_DVE * p, RW_ACT * p
                c = slice(p * P, (p + 1) * P)
                if p == 0:
                    pe.wait_ge(cum_dve, 2)
                else:
                    pe.wait_ge(rw_dve, d0)
                for h in range(HALVES):
                    for i, s in enumerate((KK, R[:, :, 0:512], AA, R[:, :, 512:1024])):
                        last = nc.tensor.transpose(B[2 + h][:, i * P:(i + 1) * P], s[:, h, c], ident)
                last.then_inc(rw_pe, 1)
                beat()
                pe.wait_ge(rw_act, a0 + 1)
                pe.wait_ge(rw_dve, d0 + 1)
                for u in range(4):
                    a, h = u // 2, u % 2
                    r = slice(64 * a, 64 * a + 64)
                    mm(B[u][:, 0:256], TT[r, h, 256:384], TT[r, h, 0:256], True, True)
                    last = mm(B[u][:, 256:512], TT[r, h, 384:512], TT[r, h, 0:256], False, True)
                last.then_inc(rw_pe, 1)
                beat()
                pe.wait_ge(rw_dve, d0 + 3)
                for u in range(4):
                    last = nc.tensor.transpose(B[0][:, u * P:(u + 1) * P], TB[:, u, P:2 * P], ident)
                last.then_inc(rw_pe, 1)
                beat()
                for n in range(1, LEVELS + 1):
                    pe.wait_ge(*((rw_act, a0 + 2) if n == 1 else (rw_dve, d0 + 2 + n)))
                    pe.wait_ge(rw_pool, LEVELS * p + n)
                    for u in range(4):
                        last = mm(B[1][:, u * P:(u + 1) * P], LM[:, u, :], TB[:, u, 0:P], True, True)
                    last.then_inc(rw_pe, 1)
                    beat()
                    pe.wait_ge(rw_act, a0 + 2 + n)
                    for u in range(4):
                        o, w = B[2 + u // 2], u % 2 * 256
                        if n < LEVELS:
                            mm(o[:, w:w + P], TB[:, u, P:2 * P], XB[:, u, :], True, True)
                        last = mm(o[:, w + P:w + 2 * P], XB[:, u, :], TB[:, u, P:2 * P], True, True)
                    last.then_inc(rw_pe, 1)
                    beat()
                for h in range(HALVES):
                    v = R[:, h, 1024 + p * P:1024 + (p + 1) * P]
                    pe.wait_ge(rw_dve, d0 + 9 + h)
                    for a in range(2):
                        last = mm(B[0][:, a * P:(a + 1) * P], AM[:, 2 * a + h, 256:384], v, True, h == 0)
                        if h:
                            last = mm(B[0][:, a * P:(a + 1) * P], TT[:, 1, 0:P], ST, False, True)
                    last.then_inc(rw_pe, 1)
                    beat()
                    pe.wait_ge(rw_act, a0 + 9 + 2 * h)
                    for a in range(2):
                        last = mm(B[1][:, a * P:(a + 1) * P], TB[:, 2 * a + h, P:2 * P], YU[:, 0:P], True, True)
                    last.then_inc(rw_pe, 1)
                    beat()
                    pe.wait_ge(rw_act, a0 + 10 + 2 * h)
                    u = YU[:, P:2 * P]
                    if h == 0:
                        mm(B[0][:, 0:P], AA[:, 0, c], u, True, False)
                        mm(B[0][:, 0:P], R[:, 0, 512 + p * P:512 + (p + 1) * P], v, False, True)
                    for a in range(2):
                        o = B[2 + h][:, a * P:(a + 1) * P]
                        mm(o, AM[:, 2 * a + h, 128:256], u, True, False)
                        last = mm(o, AM[:, 2 * a + h, 384:512], v, False, h == 0)
                        if h:
                            last = mm(o, TT[:, 1, P:2 * P], ST, False, True)
                    last.then_inc(rw_pe, 1)
                    beat()

            def mla_head(m):
                b, i = m // 2 % 2, m % 2
                if i == 0:
                    pe.wait_ge(ml_qk, m // 2 + 1)
                if m:
                    pe.wait_ge(ml_dve, 3 * m)
                for h in range(HALVES):
                    nc.tensor.transpose(B[0][:, h * P:(h + 1) * P], MQ[:, b, h, i, 0:NOPE], ident)
                    nc.tensor.transpose(B[0][:, 256 + h * P:256 + (h + 1) * P], MKV[:, b, h, i, 0:NOPE], ident)
                    nc.tensor.transpose(B[1][0:64, h * P:(h + 1) * P], MQ[:, b, h, i, NOPE:QK], ident)
                    last = nc.tensor.transpose(B[1][0:64, 256 + h * P:256 + (h + 1) * P], KRH[:, h, i, :], ident)
                last.then_inc(ml_pe, 1)
                beat()
                pe.wait_ge(ml_act, 3 * m + 1)
                pe.wait_ge(ml_dve, 3 * m + 1)
                mm(B[2][:, 0:128], QKN[:, 0:128], QKN[:, 256:384], True, False)
                mm(B[2][:, 0:128], QKR[0:64, 0:128], QKR[0:64, 256:384], False, False)
                mm(B[2][:, 0:128], early, late, False, True)
                mm(B[2][:, 128:384], QKN[:, 128:256], QKN[:, 256:512], True, False)
                mm(B[2][:, 128:384], QKR[0:64, 128:256], QKR[0:64, 256:512], False, False)
                mm(B[2][:, 256:384], early, late, False, True).then_inc(ml_pe, 1)
                beat()
                pe.wait_ge(ml_act, 3 * m + 2)
                for n in range(3):
                    last = nc.tensor.transpose(B[3][:, n * P:(n + 1) * P], PP[:, n * P:(n + 1) * P], ident)
                last.then_inc(ml_pe, 1)
                beat()
                pe.wait_ge(ml_act, 3 * m + 3)
                v = [MKV[:, b, h, i, NOPE:NOPE + VD] for h in range(2)]
                mm(B[0][:, 0:128], PT[:, 0:128], v[0], True, True)
                mm(B[0][:, 128:256], PT[:, 128:256], v[0], True, False)
                mm(B[0][:, 128:256], PT[:, 256:384], v[1], False, True).then_inc(ml_pe, 1)
                beat()

            def sb_head(h):
                if h == 0:
                    pe.wait_ge(ml_dve, 24)
                    pe.wait_ge(dense_ev, GI["sv"] + 1)
                if h:
                    pe.wait_ge(sb_dve, 2 * h)
                for i in range(2):
                    for t in range(HALVES):
                        last = nc.tensor.transpose(B[0][:, i * 256 + t * P:i * 256 + (t + 1) * P],
                                                   SQKV[:, t, i * 512 + h * P:i * 512 + (h + 1) * P], ident)
                last.then_inc(sb_pe, 1)
                beat()
                pe.wait_ge(sb_act, 3 * h + 1)
                mm(B[1][:, 0:256], QKT[:, 256:384], QKT[:, 0:256], True, True)
                mm(B[1][:, 256:384], QKT[:, 384:512], QKT[:, 128:256], False, True).then_inc(sb_pe, 1)
                beat()
                pe.wait_ge(sb_pool, 2 * h + 1)
                mm(B[1][:, 0:256], ntri, LF[:, 0:256], False, True)
                mm(B[1][:, 128:256], none, LF[:, 256:384], False, True)
                mm(B[1][:, 256:384], ntri, LF[:, 256:384], False, True).then_inc(sb_pe, 1)
                beat()
                pe.wait_ge(sb_pool, 2 * h + 2)
                v = [SQKV[:, t, 1024 + h * P:1024 + (h + 1) * P] for t in range(HALVES)]
                mm(B[2][:, 0:128], AZ[:, 0:128], v[0], True, True)
                mm(B[2][:, 128:256], AZ[:, 128:256], v[0], True, False)
                mm(B[2][:, 128:256], AZ[:, 256:384], v[1], False, True).then_inc(sb_pe, 1)
                beat()

            pe.wait_ge(con_in, 16)
            with pe.Fori(0, DEPTH) as l:
                at[0] = beats[0] = 0
                pe.wait_ge(normed, 2)
                transposes(0)
                pe.wait_ge(tr_a, 4)
                pe.wait_ge(tr_d, 4)
                dense_to(AT_LORA)
                pe.wait_ge(lora_dve, 1)
                for i in range(2):
                    for h in range(HALVES):
                        last = nc.tensor.transpose(B[i][0:64, h * P:(h + 1) * P],
                                                   WK[:, h, 64 + i * 64:128 + i * 64], ident)
                last.then_inc(lora_pe, 1)
                dense_to(AT_Z)
                pe.wait_ge(lora_act, 1)
                pe.wait_ge(lora_in, 64)
                for i, (lat, up) in enumerate(((WT, LW), (AT, LA))):
                    for h in range(HALVES):
                        last = mm(B[2 * i + h][:], lat[0:65, h * P:(h + 1) * P], up[0:65, :], True, True)
                last.then_inc(lora_pe, 1)
                dense_to(AT_LATENTS)
                pe.wait_ge(lora_act, 2)
                pe.wait_ge(lat_dve, 1)
                for i, s in enumerate((CQ, CKV)):
                    for k in range(4):
                        for h in range(HALVES):
                            last = nc.tensor.transpose(B[2 * i + k // 2][:, k % 2 * 256 + h * P:k % 2 * 256 + (h + 1) * P],
                                                       s[:, h, k * P:(k + 1) * P], ident)
                    last.then_inc(lat_pe, 1)
                dense_to(AT_DECAY)
                pe.wait_ge(lat_out_a, 2)
                pe.wait_ge(lat_out_d, 2)
                for i, k in enumerate((K_INC, K_EXC)):
                    for h in range(HALVES):
                        last = mm(B[2 * i + h][:], con[:, k:k + P], SIG[:, h, :], True, True)
                last.then_inc(cum_pe, 1)
                pe.wait_ge(cum_act, 1)
                for p in range(4):
                    for h in range(HALVES):
                        last = mm(B[0][:, p:p + 1], SIG[:, h, p * P:(p + 1) * P],
                                  con[:, K_COL + h:K_COL + h + 1], h == 0, h == 1)
                last.then_inc(cum_pe, 1)
                pe.wait_ge(cum_act, 2)
                dense_to(AT_PAIRS)
                for p in range(4):
                    rw_pair(p)
                pe.wait_ge(rw_dve, 4 * RW_DVE)
                for m in range(MLH):
                    if m % 2 == 0:
                        beat()
                    mla_head(m)
                for h in range(SBH):
                    sb_head(h)
                dense_to(END["mg1"])
                pe.wait_ge(silu_dve, 8)
                transposes(4)
                for j in range(4):
                    dense_to(END[f"bs{j}"] if j else END["br0"])
                    if j:
                        pe.wait_ge(merged, j)
                        for s in range(2):
                            if j > 1:
                                pe.wait_ge(mt_act, 2 * j - 3 + s)
                            for k in range(2):
                                for h in range(HALVES):
                                    kk = 2 * s + k
                                    last = nc.tensor.transpose(B[s][:, k * 256 + h * P:k * 256 + (h + 1) * P],
                                                               MJ[:, (j - 1) % 2, h, kk * P:(kk + 1) * P], ident)
                            last.then_inc(mt_pe, 1)
                        dense_to(END[f"br{j}"])
                dense_to(END["br3"] + 6)
                pe.wait_ge(merged, 4)
                for s in range(2):
                    pe.wait_ge(mt_act, 5 + s)
                    for k in range(2):
                        for h in range(HALVES):
                            kk = 2 * s + k
                            last = nc.tensor.transpose(B[s][:, k * 256 + h * P:k * 256 + (h + 1) * P],
                                                       MJ[:, 1, h, kk * P:(kk + 1) * P], ident)
                    last.then_inc(mt_pe, 1)
                dense_to(END["o3"])
                layer_end(pe, l)

        @block.scalar
        def _(act):
            group, beats, order = [0], [0], [0]

            def f(o, i, fn=ACT.Copy, **kw):
                return nc.scalar.activation(o, i, fn, **kw)

            def link(ins):
                order[0] += 1
                ins.then_inc(act_seq, 1)
                act.wait_ge(act_seq, order[0])

            def dense_to(end):
                while group[0] < len(GROUPS) and END[GROUPS[group[0]][0]] <= end:
                    gi = group[0]
                    name, _, _, cols, blocks = GROUPS[gi]
                    group[0] += 1
                    kind, no = name.rstrip("0123456789"), int(name[-1]) if name[-1].isdigit() else 0
                    if name.startswith("gate"):
                        no = int(name[4:])
                    if kind in ("bs", "bm", "br"):
                        n = 3 * no + ("bs", "bm", "br").index(kind)
                        act.wait_ge(gate_in[n % 3], 16 * (n // 3 + 1))
                        f(GT[:, n % 3, :, :], GT[:, n % 3, :, :], ACT.Sigmoid).then_inc(gate_sig, 1)
                        continue
                    if kind == "o":
                        continue
                    act.wait_ge(freed, END[name])
                    bank = [D[gi % 2 * 2 + h][:, 0:cols] for h in range(HALVES)]
                    scale = 1.0
                    if kind in ("rg", "sg", "mg"):
                        n = ("rg", "sg", "mg0", "mg1").index(name)
                        if n < 2:
                            act.wait_ge(spilled[n], 16 * 6)
                        else:
                            act.wait_ge(silu_dve, 2 * (n - 1))
                        for h in range(HALVES):
                            last = f(gev[:, n % 2, h, :], bank[h], ACT.Sigmoid)
                        last.then_inc(silu_sig, 1)
                        continue
                    if kind == "gate":
                        if no >= 2:
                            act.wait_ge(spilled[no % 2], 16 * (no // 2))
                        dst = [gev[:, no % 2, h, :] for h in range(HALVES)]
                    elif kind == "wk":
                        dst = [WK[:, h, :] for h in range(HALVES)]
                    elif name in ("rr", "rk", "rv"):
                        i = ("rr", "rk", "rv").index(name)
                        dst = [R[:, h, i * 512:(i + 1) * 512] for h in range(HALVES)]
                    elif name in ("sq", "sk", "sv"):
                        i = ("sq", "sk", "sv").index(name)
                        scale = SB_SCALE if i == 0 else 1.0
                        dst = [SQKV[:, h, i * 512:(i + 1) * 512] for h in range(HALVES)]
                    elif name in ("cq", "ckv"):
                        dst = [(CQ if name == "cq" else CKV)[:, h, :] for h in range(HALVES)]
                    else:
                        if no >= 2:
                            act.wait_ge(ml_dve, 6 * (no - 1))
                        t = MQ if kind == "uq" else MKV
                        dst = [t[:, no % 2, h, :, :] for h in range(HALVES)]
                        bank = [b.rearrange("p (n c) -> p n c", n=2) for b in bank]
                    for h in range(HALVES):
                        last = f(dst[h], bank[h], scale=scale)
                    last.then_inc(dense_ev, 1)

            def beat():
                beats[0] += 1
                dense_to(beat_at(beats[0]))

            def rw_pair(p):
                e = RW_PE * p
                act.wait_ge(rw_pe, e + 1)
                f(TT[:, 0, :], B[2][:]).then_inc(rw_act, 1)
                beat()
                beat()
                act.wait_ge(rw_pe, e + 3)
                f(TB[:, :, 0:P], B[0][:].rearrange("p (u c) -> p u c", u=4)).then_inc(rw_act, 1)
                beat()
                for n in range(1, LEVELS + 1):
                    act.wait_ge(rw_pe, e + 2 + 2 * n)
                    f(XB, B[1][:].rearrange("p (u c) -> p u c", u=4)).then_inc(rw_act, 1)
                    beat()
                    beat()
                for h in range(HALVES):
                    for k in range(2):
                        act.wait_ge(rw_pe, e + 16 + 3 * h + k)
                        f(as_pair(YU[:, k * P:(k + 1) * P]), own(B[k])).then_inc(rw_act, 1)
                        beat()
                    beat()

            def mla_pair(p):
                b = p % 2
                act.wait_ge(dense_ev, GI[f"ukv{p}"] + 1)
                if p:
                    act.wait_ge(ml_ss, 2 * p)
                q2 = QS.rearrange("p (h n c) -> p h n c", h=2, n=2)
                f(q2, MQ[:, b, :, :, :], ACT.Square).then_inc(ml_sq, 1)
                act.wait_ge(ml_ss, 2 * p + 1)
                f(q2[:, :, :, 0:NOPE], MKV[:, b, :, :, 0:NOPE], ACT.Square).then_inc(ml_sq, 1)
                act.wait_ge(ml_ss, 2 * p + 2)
                link(f(qss, qss, ACT.Ln, scale=1.0 / QK, bias=eps))
                link(f(nss, nss, ACT.Ln, scale=1.0 / QK, bias=eps))
                f(qss, qss, ACT.Exp, scale=-0.5)
                f(nss, nss, ACT.Exp, scale=-0.5).then_inc(ml_rs, 1)
                beat()
                for m in (2 * p, 2 * p + 1):
                    act.wait_ge(ml_pe, 4 * m + 1)
                    f(QKN[:, 0:256], B[0][:, 0:256], scale=gg)
                    f(QKN[:, 256:512], B[0][:, 256:512]).then_inc(ml_act, 1)
                    beat()
                    act.wait_ge(ml_dve, 3 * m + 2)
                    f(PP[:, 0:128], B[2][:, 0:128], ACT.Exp, scale=ML_SCALE, bias=nb[:, 0:1], accum_out=den[:, 0:1])
                    f(PP[:, 128:384], B[2][:, 128:384], ACT.Exp, scale=ML_SCALE, bias=nb[:, 1:2],
                      accum_out=den[:, 1:2]).then_inc(ml_act, 1)
                    beat()
                    act.wait_ge(ml_pe, 4 * m + 3)
                    f(PT, B[3][:, 0:384]).then_inc(ml_act, 1)
                    beat()
                    beat()

            def sb_head(h):
                act.wait_ge(sb_pe, 4 * h + 1)
                f(QKT, B[0][:]).then_inc(sb_act, 1)
                beat()
                act.wait_ge(sb_pe, 4 * h + 2)
                link(f(AZ, B[1][:, 0:384], ACT.Abs))
                link(f(AZ, AZ, ACT.Exp, scale=-1.0))
                f(LG, AZ, ACT.Ln, bias=1.0).then_inc(sb_act, 1)
                beat()
                act.wait_ge(sb_pe, 4 * h + 3)
                act.wait_ge(sb_act, 3 * h + 2)
                f(AZ, B[1][:, 0:384], ACT.Exp).then_inc(sb_act, 1)
                beat()
                beat()

            act.wait_ge(x_first, 16)
            act.wait_ge(once, 3)
            with act.Fori(0, DEPTH) as l:
                group[0] = beats[0] = order[0] = 0
                act.preload_act_table_set("natural_log_exp_and_others")
                link(f(arena[:, 0:DM], xy[:, 0, :], ACT.Square, accum_out=ss[:, 0:1]))
                link(f(arena[:, 0:DM], xy[:, 1, :], ACT.Square, accum_out=ss[:, 1:2]))
                link(f(rs, ss, ACT.Ln, scale=1.0 / DM, bias=eps))
                f(rs, rs, ACT.Exp, scale=-0.5).then_inc(rstd, 1)
                act.wait_ge(small_in, 16 * 5)
                for s in range(0, 8, 2):
                    act.wait_ge(tr, s + 1)
                    for i in range(2):
                        k = 2 * s + i
                        last = f(ht[:, k, :], B[s % 4][:, i * 256:(i + 1) * 256], scale=ng[:, k:k + 1])
                    last.then_inc(tr_a, 1)
                dense_to(AT_LORA)
                act.wait_ge(lora_pe, 1)
                act.wait_ge(preset, 6)
                f(WT[0:64, :], B[0][0:64, 0:256], ACT.Tanh)
                f(AT[0:64, :], B[1][0:64, 0:256]).then_inc(lora_act, 1)
                dense_to(AT_Z)
                act.wait_ge(lora_pe, 2)
                act.wait_ge(mixed, 1)
                for i, t in enumerate((SIG, AA)):
                    for h in range(HALVES):
                        last = f(t[:, h, :], B[2 * i + h][:], ACT.Sigmoid)
                last.then_inc(lora_act, 1)
                dense_to(END["ckv"])
                act.preload_act_table_set("natural_log_exp_and_others")
                for i, t in enumerate((CQ, CKV)):
                    if i == 0:
                        act.wait_ge(dense_ev, GI["ckv"] + 1)
                    for h in range(HALVES):
                        link(f(QS[:, 0:512], t[:, h, :], ACT.Square, accum_out=css[:, 2 * i + h:2 * i + h + 1]))
                for h in range(HALVES):
                    link(f(QS[:, 0:64], WK[:, h, 0:64], ACT.Square, accum_out=krs[:, h:h + 1]))
                link(f(css, css, ACT.Ln, scale=1.0 / LORA, bias=eps))
                f(css, css, ACT.Exp, scale=-0.5).then_inc(lat_act, 1)
                act.wait_ge(kk_ss, 1)
                link(f(kss, kss, ACT.Ln, scale=2.0 ** 20))
                f(kss, kss, ACT.Exp, scale=-0.5, bias=bias_kk).then_inc(kk_rs, 1)
                dense_to(AT_LATENTS)
                act.wait_ge(lat_pe, 1)
                for k in range(4):
                    last = f(CTQ[:, k, :], B[k // 2][:, k % 2 * 256:(k % 2 + 1) * 256], scale=cqg[:, k:k + 1])
                last.then_inc(lat_out_a, 2)
                dense_to(AT_DECAY)
                act.wait_ge(cum_pe, 1)
                act.wait_ge(ops_done, 1)
                for h in range(HALVES):
                    f(S1[:, h, :], B[h][:], ACT.Exp, scale=-1.0)
                    f(S2[:, h, :], B[h][:], ACT.Exp)
                    last = f(S3[:, h, :], B[2 + h][:], ACT.Exp)
                last.then_inc(cum_act, 1)
                act.wait_ge(cum_pe, 2)
                f(scv, B[0][:, 0:4], ACT.Exp).then_inc(cum_act, 1)
                dense_to(AT_PAIRS)
                for p in range(4):
                    rw_pair(p)
                act.wait_ge(gn_var, 1)
                link(f(var, var, ACT.Ln, scale=1.0 / 64, bias=eps_gn))
                f(var, var, ACT.Exp, scale=-0.5).then_inc(gn_rs, 1)
                for p in range(4):
                    mla_pair(p)
                for h in range(SBH):
                    sb_head(h)
                dense_to(END["mg1"])
                for s in range(0, 8, 2):
                    act.wait_ge(tr, 8 + s + 1)
                    f(ht[:, 2 * s:2 * s + 2, :], B[s % 4][:].rearrange("p (k t) -> p k t", k=2)).then_inc(tr_a, 1)

                def merged_out(j):
                    for s in range(2):
                        act.wait_ge(mt_pe, 2 * j + s + 1)
                        f(MT[:, 4 * j + 2 * s:4 * j + 2 * s + 2, :],
                          B[s][:].rearrange("p (k t) -> p k t", k=2)).then_inc(mt_act, 1)

                for j in range(4):
                    dense_to(END[f"br{j}"])
                    if j:
                        merged_out(j - 1)
                merged_out(3)
                layer_end(act, l)

        @block.vector
        def _(dve):
            v = nc.vector
            order, group = [0], [GI["rg"]]

            def link(ins):
                order[0] += 1
                ins.then_inc(dve_seq, 1)
                dve.wait_ge(dve_seq, order[0])

            def tt(o, a, b, op):
                return v.tensor_tensor(o, a, b, op)

            def over_halves(row):
                return row.unsqueeze(1).to_broadcast([P, HALVES, row.shape[-1]])

            def rope(src, dst, tmp, n):
                x1, x2 = src[:, :, :, 0:32], src[:, :, :, 32:64]
                t1, t2 = (tmp[:, i * 64 * n:(i + 1) * 64 * n].rearrange("p (h n c) -> p h n c", h=2, n=n) for i in range(2))
                cs, sn = (t.unsqueeze(2).to_broadcast([P, HALVES, n, 32]) for t in (cosx, sinx))
                tt(t1, x1, cs, ALU.mult)
                link(tt(t2, x2, sn, ALU.mult))
                link(tt(dst[:, :, :, 0:32], t1, t2, ALU.subtract))
                tt(t1, x1, sn, ALU.mult)
                link(tt(t2, x2, cs, ALU.mult))
                link(tt(dst[:, :, :, 32:64], t1, t2, ALU.add))

            def split_heads(t, h):
                return t[:, h, :].rearrange("p (n c) -> p n c", c=64)

            def per_head(o, t, s, op=ALU.mult):
                for h in range(HALVES):
                    last = tt(split_heads(o, h), split_heads(t, h),
                              s[:, 8 * h:8 * h + 8].unsqueeze(2).to_broadcast([P, 8, 64]), op)
                return last

            def head_sums(o, t):
                for h in range(HALVES):
                    last = v.tensor_reduce(o[:, 8 * h:8 * h + 8], split_heads(t, h), axis=X, op=ALU.add)
                return last

            def rw_pair(p):
                e = RW_PE * p
                c = slice(p * P, (p + 1) * P)
                dve.wait_ge(rw_pe, e + 1)
                v.tensor_copy(TT[:, 1, :], B[3][:]).then_inc(rw_dve, 1)
                dve.wait_ge(rw_pe, e + 2)
                if p:
                    dve.wait_ge(rw_pool, LEVELS * p)
                for u in range(4):
                    last = v.copy_predicated(AM[:, u, :], con[:, K_RWM:K_RWM + 512].bitcast(U32), B[u][:])
                last.then_inc(rw_dve, 1)
                dve.wait_ge(rw_dve, RW_DVE * p + 2)
                link(tt(TB[:, :, P:2 * P], AM[:, :, 0:P], level[0].unsqueeze(1).to_broadcast([P, 4, P]), ALU.mult))
                tt(TB[:, :, P:2 * P], TB[:, :, P:2 * P], ident.unsqueeze(1).to_broadcast([P, 4, P]), ALU.add
                   ).then_inc(rw_dve, 1)
                for n in range(1, LEVELS + 1):
                    dve.wait_ge(rw_pe, e + 3 + 2 * n)
                    for i in range(2):
                        t = TB[:, 2 * i:2 * i + 2, :] if n < LEVELS else TB[:, 2 * i:2 * i + 2, P:2 * P]
                        b = B[2 + i][:].rearrange("p (u c) -> p u c", u=2)
                        last = tt(t, t, b if n < LEVELS else b[:, :, P:2 * P], ALU.add)
                    last.then_inc(rw_dve, 1)
                for h in range(HALVES):
                    dve.wait_ge(rw_pe, e + 18 + 3 * h)
                    if h == 0:
                        for a in range(2):
                            d = slice(64 * a, 64 * a + 64)
                            v.tensor_scalar(ST[d, d], B[0][d, d], scv[d, p:p + 1], None, ALU.mult)
                    v.tensor_copy(as_pair(S2[:, h, c]), own(B[2 + h])).then_inc(rw_dve, 1)

            def mla_pair(p):
                b = p % 2
                dve.wait_ge(ml_sq, 2 * p + 1)
                q2 = QS.rearrange("p (a c) -> p a c", a=4)
                v.tensor_reduce(qss, q2, axis=X, op=ALU.add).then_inc(ml_ss, 1)
                dve.wait_ge(ml_sq, 2 * p + 2)
                link(v.tensor_reduce(nss, q2[:, :, 0:NOPE], axis=X, op=ALU.add))
                nss2 = nss.rearrange("p (h n) -> p h n", h=2)
                tt(nss2, nss2, krs.unsqueeze(2).to_broadcast([P, 2, 2]), ALU.add).then_inc(ml_ss, 1)
                dve.wait_ge(ml_rs, p + 1)
                mq, mk = MQ[:, b, :, :, :], MKV[:, b, :, :, :]
                for h in range(HALVES):
                    for i in range(2):
                        k = 2 * h + i
                        v.tensor_scalar(mq[:, h, i, :], mq[:, h, i, :], qss[:, k:k + 1], None, ALU.mult)
                        v.tensor_scalar(mk[:, h, i, 0:NOPE], mk[:, h, i, 0:NOPE], nss[:, k:k + 1], None, ALU.mult)
                        last = v.tensor_scalar(KRH[:, h, i, :], KR[:, h, :], nss[:, k:k + 1], None, ALU.mult)
                link(last)
                for h in range(HALVES):
                    last = tt(mq[:, h, :, NOPE:QK], mq[:, h, :, NOPE:QK],
                              GR[:, 0:64].unsqueeze(1).to_broadcast([P, 2, 64]), ALU.mult)
                link(last)
                rope(mq[:, :, :, NOPE:QK], QS[:, 0:256].rearrange("p (h n c) -> p h n c", h=2, n=2), QS[:, 256:512], 2)
                v.tensor_copy(mq[:, :, :, NOPE:QK], QS[:, 0:256].rearrange("p (h n c) -> p h n c", h=2, n=2)
                              ).then_inc(ml_qk, 1)
                for m in (2 * p, 2 * p + 1):
                    dve.wait_ge(ml_pe, 4 * m + 1)
                    v.tensor_copy(QKR[0:64, :], B[1][0:64, :]).then_inc(ml_dve, 1)
                    dve.wait_ge(ml_pe, 4 * m + 2)
                    v.reduce_max(mx[:, 0:1], B[2][:, 0:128], axis=X)
                    link(v.reduce_max(mx[:, 1:2], B[2][:, 128:384], axis=X))
                    v.tensor_scalar(nb, mx, -ML_SCALE, None, ALU.mult).then_inc(ml_dve, 1)
                    dve.wait_ge(ml_act, 3 * m + 2)
                    link(v.reciprocal(rden, den))
                    dve.wait_ge(ml_pe, 4 * m + 4)
                    c0 = 512 + m * VD
                    for h in range(HALVES):
                        last = v.tensor_scalar(xy[:, h, c0:c0 + VD], B[0][:, h * P:(h + 1) * P], rden[:, h:h + 1],
                                               None, ALU.mult)
                    last.then_inc(ml_dve, 1)

            def sb_head(h):
                dve.wait_ge(sb_act, 3 * h + 2)
                v.scalar_tensor_tensor(LF, B[1][:, 0:384], 0.0, LG, ALU.max, ALU.add).then_inc(sb_dve, 1)
                dve.wait_ge(sb_pe, 4 * h + 4)
                v.tensor_copy(xy[:, :, h * P:(h + 1) * P], B[2][:, 0:256].rearrange("p (h c) -> p h c", h=2)
                              ).then_inc(sb_dve, 1)

            dve.wait_ge(con_in, 16)
            with dve.Fori(0, DEPTH) as l:
                order[0] = 0
                dve.wait_ge(rstd, 1)
                for h in range(HALVES):
                    v.tensor_scalar(xy[:, h, :], xy[:, h, :], rs[:, h:h + 1], None, ALU.mult).then_inc(normed, 1)
                dve.wait_ge(small_in, 16 * 5)
                tt(gg, gq, gk, ALU.mult).then_inc(lat_gain, 1)
                for s in range(1, 8, 2):
                    dve.wait_ge(tr, s + 1)
                    for i in range(2):
                        k = 2 * s + i
                        last = v.tensor_scalar(ht[:, k, :], B[s % 4][:, i * 256:(i + 1) * 256], ng[:, k:k + 1], None, ALU.mult)
                    last.then_inc(tr_d, 1)
                dve.wait_ge(mu_in, 16)
                for s in wk_shift:
                    dve.wait_ge(s, 16)
                dve.wait_ge(preset, 6)
                lat = WK[:, :, 64:192]
                link(tt(PW, PW, lat, ALU.subtract))
                link(tt(PW, PW, over_halves(MU[:, 1536:1664]), ALU.mult))
                tt(lat, lat, PW, ALU.add).then_inc(lora_dve, 1)
                for s in r_shift:
                    dve.wait_ge(s, 16)
                link(tt(PV, PV, R, ALU.subtract))
                link(tt(PV, PV, over_halves(MU[:, 0:1536]), ALU.mult))
                tt(R, R, PV, ALU.add).then_inc(mixed, 1)
                dve.wait_ge(mixed, 1)
                rr, rk, rv = (R[:, :, i * 512:(i + 1) * 512] for i in range(3))
                k_k, k_a, r_k, gn_g, gn_b = (over_halves(ROWS[:, i * 512:(i + 1) * 512]) for i in range(5))
                dve.wait_ge(rows_in, 16 * 7)
                link(tt(KK, rk, k_k, ALU.mult))
                link(tt(S1, KK, KK, ALU.mult))
                link(head_sums(kss, S1))
                v.tensor_scalar(kss, kss, 1e-24, None, ALU.max).then_inc(kk_ss, 1)
                link(tt(KR, WK[:, :, 0:64], over_halves(GR[:, 64:128]), ALU.mult))
                dve.wait_ge(lat_act, 1)
                dst = QS[:, 0:128].rearrange("p (h n c) -> p h n c", h=2, n=1)
                rope(KR.unsqueeze(2), dst, QS[:, 128:256], 1)
                link(v.tensor_copy(KR, dst[:, :, 0, :]))
                for i, t in enumerate((CQ, CKV)):
                    for h in range(HALVES):
                        last = v.tensor_scalar(t[:, h, :], t[:, h, :], css[:, 2 * i + h:2 * i + h + 1], None, ALU.mult)
                last.then_inc(lat_dve, 1)
                dve.wait_ge(kk_rs, 1)
                dve.wait_ge(lora_act, 2)
                per_head(KK, KK, kss)
                for h in range(HALVES):
                    last = v.scalar_tensor_tensor(S1[:, h, :], AA[:, h, :], -1.0, ROWS[:, 512:1024], ALU.add, ALU.mult)
                link(last)
                for h in range(HALVES):
                    v.scalar_tensor_tensor(R[:, h, 512:1024], S1[:, h, :], 1.0, R[:, h, 512:1024], ALU.add, ALU.mult)
                link(tt(AA, AA, KK, ALU.mult))
                link(tt(S1, rr, rk, ALU.mult))
                link(tt(S1, S1, r_k, ALU.mult))
                head_sums(bon, S1).then_inc(ops_done, 1)
                dve.wait_ge(lat_pe, 2)
                for k in range(4):
                    last = v.tensor_scalar(CTK[:, k, :], B[2 + k // 2][:, k % 2 * 256:(k % 2 + 1) * 256], ckg[:, k:k + 1],
                                           None, ALU.mult)
                last.then_inc(lat_out_d, 2)
                dve.wait_ge(cum_act, 1)
                tt(rr, rr, S2, ALU.mult)
                tt(rk, rk, S1, ALU.mult)
                tt(AA, AA, S1, ALU.mult)
                for h in range(HALVES):
                    last = v.scalar_tensor_tensor(KK[:, h, :], KK[:, h, :], -1.0, S3[:, h, :], ALU.mult, ALU.mult)
                last.then_inc(cum_dve, 2)
                dve.wait_ge(cum_dve, 2)
                dve.wait_ge(cum_act, 2)
                for p in range(4):
                    rw_pair(p)
                dve.wait_ge(rw_dve, 4 * RW_DVE)
                link(head_sums(mean, S2))
                link(v.tensor_scalar(mean, mean, 1.0 / 64, None, ALU.mult))
                link(per_head(S2, S2, mean, ALU.subtract))
                link(tt(S1, S2, S2, ALU.mult))
                head_sums(var, S1).then_inc(gn_var, 1)
                dve.wait_ge(gn_rs, 1)
                per_head(S1, rv, bon)
                link(per_head(S2, S2, var))
                link(tt(S2, S2, gn_g, ALU.mult))
                link(tt(S2, S2, gn_b, ALU.add))
                link(tt(xy[:, :, 1536:2048], S2, S1, ALU.add))
                for p in range(4):
                    mla_pair(p)
                for h in range(SBH):
                    sb_head(h)
                dve.wait_ge(sb_dve, 2 * SBH)
                dve.wait_ge(ml_dve, 3 * MLH)
                for n, (name, c0) in enumerate((("rg", 1536), ("sg", 0), ("mg0", 512), ("mg1", 1024))):
                    gi = GI[name]
                    dve.wait_ge(silu_sig, n + 1)
                    for h in range(HALVES):
                        last = tt(gev[:, n % 2, h, :], gev[:, n % 2, h, :], D[gi % 2 * 2 + h][:], ALU.mult)
                    last.then_inc(dense_ev, 1)
                    dve.wait_ge(dense_ev, gi + 1)
                    y = xy[:, :, c0:c0 + 512]
                    tt(y, y, gev[:, n % 2, :, :], ALU.mult).then_inc(silu_dve, 2)
                for s in range(1, 8, 2):
                    dve.wait_ge(tr, 8 + s + 1)
                    v.tensor_copy(ht[:, 2 * s:2 * s + 2, :], B[s % 4][:].rearrange("p (k t) -> p k t", k=2)
                                  ).then_inc(tr_d, 1)
                for n in range(12):
                    j, b = n // 3, n % 3
                    gi = GI[f"{('bs', 'bm', 'br')[b]}{j}"]
                    dve.wait_ge(gate_sig, n + 1)
                    dve.wait_ge(freed, END[GROUPS[gi][0]])
                    if b == 0 and j >= 2:
                        dve.wait_ge(mt_pe, 2 * (j - 1))
                    o = MJ[:, j % 2, :, :] if b == 0 else MG
                    for h in range(HALVES):
                        last = tt(o[:, h, :], GT[:, b, h, :], D[gi % 2 * 2 + h][:], ALU.mult)
                    last.then_inc(dense_ev, 1)
                    dve.wait_ge(dense_ev, gi + 1)
                    if b:
                        link(tt(MJ[:, j % 2, :, :], MJ[:, j % 2, :, :], MG, ALU.add))
                    v.sem_inc(gate_used, 1)
                    if b == 2:
                        v.sem_inc(merged, 1)
                dve.wait_ge(x_in, 16)
                for j in range(4):
                    gi = GI[f"o{j}"]
                    dve.wait_ge(freed, END[f"o{j}"])
                    for h in range(HALVES):
                        t = xy[:, h, j * 512:(j + 1) * 512]
                        last = tt(t, t, D[gi % 2 * 2 + h][:], ALU.add)
                    last.then_inc(x_new, 1)
                    dve.wait_ge(x_new, j + 1)
                    v.sem_inc(dense_ev, 1)
                layer_end(dve, l)


NAMES = ["x", "norm_g", "w_in", "mla_q_norm_g", "mla_kv_norm_g", "mla_w_uq", "mla_w_ukv", "mla_qn_g", "mla_kn_g",
         "rw_mu", "rw_w0", "rw_w_up", "rw_a0", "rw_a_up", "rw_k_k", "rw_k_a", "rw_r_k", "rw_gn_g", "rw_gn_b",
         "w_br_sb", "w_br_mla", "w_br_rw", "w_out"]


def kernel(**inputs):
    import concourse.bacc as bacc
    from concourse.bass_utils import run_bass_kernel_spmd

    nc = bacc.Bacc("TRN2", target_bir_lowering=False, num_devices=1)
    arrays, args = {}, []
    for name in NAMES:
        a = np.ascontiguousarray(inputs[name])
        arrays["in_" + name] = a
        args.append(nc.dram_tensor("in_" + name, a.shape, mybir.dt.from_np(a.dtype), kind="ExternalInput").ap())
    arrays["in_consts"] = constants()
    args.append(nc.dram_tensor("in_consts", (P, K_END), F32, kind="ExternalInput").ap())
    args.append(nc.dram_tensor("out_x", (1, SEQ, DM), F32, kind="ExternalOutput").ap())
    args.append(nc.dram_tensor("gate_spill", (12, SEQ, 512), F32, kind="Internal").ap())
    program(nc, *args)
    r = run_bass_kernel_spmd(nc, [arrays], core_ids=[0])
    return r.results[0]["out_x"]
```

```python
import numpy as np
import concourse.bass as bass
from concourse import mybir
from contextlib import ExitStack

F32 = mybir.dt.float32
U32 = mybir.dt.uint32
F32R = mybir.dt.float32r
ALU = mybir.AluOpType
ACT = mybir.ActivationFunctionType
X = mybir.AxisListType.X

DEPTH, SEQ, DM = 2, 256, 2048
P = 128
HALVES = SEQ // P
KD = DM // P
SBH, MLH, RWH = 4, 8, 8
NOPE, ROPE, VD = 128, 64, 128
QK = NOPE + ROPE
LORA = 512
RWW = 512
EPS = 1e-6
C_SB = 0
C_CQ = 2048
C_CKV = C_CQ + LORA
C_KR = C_CKV + LORA
C_MG = C_KR + ROPE
C_RW = C_MG + MLH * VD
C_WD = C_RW + 3 * RWW
C_RG = C_WD + 128
C_GATE = C_RG + RWW
N_IN = C_GATE + 3 * DM
DECAY = float(np.exp(-0.5))
MID = P // 2 - 1
LEVELS = 6
KC = 2
RING = 4
HALF_RING = 4
LEAD = HALF_RING - 1
ARENA = 18700
SB_SCALE = 128.0 ** -0.5
ML_SCALE = QK ** -0.5
MASKED = -1e30

K_ID, K_INC, K_EXC, K_NTRI, K_NONE, K_RWM, K_LEV = 0, 128, 256, 384, 512, 640, 1152
K_COS = K_LEV + (LEVELS + 1) * 128
K_SIN = K_COS + 64
K_COL = K_SIN + 64
K_LATE = K_COL + 2
K_EARLY = K_LATE + P
K_END = K_EARLY + P


def constants():
    c = np.zeros((P, K_END), np.float32)
    i = np.arange(P)
    row, col = i[:, None], i[None, :]
    c[:, K_ID:K_ID + P] = row == col
    past_mid = (row <= MID).astype(np.float32)
    c[:, K_INC:K_INC + P] = -DECAY * ((row <= col).astype(np.float32) - past_mid)
    c[:, K_EXC:K_EXC + P] = -DECAY * ((row < col).astype(np.float32) - past_mid)
    c[:, K_NTRI:K_NTRI + P] = -(row >= col).astype(np.float32)
    c[:, K_NONE:K_NONE + P] = -1.0
    strict, incl = (row < col), (row <= col)
    c[:, K_RWM:K_RWM + 512] = np.concatenate([strict, incl, strict, incl], 1)
    for n in range(LEVELS + 1):
        b = 2 ** n
        c[:, K_LEV + n * P:K_LEV + (n + 1) * P] = (row // (2 * b) == col // (2 * b)) & (row // b < col // b)
    half = ROPE // 2
    freqs = (np.float32(10000.0) ** (-np.arange(half, dtype=np.float32) / np.float32(half))).astype(np.float32)
    ang = np.arange(SEQ, dtype=np.float32)[:, None] * freqs[None, :]
    for h in range(HALVES):
        c[:, K_COS + h * half:K_COS + (h + 1) * half] = np.cos(ang[h * P:(h + 1) * P])
        c[:, K_SIN + h * half:K_SIN + (h + 1) * half] = np.sin(ang[h * P:(h + 1) * P])
    c[:, K_COL] = -DECAY * (i > MID)
    c[:, K_COL + 1] = -DECAY * (i <= MID)
    c[:, K_LATE + 64:K_LATE + P] = 1.0
    c[:, K_EARLY:K_EARLY + 64] = MASKED
    return c


def groups():
    def wide(name, c0):
        return [(name, "w_in", c0, 512, KD)]

    def pair(p):
        return [(f"uq{p}", "uq", p * 2 * QK, 2 * QK, 4), (f"ukv{p}", "ukv", p * 512, 512, 4)]

    gates = [wide(f"gate{n}", C_GATE + n * 512)[0] for n in range(12)]
    g = [("wk", "w_in", C_KR, 256, KD)]
    g += wide("rr", C_RW) + wide("rk", C_RW + 512) + wide("rv", C_RW + 1024)
    g += wide("cq", C_CQ) + wide("ckv", C_CKV)
    g += gates[:9] + pair(0) + pair(1) + gates[9:11] + pair(2) + wide("sq", C_SB) + pair(3)
    g += wide("sk", C_SB + 512) + wide("sv", C_SB + 1024) + gates[11:]
    g += wide("rg", C_RG) + wide("sg", C_SB + 1536) + wide("mg0", C_MG) + wide("mg1", C_MG + 512)
    for j in range(4):
        g += [(f"bs{j}", "bs", j * 512, 512, 4), (f"bm{j}", "bm", j * 512, 512, 8), (f"br{j}", "br", j * 512, 512, 4)]
    g += [(f"o{j}", "w_out", j * 512, 512, KD) for j in range(4)]
    return g


GROUPS = groups()
CHUNKS = [(gi, c) for gi, g in enumerate(GROUPS) for c in range(g[4] // KC)]
GI = {g[0]: i for i, g in enumerate(GROUPS)}
END = {g[0]: sum(x[4] // KC for x in GROUPS[:i + 1]) for i, g in enumerate(GROUPS)}

AT_MIX = [END[n] + 2 for n in ("rr", "rk", "rv")]
AT_LORA = END["wk"] + 3
AT_Z = END["rv"] + 2
AT_KK = AT_Z + 1
AT_LATENTS = END["ckv"] + 2
AT_DECAY = AT_LATENTS + 4
AT_PAIRS = AT_DECAY + 3
RW_BEATS, GN_BEATS, ML_BEATS, SB_BEATS = 21, 8, 11, 4
BEATS = 4 * RW_BEATS + GN_BEATS + 4 * ML_BEATS + SBH * SB_BEATS


def beat_at(n):
    return AT_PAIRS + n * (END["gate11"] - AT_PAIRS) // BEATS


def merged_at(j):
    return END[f"bs{j + 1}"] if j < 3 else END["br3"] + 4


RW_PE, RW_ACT, RW_DVE = 21, 12, 11


def program(nc, x, norm_g, w_in, mla_q_norm_g, mla_kv_norm_g, mla_w_uq, mla_w_ukv, mla_qn_g, mla_kn_g,
            rw_mu, rw_w0, rw_w_up, rw_a0, rw_a_up, rw_k_k, rw_k_a, rw_r_k, rw_gn_g, rw_gn_b,
            w_br_sb, w_br_mla, w_br_rw, w_out, consts, out, spill):
    weights = dict(w_in=w_in, uq=mla_w_uq, ukv=mla_w_ukv, bs=w_br_sb, bm=w_br_mla, br=w_br_rw, w_out=w_out)
    with ExitStack() as ctx:
        def sb(name, shape):
            return ctx.enter_context(nc.sbuf_tensor(name, shape, F32))

        def sbr(name, shape):
            return ctx.enter_context(nc.sbuf_tensor(name, shape, F32R))

        sems = []

        def sem(name):
            s = ctx.enter_context(nc.semaphore(name))
            sems.append(s)
            return s

        con = sb("con", [P, K_END])
        xy = sb("xy", [P, HALVES, DM])
        hth, htl = sbr("ht_hi", [P, KD, SEQ]), sbr("ht_lo", [P, KD, SEQ])
        ring = sb("ring", [P, RING, KC, 512])
        wh, wl = sbr("w_hi", [P, HALF_RING, KC, 512]), sbr("w_lo", [P, HALF_RING, KC, 512])
        cqh, cql = sbr("cq_hi", [P, 4, SEQ]), sbr("cq_lo", [P, 4, SEQ])
        ckh, ckl = sbr("ckv_hi", [P, 4, SEQ]), sbr("ckv_lo", [P, 4, SEQ])
        small = sb("small", [P, 160])
        gev = sb("gev", [P, 2, HALVES, 512])
        with nc.sbuf_tensor("arena", [P, ARENA], F32) as arena:
            pass
        mth, mtl = sbr("mt_hi", [P, KD, SEQ]), sbr("mt_lo", [P, KD, SEQ])
        used = [0]

        def take(n):
            a = arena[:, used[0]:used[0] + n]
            used[0] += n
            assert used[0] <= ARENA, used[0]
            return a

        def halved(n):
            return take(n).rearrange("p (h c) -> p h c", h=HALVES)

        def units(n, u):
            return take(n).rearrange("p (u c) -> p u c", u=u)

        def again(tile_start, *makers):
            end, used[0] = used[0], tile_start
            made = [m() for m in makers]
            used[0] = end
            return made

        R = halved(3072)
        SQKV = R
        PV = halved(3072)
        S1, SIG, AA = (PV[:, :, n * 512:(n + 1) * 512] for n in range(3))
        WK = halved(384)
        PW = halved(256)
        ROWS = take(3 * 512)
        KK, S2 = xy[:, :, 0:512], xy[:, :, 1536:2048]
        at_tt = used[0]
        TT = units(1024, 2)
        XB = units(512, 4)
        LW, LA, WT, AT = again(at_tt, lambda: take(512), lambda: take(512), lambda: take(256), lambda: take(256))
        at_am = used[0]
        AM = units(2048, 4)
        MU, = again(at_am, lambda: take(1664))
        QKN, QKR, PP, PT, KRH = again(at_am, *[lambda n=n: take(n) for n in (512, 512, 384, 384, 256)])
        KRH = KRH.rearrange("p (h n c) -> p h n c", h=2, n=2)
        at_tb = used[0]
        TB = units(1024, 4)
        LM = units(512, 4)
        QKT, AZ, LF = again(at_tb, *[lambda n=n: take(n) for n in (512, 384, 384)])
        LG = LF
        YU = take(256)
        ST = take(128)
        QS = take(768)
        at_mq = used[0]
        MQ = take(1536).rearrange("p (b h n c) -> p b h n c", b=2, h=2, n=2)
        S3, = again(at_mq, lambda: halved(1024))
        at_mkv = used[0]
        MKV = take(2048).rearrange("p (b h n c) -> p b h n c", b=2, h=2, n=2)
        CQ, CKV = again(at_mkv, lambda: halved(1024), lambda: halved(1024))
        KR = halved(128)
        GR = take(128)
        used[0] = 2 * KD * SEQ
        GT = take(3072).rearrange("p (n h c) -> p n h c", n=3, h=2)
        MJ = take(2048).rearrange("p (n h c) -> p n h c", n=2, h=2)
        MG = halved(1024)

        cell = [0]

        def cells(n):
            cell[0] += n
            return small[:, cell[0] - n:cell[0]]

        ng, cqg, ckg, gq, gk, gg = cells(16), cells(4), cells(4), cells(1), cells(1), cells(1)
        ss, rs = cells(2), cells(2)
        kss, bon, mean, var = cells(16), cells(16), cells(16), cells(16)
        scv, css, qss, nss, krs = cells(4), cells(4), cells(4), cells(4), cells(2)
        mx, nb, den, rden = cells(2), cells(2), cells(2), cells(2)
        eps, eps_gn, bias_kk = cells(1), cells(1), cells(1)

        ident = con[:, K_ID:K_ID + P]
        level = [con[:, K_LEV + n * P:K_LEV + (n + 1) * P] for n in range(LEVELS + 1)]
        ntri, none = con[:, K_NTRI:K_NTRI + P], con[:, K_NONE:K_NONE + P]
        late, early = con[0:1, K_LATE:K_LATE + P], con[0:1, K_EARLY:K_EARLY + P]
        cosx = con[:, K_COS:K_COS + 64].rearrange("p (h c) -> p h c", h=2)
        sinx = con[:, K_SIN:K_SIN + 64].rearrange("p (h c) -> p h c", h=2)

        def psum(name):
            return ctx.enter_context(nc.psum_tensor(name, [P, 512], F32))

        D = [psum(f"D{i}") for i in range(4)]
        B = [psum(f"B{i}") for i in range(4)]

        def own(bank):
            return bank[:, 0:384].rearrange("p (a c) -> p a c", a=2)[:, :, 0:64]

        def as_pair(a):
            return a.rearrange("p (a c) -> p a c", a=2)

        full = [sem(f"ring_full{i}") for i in range(RING)]
        split_hi, split_lo = sem("weights_hi"), sem("weights_lo")
        freed = sem("ring_freed")
        dense_ev = sem("dense_out")
        small_in, mu_in, rows_in, lora_in, gn_in = (sem(n + "_in") for n in ("gains", "mu", "rows", "lora", "gn"))
        wk_shift = [sem(f"latents_shifted{i}") for i in range(2)]
        r_shift = [sem(f"rkv_shifted{i}") for i in range(6)]
        preset = sem("preset")
        act_seq, dve_seq = sem("act_order"), sem("dve_order")
        rstd = sem("rstd")
        normed = sem("normed")
        tr = sem("transposed")
        tr_a, tr_d = sem("transposed_out_act"), sem("transposed_out_dve")
        lora_dve, lora_pe, lora_act = sem("lora_mixed"), sem("lora_pe"), sem("lora_act")
        mixed = sem("rkv_mixed")
        kk_ss, kk_rs = sem("kk_squares"), sem("kk_rstd")
        ops_done = sem("rw_operands")
        cum_pe, cum_act = sem("decay_sums"), sem("decay_exps")
        cum_dve = sem("decayed")
        rw_pe, rw_act, rw_dve, rw_pool = sem("rw_pe"), sem("rw_act"), sem("rw_dve"), sem("rw_levels")
        gn_var, gn_rs, gn_done = sem("gn_var"), sem("gn_rstd"), sem("gn_done")
        lat_act, lat_dve, lat_pe, lat_gain, lat_hi, lat_out = (sem("latents_" + n) for n in (
            "rstd", "normed", "transposed", "gain", "hi", "lo"))
        ml_sq, ml_ss, ml_rs, ml_qk = (sem("ml_" + n) for n in ("squares", "sums", "rstd", "qk"))
        ml_pe, ml_act, ml_dve = sem("ml_pe"), sem("ml_act"), sem("ml_dve")
        sb_pe, sb_act, sb_dve, sb_pool = sem("sb_pe"), sem("sb_act"), sem("sb_dve"), sem("sb_pool")
        spilled = [sem(f"gates_spilled{i}") for i in range(2)]
        silu_sig, silu_dve = sem("silu_sigmoid"), sem("silu_gated")
        gate_in = [sem(f"gate_in{i}") for i in range(3)]
        gate_sig, gate_used = sem("gate_sigmoid"), sem("gate_used")
        merged, mt_pe, mt_act, mt_dve = (sem("merged" + n) for n in ("", "_transposed", "_hi", "_lo"))
        x_in, x_new = sem("x_back"), sem("x_new")
        x_out = [sem(f"x_stored{i}") for i in range(4)]
        s_done = sem("engines_done")
        last_sem = sems[-1]
        s_go = ctx.enter_context(nc.semaphore("next_layer"))
        con_in = ctx.enter_context(nc.semaphore("constants_in"))
        x_first = ctx.enter_context(nc.semaphore("x_in"))
        x_copy = ctx.enter_context(nc.semaphore("x_to_out"))
        resumed = ctx.enter_context(nc.semaphore("resumed"))
        once = ctx.enter_context(nc.semaphore("set_once"))
        numbers = sorted(s.num for s in sems)
        assert numbers == list(range(numbers[0], numbers[-1] + 1))
        block = ctx.enter_context(nc.Block())

        def layer_end(eng, l):
            eng.drain().then_inc(s_done, 1)
            eng.wait_ge(s_go, l + 1)
            eng.sem_inc(resumed, 1)

        def filled(n):
            double = sum(1 for m in range(n % RING, min(n + 1, END["wk"]), RING))
            return 16 * (n // RING + 1 + double)

        @block.sync
        def _(sp):
            sp.dma_start(xy[:], x[0].rearrange("(h p) d -> p h d", p=P)).then_inc(x_first, 16)
            sp.dma_start(con[:], consts).then_inc(con_in, 16)
            with sp.Fori(0, DEPTH) as l:
                with nc.allow_non_contiguous_dma("gains as columns"):
                    for dst, src in ((ng, norm_g[l]), (cqg, mla_q_norm_g[l]), (ckg, mla_kv_norm_g[l]),
                                     (gq, mla_qn_g[l, 0:P]), (gk, mla_kn_g[l, 0:P])):
                        sp.dma_start(dst, src.rearrange("(k p) -> p k", p=P)).then_inc(small_in, 16)

                def row(dst, src, s):
                    sp.dma_start(dst, src.rearrange("(a n) -> a n", a=1).to_broadcast([P, dst.shape[-1]])
                                   ).then_inc(s, 16)

                for n, (gi, c) in enumerate(CHUNKS):
                    name, w, c0, cols, _ = GROUPS[gi]
                    slot = n % RING
                    if n == RING:
                        row(MU, rw_mu[l], mu_in)
                        row(GR[:, 0:64], mla_qn_g[l, P:QK], rows_in)
                        row(GR[:, 64:128], mla_kn_g[l, P:QK], rows_in)
                        for i, src in enumerate((rw_k_k[l], rw_k_a[l], rw_r_k[l].rearrange("h n -> (h n)"))):
                            row(ROWS[:, i * 512:(i + 1) * 512], src, rows_in)
                        for dst, up, bias in ((LW, rw_w_up, rw_w0), (LA, rw_a_up, rw_a0)):
                            sp.dma_start(dst[0:64, :], up[l]).then_inc(lora_in, 16)
                            sp.dma_start(dst[64:65, :], bias[l].rearrange("(a n) -> a n", a=1)).then_inc(lora_in, 16)
                    if n == END["ckv"] + RING:
                        sp.wait_ge(ops_done, 1)
                        row(ROWS[:, 0:512], rw_gn_g[l], gn_in)
                        row(ROWS[:, 512:1024], rw_gn_b[l], gn_in)
                    if n >= RING:
                        sp.wait_ge(split_lo, n - RING + 1)
                    rows = slice(c * KC * P, (c + 1) * KC * P)
                    pieces = ((0, C_KR, ROPE), (ROPE, C_WD, 192)) if name == "wk" else ((0, c0, cols),)
                    for d0, s0, m in pieces:
                        sp.dma_start(ring[:, slot, :, d0:d0 + m],
                                     weights[w][l, rows, s0:s0 + m].rearrange("(k p) n -> p k n", p=P)
                                     ).then_inc(full[slot], 16)
                layer_end(sp, l)

        @block.gpsimd
        def _(pool):
            pool.dma_start(out[0], x[0]).then_inc(x_copy, 16)
            nc.gpsimd.memset(eps, EPS).then_inc(once, 1)
            pool.wait_ge(once, 1)
            nc.gpsimd.memset(eps_gn, 64e-5).then_inc(once, 1)
            pool.wait_ge(once, 2)
            nc.gpsimd.memset(bias_kk, float(10 * np.log(2.0))).then_inc(once, 1)
            pool.wait_ge(once, 3)
            pool.wait_ge(x_copy, 16)
            pool.wait_ge(con_in, 16)
            with pool.Fori(0, DEPTH) as l:
                for n, (t, value) in enumerate(((PV[0:1, 0, :], 0.0), (PW[0:1, 0, :], 0.0), (WT[64:65, :], 1.0),
                                                (AT[64:65, :], 1.0), (ST, 0.0))):
                    nc.gpsimd.memset(t, value).then_inc(preset, 1)
                    pool.wait_ge(preset, n + 1)
                def shift(dst, src, s):
                    pool.dma_start(dst[1:P, :, :], src[0:P - 1, :, :]).then_inc(s[0], 16)
                    pool.dma_start(dst[0:1, 1, :], src[P - 1:P, 0, :]).then_inc(s[1], 16)

                pool.wait_ge(dense_ev, GI["wk"] + 1)
                shift(PW, WK[:, :, 64:192], wk_shift)
                for i in range(3):
                    pool.wait_ge(dense_ev, GI["rr"] + i + 1)
                    shift(PV[:, :, i * 512:(i + 1) * 512], R[:, :, i * 512:(i + 1) * 512], r_shift[2 * i:2 * i + 2])

                pool.wait_ge(mixed, 3)
                nc.gpsimd.memset(AM, 0.0).then_inc(preset, 1)
                gate, beats = [0], [0]

                def dense_to(end):
                    while gate[0] < 12 and END[f"gate{gate[0]}"] <= end:
                        n = gate[0]
                        pool.wait_ge(dense_ev, GI[f"gate{n}"] + 1)
                        pool.dma_start(spill[n].rearrange("(h p) c -> p h c", p=P), gev[:, n % 2, :, :]
                                       ).then_inc(spilled[n % 2], 16)
                        gate[0] += 1

                def beat(count=1):
                    beats[0] += count
                    dense_to(beat_at(beats[0]))

                def rw_level(p, n):
                    nc.gpsimd.tensor_tensor(LM, AM[:, :, 0:P], level[n].unsqueeze(1).to_broadcast([P, 4, P]),
                                            ALU.mult).then_inc(rw_pool, 1)

                for p in range(4):
                    beat(2)
                    pool.wait_ge(rw_dve, RW_DVE * p + 2)
                    rw_level(p, 1)
                    beat()
                    for n in range(1, LEVELS + 1):
                        beat()
                        if n < LEVELS:
                            pool.wait_ge(rw_pe, RW_PE * p + 2 + 2 * n)
                            rw_level(p, n + 1)
                        beat()
                    beat(6)
                beat(GN_BEATS + 4 * ML_BEATS)
                dense_to(END["sv"])
                for h in range(SBH):
                    for k, buf in enumerate((LF, AZ)):
                        beat(2 - k)
                        pool.wait_ge(*((sb_dve, 2 * h + 1) if k == 0 else (sb_act, 3 * h + 3)))
                        for c0 in (0, 256):
                            part = buf[:, c0:c0 + P]
                            last = nc.gpsimd.affine_select(out=part, in_=part, compare_op=ALU.is_gt, fill=0.0, base=0,
                                                           pattern=[[1, P]], channel_multiplier=-1)
                        last.then_inc(sb_pool, 1)
                    beat()
                dense_to(END["gate11"])
                for i in range(2):
                    pool.wait_ge(spilled[i], 16 * 6)
                pool.wait_ge(silu_dve, 8)
                for n in range(12):
                    if n >= 3:
                        pool.wait_ge(gate_used, n - 2)
                    pool.dma_start(GT[:, n % 3, :, :], spill[n % 3 * 4 + n // 3].rearrange("(h p) c -> p h c", p=P)
                                   ).then_inc(gate_in[n % 3], 16)
                    if n == 2:
                        pool.wait_ge(tr, 16)
                        pool.dma_start(xy[:], out[0].rearrange("(h p) d -> p h d", p=P)).then_inc(x_in, 16)
                for j in range(4):
                    pool.wait_ge(x_new, j + 1)
                    pool.dma_start(out[0, :, j * 512:(j + 1) * 512].rearrange("(h p) d -> p h d", p=P),
                                   xy[:, :, j * 512:(j + 1) * 512]).then_inc(x_out[j], 16)
                for j in range(4):
                    pool.wait_ge(x_out[j], 16)
                pool.wait_ge(s_done, 4)
                pool.dma_reset(range(numbers[0], numbers[-1] + 1))
                pool.sem_clear(range(numbers[0], numbers[-1] + 1))
                pool.drain().then_inc(s_go, 1)

        @block.tensor
        def _(pe):
            at, beats = [0], [0]

            def mm(o, a, b, start, stop):
                return nc.tensor.matmul(o, a, b, start=start, stop=stop, skip_group_check=True)

            def stationary(name):
                return {"uq": (cqh, cql, 0), "ukv": (ckh, ckl, 0), "bs": (hth, htl, 0), "bm": (hth, htl, 4),
                        "br": (hth, htl, 12), "o": (mth, mtl, 0)}.get(name.rstrip("0123456789"), (hth, htl, 0))

            def dense_to(end):
                while at[0] < end:
                    n = at[0]
                    gi, c = CHUNKS[n]
                    name, _, _, cols, blocks = GROUPS[gi]
                    if c == 0 and gi >= 2:
                        pe.wait_ge(dense_ev, gi - 1)
                    if c == 0 and name == "uq0":
                        pe.wait_ge(lat_out, 16)
                    if name == "wk":
                        pe.wait_ge(tr_d, c + 1)
                    if name[:-1] in ("bs", "bm", "br") and name[-1] == "0":
                        pe.wait_ge(tr_d, 8 + n - END["mg1"] + 1)
                    if name == "o0":
                        pe.wait_ge(mt_dve, c + 1)
                    pe.wait_ge(split_lo, n + 1)
                    sh, sl, first = stationary(name)
                    w = n % HALF_RING
                    for kk in range(KC):
                        for h in range(HALVES):
                            k = c * KC + kk
                            o, t = D[gi % 2 * 2 + h][:, 0:cols], slice(h * P, (h + 1) * P)
                            mm(o, sh[:, first + k, t], wh[:, w, kk, 0:cols], k == 0, False)
                            mm(o, sh[:, first + k, t], wl[:, w, kk, 0:cols], False, False)
                            last = mm(o, sl[:, first + k, t], wh[:, w, kk, 0:cols], False, k == blocks - 1)
                    last.then_inc(freed, 1)
                    at[0] += 1

            def beat(count=1):
                for _ in range(count):
                    beats[0] += 1
                    dense_to(beat_at(beats[0]))

            def transposes(base):
                for s in range(8):
                    if s >= 4:
                        pe.wait_ge(tr_d, base + s - 3)
                    for i in range(2):
                        for h in range(HALVES):
                            k = 2 * s + i
                            last = nc.tensor.transpose(B[s % 4][:, i * 256 + h * P:i * 256 + (h + 1) * P],
                                                       xy[:, h, k * P:(k + 1) * P], ident)
                    last.then_inc(tr, 1)

            def rw_pair(p):
                e, d0, a0 = RW_PE * p, RW_DVE * p, RW_ACT * p
                c = slice(p * P, (p + 1) * P)
                if p == 0:
                    pe.wait_ge(cum_dve, 2)
                else:
                    pe.wait_ge(rw_dve, d0)
                for h in range(HALVES):
                    for i, s in enumerate((KK, R[:, :, 0:512], AA, R[:, :, 512:1024])):
                        last = nc.tensor.transpose(B[2 + h][:, i * P:(i + 1) * P], s[:, h, c], ident)
                last.then_inc(rw_pe, 1)
                beat()
                pe.wait_ge(rw_act, a0 + 1)
                pe.wait_ge(rw_dve, d0 + 1)
                for u in range(4):
                    a, h = u // 2, u % 2
                    r = slice(64 * a, 64 * a + 64)
                    mm(B[u][:, 0:256], TT[r, h, 256:384], TT[r, h, 0:256], True, True)
                    last = mm(B[u][:, 256:512], TT[r, h, 384:512], TT[r, h, 0:256], False, True)
                last.then_inc(rw_pe, 1)
                beat()
                pe.wait_ge(rw_dve, d0 + 3)
                for u in range(4):
                    last = nc.tensor.transpose(B[0][:, u * P:(u + 1) * P], TB[:, u, P:2 * P], ident)
                last.then_inc(rw_pe, 1)
                beat()
                for n in range(1, LEVELS + 1):
                    pe.wait_ge(*((rw_act, a0 + 2) if n == 1 else (rw_dve, d0 + 2 + n)))
                    pe.wait_ge(rw_pool, LEVELS * p + n)
                    for u in range(4):
                        last = mm(B[1][:, u * P:(u + 1) * P], LM[:, u, :], TB[:, u, 0:P], True, True)
                    last.then_inc(rw_pe, 1)
                    beat()
                    pe.wait_ge(rw_act, a0 + 2 + n)
                    for u in range(4):
                        o, w = B[2 + u // 2], u % 2 * 256
                        if n < LEVELS:
                            mm(o[:, w:w + P], TB[:, u, P:2 * P], XB[:, u, :], True, True)
                        last = mm(o[:, w + P:w + 2 * P], XB[:, u, :], TB[:, u, P:2 * P], True, True)
                    last.then_inc(rw_pe, 1)
                    beat()
                for h in range(HALVES):
                    v = R[:, h, 1024 + p * P:1024 + (p + 1) * P]
                    pe.wait_ge(rw_dve, d0 + 9 + h)
                    for a in range(2):
                        last = mm(B[0][:, a * P:(a + 1) * P], AM[:, 2 * a + h, 256:384], v, True, h == 0)
                        if h:
                            last = mm(B[0][:, a * P:(a + 1) * P], TT[:, 1, 0:P], ST, False, True)
                    last.then_inc(rw_pe, 1)
                    beat()
                    pe.wait_ge(rw_act, a0 + 9 + 2 * h)
                    for a in range(2):
                        last = mm(B[1][:, a * P:(a + 1) * P], TB[:, 2 * a + h, P:2 * P], YU[:, 0:P], True, True)
                    last.then_inc(rw_pe, 1)
                    beat()
                    pe.wait_ge(rw_act, a0 + 10 + 2 * h)
                    u = YU[:, P:2 * P]
                    if h == 0:
                        mm(B[0][:, 0:P], AA[:, 0, c], u, True, False)
                        mm(B[0][:, 0:P], R[:, 0, 512 + p * P:512 + (p + 1) * P], v, False, True)
                    for a in range(2):
                        o = B[2 + h][:, a * P:(a + 1) * P]
                        mm(o, AM[:, 2 * a + h, 128:256], u, True, False)
                        last = mm(o, AM[:, 2 * a + h, 384:512], v, False, h == 0)
                        if h:
                            last = mm(o, TT[:, 1, P:2 * P], ST, False, True)
                    last.then_inc(rw_pe, 1)
                    beat()

            def mla_head(m):
                b, i = m // 2 % 2, m % 2
                if i == 0:
                    pe.wait_ge(ml_qk, m // 2 + 1)
                if m:
                    pe.wait_ge(ml_dve, 3 * m)
                for h in range(HALVES):
                    nc.tensor.transpose(B[0][:, h * P:(h + 1) * P], MQ[:, b, h, i, 0:NOPE], ident)
                    nc.tensor.transpose(B[0][:, 256 + h * P:256 + (h + 1) * P], MKV[:, b, h, i, 0:NOPE], ident)
                    nc.tensor.transpose(B[1][0:64, h * P:(h + 1) * P], MQ[:, b, h, i, NOPE:QK], ident)
                    last = nc.tensor.transpose(B[1][0:64, 256 + h * P:256 + (h + 1) * P], KRH[:, h, i, :], ident)
                last.then_inc(ml_pe, 1)
                beat()
                pe.wait_ge(ml_act, 3 * m + 1)
                pe.wait_ge(ml_dve, 3 * m + 1)
                mm(B[2][:, 0:128], QKN[:, 0:128], QKN[:, 256:384], True, False)
                mm(B[2][:, 0:128], QKR[0:64, 0:128], QKR[0:64, 256:384], False, False)
                mm(B[2][:, 0:128], early, late, False, True)
                mm(B[2][:, 128:384], QKN[:, 128:256], QKN[:, 256:512], True, False)
                mm(B[2][:, 128:384], QKR[0:64, 128:256], QKR[0:64, 256:512], False, False)
                mm(B[2][:, 256:384], early, late, False, True).then_inc(ml_pe, 1)
                beat()
                pe.wait_ge(ml_act, 3 * m + 2)
                for n in range(3):
                    last = nc.tensor.transpose(B[3][:, n * P:(n + 1) * P], PP[:, n * P:(n + 1) * P], ident)
                last.then_inc(ml_pe, 1)
                beat()
                pe.wait_ge(ml_act, 3 * m + 3)
                v = [MKV[:, b, h, i, NOPE:NOPE + VD] for h in range(2)]
                mm(B[0][:, 0:128], PT[:, 0:128], v[0], True, True)
                mm(B[0][:, 128:256], PT[:, 128:256], v[0], True, False)
                mm(B[0][:, 128:256], PT[:, 256:384], v[1], False, True).then_inc(ml_pe, 1)
                beat()

            def sb_head(h):
                if h == 0:
                    pe.wait_ge(ml_dve, 24)
                    pe.wait_ge(dense_ev, GI["sv"] + 1)
                if h:
                    pe.wait_ge(sb_dve, 2 * h)
                for i in range(2):
                    for t in range(HALVES):
                        last = nc.tensor.transpose(B[0][:, i * 256 + t * P:i * 256 + (t + 1) * P],
                                                   SQKV[:, t, i * 512 + h * P:i * 512 + (h + 1) * P], ident)
                last.then_inc(sb_pe, 1)
                beat()
                pe.wait_ge(sb_act, 3 * h + 1)
                mm(B[1][:, 0:256], QKT[:, 256:384], QKT[:, 0:256], True, True)
                mm(B[1][:, 256:384], QKT[:, 384:512], QKT[:, 128:256], False, True).then_inc(sb_pe, 1)
                beat()
                pe.wait_ge(sb_pool, 2 * h + 1)
                mm(B[1][:, 0:256], ntri, LF[:, 0:256], False, True)
                mm(B[1][:, 128:256], none, LF[:, 256:384], False, True)
                mm(B[1][:, 256:384], ntri, LF[:, 256:384], False, True).then_inc(sb_pe, 1)
                beat()
                pe.wait_ge(sb_pool, 2 * h + 2)
                v = [SQKV[:, t, 1024 + h * P:1024 + (h + 1) * P] for t in range(HALVES)]
                mm(B[2][:, 0:128], AZ[:, 0:128], v[0], True, True)
                mm(B[2][:, 128:256], AZ[:, 128:256], v[0], True, False)
                mm(B[2][:, 128:256], AZ[:, 256:384], v[1], False, True).then_inc(sb_pe, 1)
                beat()

            pe.wait_ge(con_in, 16)
            with pe.Fori(0, DEPTH) as l:
                at[0] = beats[0] = 0
                pe.wait_ge(normed, 2)
                transposes(0)
                dense_to(AT_LORA)
                pe.wait_ge(tr_d, 8)
                pe.wait_ge(lora_dve, 1)
                for i in range(2):
                    for h in range(HALVES):
                        last = nc.tensor.transpose(B[i][0:64, h * P:(h + 1) * P],
                                                   WK[:, h, 64 + i * 64:128 + i * 64], ident)
                last.then_inc(lora_pe, 1)
                dense_to(AT_Z)
                pe.wait_ge(lora_act, 1)
                pe.wait_ge(lora_in, 64)
                for i, (lat, up) in enumerate(((WT, LW), (AT, LA))):
                    for h in range(HALVES):
                        last = mm(B[2 * i + h][:], lat[0:65, h * P:(h + 1) * P], up[0:65, :], True, True)
                last.then_inc(lora_pe, 1)
                dense_to(AT_LATENTS)
                pe.wait_ge(lora_act, 2)
                pe.wait_ge(lat_dve, 1)
                for i, s in enumerate((CQ, CKV)):
                    for k in range(4):
                        for h in range(HALVES):
                            last = nc.tensor.transpose(B[2 * i + k // 2][:, k % 2 * 256 + h * P:k % 2 * 256 + (h + 1) * P],
                                                       s[:, h, k * P:(k + 1) * P], ident)
                    last.then_inc(lat_pe, 1)
                dense_to(AT_DECAY)
                pe.wait_ge(lat_out, 16)
                for i, k in enumerate((K_INC, K_EXC)):
                    for h in range(HALVES):
                        last = mm(B[2 * i + h][:], con[:, k:k + P], SIG[:, h, :], True, True)
                last.then_inc(cum_pe, 1)
                pe.wait_ge(cum_act, 1)
                for p in range(4):
                    for h in range(HALVES):
                        last = mm(B[0][:, p:p + 1], SIG[:, h, p * P:(p + 1) * P],
                                  con[:, K_COL + h:K_COL + h + 1], h == 0, h == 1)
                last.then_inc(cum_pe, 1)
                pe.wait_ge(cum_act, 2)
                dense_to(AT_PAIRS)
                for p in range(4):
                    rw_pair(p)
                pe.wait_ge(rw_dve, 4 * RW_DVE)
                beat(GN_BEATS)
                for m in range(MLH):
                    if m % 2 == 0:
                        dense_to(END[f"ukv{m // 2}"])
                        beat(3)
                    mla_head(m)
                dense_to(END["sv"])
                for h in range(SBH):
                    sb_head(h)
                dense_to(END["mg1"])
                pe.wait_ge(silu_dve, 8)
                transposes(8)
                dense_to(END["br0"])
                for j in range(4):
                    dense_to(merged_at(j))
                    pe.wait_ge(merged, j + 1)
                    for s in range(2):
                        if j:
                            pe.wait_ge(mt_dve, 2 * j - 1 + s)
                        for k in range(2):
                            for h in range(HALVES):
                                kk = 2 * s + k
                                last = nc.tensor.transpose(B[s][:, k * 256 + h * P:k * 256 + (h + 1) * P],
                                                           MJ[:, j % 2, h, kk * P:(kk + 1) * P], ident)
                        last.then_inc(mt_pe, 1)
                dense_to(END["o3"])
                layer_end(pe, l)

        @block.scalar
        def _(act):
            at, group, beats, order = [0], [0], [0], [0]

            def f(o, i, fn=ACT.Copy, **kw):
                return nc.scalar.activation(o, i, fn, **kw)

            def link(ins):
                order[0] += 1
                ins.then_inc(act_seq, 1)
                act.wait_ge(act_seq, order[0])

            def split(n):
                if n < len(CHUNKS):
                    cols = GROUPS[CHUNKS[n][0]][3]
                    act.wait_ge(full[n % RING], filled(n))
                    if n >= HALF_RING:
                        act.wait_ge(freed, n - HALF_RING + 1)
                    f(wh[:, n % HALF_RING, :, 0:cols], ring[:, n % RING, :, 0:cols]).then_inc(split_hi, 1)

            def dense_to(end):
                while at[0] < end:
                    at[0] += 1
                    split(at[0] + LEAD - 1)
                    take_out(at[0])

            def take_out(end):
                while group[0] < len(GROUPS) and END[GROUPS[group[0]][0]] <= end:
                    gi = group[0]
                    name, _, _, cols, blocks = GROUPS[gi]
                    group[0] += 1
                    kind, no = name.rstrip("0123456789"), int(name[-1]) if name[-1].isdigit() else 0
                    if name.startswith("gate"):
                        no = int(name[4:])
                    if kind in ("bs", "bm", "br"):
                        n = 3 * no + ("bs", "bm", "br").index(kind)
                        act.wait_ge(gate_in[n % 3], 16 * (n // 3 + 1))
                        f(GT[:, n % 3, :, :], GT[:, n % 3, :, :], ACT.Sigmoid).then_inc(gate_sig, 1)
                        continue
                    if kind == "o":
                        continue
                    act.wait_ge(freed, END[name])
                    bank = [D[gi % 2 * 2 + h][:, 0:cols] for h in range(HALVES)]
                    scale = 1.0
                    if kind in ("rg", "sg", "mg"):
                        n = ("rg", "sg", "mg0", "mg1").index(name)
                        if n < 2:
                            act.wait_ge(spilled[n], 16 * 6)
                        else:
                            act.wait_ge(silu_dve, 2 * (n - 1))
                        for h in range(HALVES):
                            last = f(gev[:, n % 2, h, :], bank[h], ACT.Sigmoid)
                        last.then_inc(silu_sig, 1)
                        continue
                    if kind == "gate":
                        if no >= 2:
                            act.wait_ge(spilled[no % 2], 16 * (no // 2))
                        dst = [gev[:, no % 2, h, :] for h in range(HALVES)]
                    elif kind == "wk":
                        bank = [b[:, 0:192] for b in bank]
                        dst = [WK[:, h, :] for h in range(HALVES)]
                    elif name in ("rr", "rk", "rv"):
                        i = ("rr", "rk", "rv").index(name)
                        dst = [R[:, h, i * 512:(i + 1) * 512] for h in range(HALVES)]
                    elif name in ("sq", "sk", "sv"):
                        i = ("sq", "sk", "sv").index(name)
                        scale = SB_SCALE if i == 0 else 1.0
                        if i == 0:
                            act.wait_ge(gn_done, 1)
                        dst = [SQKV[:, h, i * 512:(i + 1) * 512] for h in range(HALVES)]
                    elif name in ("cq", "ckv"):
                        dst = [(CQ if name == "cq" else CKV)[:, h, :] for h in range(HALVES)]
                    else:
                        act.wait_ge(lat_out, 16)
                        act.wait_ge(cum_dve, 1)
                        if no >= 2:
                            act.wait_ge(ml_dve, 6 * (no - 1))
                        t = MQ if kind == "uq" else MKV
                        dst = [t[:, no % 2, h, :, :] for h in range(HALVES)]
                        bank = [b.rearrange("p (n c) -> p n c", n=2) for b in bank]
                    for h in range(HALVES):
                        last = f(dst[h], bank[h], scale=scale)
                    last.then_inc(dense_ev, 1)

            def beat(count=1):
                for _ in range(count):
                    beats[0] += 1
                    dense_to(beat_at(beats[0]))

            def rw_pair(p):
                e = RW_PE * p
                act.wait_ge(rw_pe, e + 1)
                f(TT[:, 0, :], B[2][:]).then_inc(rw_act, 1)
                beat()
                beat()
                act.wait_ge(rw_pe, e + 3)
                f(TB[:, :, 0:P], B[0][:].rearrange("p (u c) -> p u c", u=4)).then_inc(rw_act, 1)
                beat()
                for n in range(1, LEVELS + 1):
                    act.wait_ge(rw_pe, e + 2 + 2 * n)
                    f(XB, B[1][:].rearrange("p (u c) -> p u c", u=4)).then_inc(rw_act, 1)
                    beat()
                    beat()
                for h in range(HALVES):
                    for k in range(2):
                        act.wait_ge(rw_pe, e + 16 + 3 * h + k)
                        f(as_pair(YU[:, k * P:(k + 1) * P]), own(B[k])).then_inc(rw_act, 1)
                        beat()
                    beat()

            def mla_pair(p):
                b = p % 2
                dense_to(END[f"ukv{p}"])
                act.wait_ge(dense_ev, GI[f"ukv{p}"] + 1)
                if p:
                    act.wait_ge(ml_ss, 2 * p)
                q2 = QS.rearrange("p (h n c) -> p h n c", h=2, n=2)
                f(q2, MQ[:, b, :, :, :], ACT.Square).then_inc(ml_sq, 1)
                act.wait_ge(ml_ss, 2 * p + 1)
                f(q2[:, :, :, 0:NOPE], MKV[:, b, :, :, 0:NOPE], ACT.Square).then_inc(ml_sq, 1)
                act.wait_ge(ml_ss, 2 * p + 2)
                link(f(qss, qss, ACT.Ln, scale=1.0 / QK, bias=eps))
                link(f(nss, nss, ACT.Ln, scale=1.0 / QK, bias=eps))
                f(qss, qss, ACT.Exp, scale=-0.5)
                f(nss, nss, ACT.Exp, scale=-0.5).then_inc(ml_rs, 1)
                beat(3)
                for m in (2 * p, 2 * p + 1):
                    act.wait_ge(ml_pe, 4 * m + 1)
                    f(QKN[:, 0:256], B[0][:, 0:256], scale=gg)
                    f(QKN[:, 256:512], B[0][:, 256:512]).then_inc(ml_act, 1)
                    beat()
                    act.wait_ge(ml_dve, 3 * m + 2)
                    f(PP[:, 0:128], B[2][:, 0:128], ACT.Exp, scale=ML_SCALE, bias=nb[:, 0:1], accum_out=den[:, 0:1])
                    f(PP[:, 128:384], B[2][:, 128:384], ACT.Exp, scale=ML_SCALE, bias=nb[:, 1:2],
                      accum_out=den[:, 1:2]).then_inc(ml_act, 1)
                    beat()
                    act.wait_ge(ml_pe, 4 * m + 3)
                    f(PT, B[3][:, 0:384]).then_inc(ml_act, 1)
                    beat()
                    beat()

            def sb_head(h):
                act.wait_ge(sb_pe, 4 * h + 1)
                f(QKT, B[0][:]).then_inc(sb_act, 1)
                beat()
                act.wait_ge(sb_pe, 4 * h + 2)
                link(f(AZ, B[1][:, 0:384], ACT.Abs))
                link(f(AZ, AZ, ACT.Exp, scale=-1.0))
                f(LG, AZ, ACT.Ln, bias=1.0).then_inc(sb_act, 1)
                beat()
                act.wait_ge(sb_pe, 4 * h + 3)
                act.wait_ge(sb_act, 3 * h + 2)
                f(AZ, B[1][:, 0:384], ACT.Exp).then_inc(sb_act, 1)
                beat()
                beat()

            act.wait_ge(x_first, 16)
            act.wait_ge(once, 3)
            with act.Fori(0, DEPTH) as l:
                at[0] = group[0] = beats[0] = order[0] = 0
                act.preload_act_table_set("natural_log_exp_and_others")
                link(f(arena[:, 0:DM], xy[:, 0, :], ACT.Square, accum_out=ss[:, 0:1]))
                link(f(arena[:, 0:DM], xy[:, 1, :], ACT.Square, accum_out=ss[:, 1:2]))
                link(f(rs, ss, ACT.Ln, scale=1.0 / DM, bias=eps))
                f(rs, rs, ACT.Exp, scale=-0.5).then_inc(rstd, 1)
                for n in range(LEAD):
                    split(n)
                act.wait_ge(small_in, 16 * 5)
                for s in range(8):
                    act.wait_ge(tr, s + 1)
                    for i in range(2):
                        k = 2 * s + i
                        last = f(hth[:, k, :], B[s % 4][:, i * 256:(i + 1) * 256], scale=ng[:, k:k + 1])
                    last.then_inc(tr_a, 1)
                dense_to(AT_LORA)
                act.wait_ge(lora_pe, 1)
                act.wait_ge(preset, 5)
                f(WT[0:64, :], B[0][0:64, 0:256], ACT.Tanh)
                f(AT[0:64, :], B[1][0:64, 0:256]).then_inc(lora_act, 1)
                dense_to(AT_Z)
                act.preload_act_table_set("sigmoid_and_others")
                act.wait_ge(lora_pe, 2)
                act.wait_ge(mixed, 3)
                for i, t in enumerate((SIG, AA)):
                    for h in range(HALVES):
                        last = f(t[:, h, :], B[2 * i + h][:], ACT.Sigmoid)
                last.then_inc(lora_act, 1)
                act.preload_act_table_set("natural_log_exp_and_others")
                dense_to(AT_KK + 1)
                act.wait_ge(kk_ss, 1)
                link(f(kss, kss, ACT.Ln, scale=2.0 ** 20))
                f(kss, kss, ACT.Exp, scale=-0.5, bias=bias_kk).then_inc(kk_rs, 1)
                dense_to(END["ckv"])
                for i, t in enumerate((CQ, CKV)):
                    if i == 0:
                        act.wait_ge(dense_ev, GI["ckv"] + 1)
                    for h in range(HALVES):
                        link(f(QS[:, 0:512], t[:, h, :], ACT.Square, accum_out=css[:, 2 * i + h:2 * i + h + 1]))
                for h in range(HALVES):
                    link(f(QS[:, 0:64], WK[:, h, 0:64], ACT.Square, accum_out=krs[:, h:h + 1]))
                link(f(css, css, ACT.Ln, scale=1.0 / LORA, bias=eps))
                f(css, css, ACT.Exp, scale=-0.5).then_inc(lat_act, 1)
                dense_to(AT_LATENTS)
                act.wait_ge(lat_pe, 1)
                for i, (t, g) in enumerate(((cqh, cqg), (ckh, ckg))):
                    act.wait_ge(lat_pe, i + 1)
                    for k in range(4):
                        f(t[:, k, :], B[2 * i + k // 2][:, k % 2 * 256:(k % 2 + 1) * 256], scale=g[:, k:k + 1]
                          ).then_inc(lat_hi, 1)
                dense_to(AT_DECAY)
                act.wait_ge(cum_pe, 1)
                act.wait_ge(ops_done, 1)
                for h in range(HALVES):
                    f(S1[:, h, :], B[h][:], ACT.Exp, scale=-1.0)
                    f(S2[:, h, :], B[h][:], ACT.Exp)
                    last = f(S3[:, h, :], B[2 + h][:], ACT.Exp)
                last.then_inc(cum_act, 1)
                act.wait_ge(cum_pe, 2)
                f(scv, B[0][:, 0:4], ACT.Exp).then_inc(cum_act, 1)
                dense_to(AT_PAIRS)
                for p in range(4):
                    rw_pair(p)
                beat(4)
                act.wait_ge(gn_var, 1)
                link(f(var, var, ACT.Ln, scale=1.0 / 64, bias=eps_gn))
                f(var, var, ACT.Exp, scale=-0.5).then_inc(gn_rs, 1)
                beat(GN_BEATS - 4)
                for p in range(4):
                    mla_pair(p)
                dense_to(END["sv"])
                for h in range(SBH):
                    sb_head(h)
                dense_to(END["mg1"])
                for s in range(8):
                    act.wait_ge(tr, 8 + s + 1)
                    f(hth[:, 2 * s:2 * s + 2, :], B[s % 4][:].rearrange("p (k t) -> p k t", k=2)).then_inc(tr_a, 1)
                for j in range(4):
                    dense_to(merged_at(j))
                    for s in range(2):
                        act.wait_ge(mt_pe, 2 * j + s + 1)
                        f(mth[:, 4 * j + 2 * s:4 * j + 2 * s + 2, :],
                          B[s][:].rearrange("p (k t) -> p k t", k=2)).then_inc(mt_act, 1)
                dense_to(END["o3"])
                layer_end(act, l)

        @block.vector
        def _(dve):
            v = nc.vector
            at, group, beats, order = [0], [GI["rg"]], [0], [0]

            def link(ins):
                order[0] += 1
                ins.then_inc(dve_seq, 1)
                dve.wait_ge(dve_seq, order[0])

            def tt(o, a, b, op):
                return v.tensor_tensor(o, a, b, op)

            def split(n):
                if n < len(CHUNKS):
                    cols, slot = GROUPS[CHUNKS[n][0]][3], n % HALF_RING
                    dve.wait_ge(split_hi, n + 1)
                    tt(wl[:, slot, :, 0:cols], ring[:, n % RING, :, 0:cols], wh[:, slot, :, 0:cols].bitcast(F32),
                       ALU.subtract).then_inc(split_lo, 1)

            def dense_to(end):
                while at[0] < end:
                    at[0] += 1
                    split(at[0] + LEAD - 1)
                    while group[0] < len(GROUPS) and END[GROUPS[group[0]][0]] <= at[0]:
                        take_out(group[0])
                        group[0] += 1

            def beat(count=1):
                for _ in range(count):
                    beats[0] += 1
                    dense_to(beat_at(beats[0]))

            def take_out(gi):
                name = GROUPS[gi][0]
                kind, j = name.rstrip("0123456789"), int(name[-1]) if name[-1].isdigit() else 0
                bank = [D[gi % 2 * 2 + h][:] for h in range(HALVES)]
                if kind in ("rg", "sg", "mg"):
                    n = ("rg", "sg", "mg0", "mg1").index(name)
                    dve.wait_ge(silu_sig, n + 1)
                    for h in range(HALVES):
                        last = tt(gev[:, n % 2, h, :], gev[:, n % 2, h, :], bank[h], ALU.mult)
                    last.then_inc(dense_ev, 1)
                    dve.wait_ge(dense_ev, gi + 1)
                    c0 = (1536, 0, 512, 1024)[n]
                    y = xy[:, :, c0:c0 + 512]
                    tt(y, y, gev[:, n % 2, :, :], ALU.mult).then_inc(silu_dve, 2)
                elif kind in ("bs", "bm", "br"):
                    b = ("bs", "bm", "br").index(kind)
                    dve.wait_ge(gate_sig, 3 * j + b + 1)
                    dve.wait_ge(freed, END[name])
                    if b == 0 and j >= 2:
                        dve.wait_ge(mt_pe, 2 * (j - 1))
                    o = MJ[:, j % 2, :, :] if b == 0 else MG
                    for h in range(HALVES):
                        last = tt(o[:, h, :], GT[:, b, h, :], bank[h], ALU.mult)
                    last.then_inc(dense_ev, 1)
                    dve.wait_ge(dense_ev, gi + 1)
                    if b:
                        link(tt(MJ[:, j % 2, :, :], MJ[:, j % 2, :, :], MG, ALU.add))
                    v.sem_inc(gate_used, 1)
                    if b == 2:
                        v.sem_inc(merged, 1)
                else:
                    if j == 0:
                        dve.wait_ge(x_in, 16)
                    dve.wait_ge(freed, END[name])
                    for h in range(HALVES):
                        t = xy[:, h, j * 512:(j + 1) * 512]
                        last = tt(t, t, bank[h], ALU.add)
                    last.then_inc(x_new, 1)
                    dve.wait_ge(x_new, j + 1)
                    v.sem_inc(dense_ev, 1)

            def over_halves(row):
                return row.unsqueeze(1).to_broadcast([P, HALVES, row.shape[-1]])

            def rope(src, dst, tmp, n):
                x1, x2 = src[:, :, :, 0:32], src[:, :, :, 32:64]
                t1, t2 = (tmp[:, i * 64 * n:(i + 1) * 64 * n].rearrange("p (h n c) -> p h n c", h=2, n=n) for i in range(2))
                cs, sn = (t.unsqueeze(2).to_broadcast([P, HALVES, n, 32]) for t in (cosx, sinx))
                tt(t1, x1, cs, ALU.mult)
                link(tt(t2, x2, sn, ALU.mult))
                link(tt(dst[:, :, :, 0:32], t1, t2, ALU.subtract))
                tt(t1, x1, sn, ALU.mult)
                link(tt(t2, x2, cs, ALU.mult))
                link(tt(dst[:, :, :, 32:64], t1, t2, ALU.add))

            def split_heads(t, h):
                return t[:, h, :].rearrange("p (n c) -> p n c", c=64)

            def per_head(o, t, s, op=ALU.mult):
                for h in range(HALVES):
                    last = tt(split_heads(o, h), split_heads(t, h),
                              s[:, 8 * h:8 * h + 8].unsqueeze(2).to_broadcast([P, 8, 64]), op)
                return last

            def head_sums(o, t):
                for h in range(HALVES):
                    last = v.tensor_reduce(o[:, 8 * h:8 * h + 8], split_heads(t, h), axis=X, op=ALU.add)
                return last

            def rw_pair(p):
                e = RW_PE * p
                c = slice(p * P, (p + 1) * P)
                dve.wait_ge(rw_pe, e + 1)
                v.tensor_copy(TT[:, 1, :], B[3][:]).then_inc(rw_dve, 1)
                beat()
                dve.wait_ge(rw_pe, e + 2)
                if p:
                    dve.wait_ge(rw_pool, LEVELS * p)
                for u in range(4):
                    last = v.copy_predicated(AM[:, u, :], con[:, K_RWM:K_RWM + 512].bitcast(U32), B[u][:])
                last.then_inc(rw_dve, 1)
                dve.wait_ge(rw_dve, RW_DVE * p + 2)
                link(tt(TB[:, :, P:2 * P], AM[:, :, 0:P], level[0].unsqueeze(1).to_broadcast([P, 4, P]), ALU.mult))
                tt(TB[:, :, P:2 * P], TB[:, :, P:2 * P], ident.unsqueeze(1).to_broadcast([P, 4, P]), ALU.add
                   ).then_inc(rw_dve, 1)
                beat(2)
                for n in range(1, LEVELS + 1):
                    beat()
                    dve.wait_ge(rw_pe, e + 3 + 2 * n)
                    for i in range(2):
                        t = TB[:, 2 * i:2 * i + 2, :] if n < LEVELS else TB[:, 2 * i:2 * i + 2, P:2 * P]
                        b = B[2 + i][:].rearrange("p (u c) -> p u c", u=2)
                        last = tt(t, t, b if n < LEVELS else b[:, :, P:2 * P], ALU.add)
                    last.then_inc(rw_dve, 1)
                    beat()
                for h in range(HALVES):
                    beat(2)
                    dve.wait_ge(rw_pe, e + 18 + 3 * h)
                    if h == 0:
                        for a in range(2):
                            d = slice(64 * a, 64 * a + 64)
                            v.tensor_scalar(ST[d, d], B[0][d, d], scv[d, p:p + 1], None, ALU.mult)
                    v.tensor_copy(as_pair(S2[:, h, c]), own(B[2 + h])).then_inc(rw_dve, 1)
                    beat()

            def mla_pair(p):
                b = p % 2
                dense_to(END[f"ukv{p}"])
                dve.wait_ge(ml_sq, 2 * p + 1)
                q2 = QS.rearrange("p (a c) -> p a c", a=4)
                v.tensor_reduce(qss, q2, axis=X, op=ALU.add).then_inc(ml_ss, 1)
                dve.wait_ge(ml_sq, 2 * p + 2)
                link(v.tensor_reduce(nss, q2[:, :, 0:NOPE], axis=X, op=ALU.add))
                nss2 = nss.rearrange("p (h n) -> p h n", h=2)
                tt(nss2, nss2, krs.unsqueeze(2).to_broadcast([P, 2, 2]), ALU.add).then_inc(ml_ss, 1)
                beat()
                dve.wait_ge(ml_rs, p + 1)
                mq, mk = MQ[:, b, :, :, :], MKV[:, b, :, :, :]
                for h in range(HALVES):
                    for i in range(2):
                        k = 2 * h + i
                        v.tensor_scalar(mq[:, h, i, :], mq[:, h, i, :], qss[:, k:k + 1], None, ALU.mult)
                        v.tensor_scalar(mk[:, h, i, 0:NOPE], mk[:, h, i, 0:NOPE], nss[:, k:k + 1], None, ALU.mult)
                        last = v.tensor_scalar(KRH[:, h, i, :], KR[:, h, :], nss[:, k:k + 1], None, ALU.mult)
                link(last)
                beat()
                for h in range(HALVES):
                    last = tt(mq[:, h, :, NOPE:QK], mq[:, h, :, NOPE:QK],
                              GR[:, 0:64].unsqueeze(1).to_broadcast([P, 2, 64]), ALU.mult)
                link(last)
                rope(mq[:, :, :, NOPE:QK], QS[:, 0:256].rearrange("p (h n c) -> p h n c", h=2, n=2), QS[:, 256:512], 2)
                v.tensor_copy(mq[:, :, :, NOPE:QK], QS[:, 0:256].rearrange("p (h n c) -> p h n c", h=2, n=2)
                              ).then_inc(ml_qk, 1)
                beat()
                for m in (2 * p, 2 * p + 1):
                    dve.wait_ge(ml_pe, 4 * m + 1)
                    v.tensor_copy(QKR[0:64, :], B[1][0:64, :]).then_inc(ml_dve, 1)
                    beat()
                    dve.wait_ge(ml_pe, 4 * m + 2)
                    v.reduce_max(mx[:, 0:1], B[2][:, 0:128], axis=X)
                    link(v.reduce_max(mx[:, 1:2], B[2][:, 128:384], axis=X))
                    v.tensor_scalar(nb, mx, -ML_SCALE, None, ALU.mult).then_inc(ml_dve, 1)
                    beat()
                    dve.wait_ge(ml_act, 3 * m + 2)
                    link(v.reciprocal(rden, den))
                    beat()
                    dve.wait_ge(ml_pe, 4 * m + 4)
                    c0 = 512 + m * VD
                    for h in range(HALVES):
                        last = v.tensor_scalar(xy[:, h, c0:c0 + VD], B[0][:, h * P:(h + 1) * P], rden[:, h:h + 1],
                                               None, ALU.mult)
                    last.then_inc(ml_dve, 1)
                    beat()

            def sb_head(h):
                beat(2)
                dve.wait_ge(sb_act, 3 * h + 2)
                v.scalar_tensor_tensor(LF, B[1][:, 0:384], 0.0, LG, ALU.max, ALU.add).then_inc(sb_dve, 1)
                beat()
                dve.wait_ge(sb_pe, 4 * h + 4)
                v.tensor_copy(xy[:, :, h * P:(h + 1) * P], B[2][:, 0:256].rearrange("p (h c) -> p h c", h=2)
                              ).then_inc(sb_dve, 1)
                beat()

            dve.wait_ge(con_in, 16)
            with dve.Fori(0, DEPTH) as l:
                at[0] = beats[0] = order[0] = 0
                group[0] = GI["rg"]
                dve.wait_ge(rstd, 1)
                for h in range(HALVES):
                    v.tensor_scalar(xy[:, h, :], xy[:, h, :], rs[:, h:h + 1], None, ALU.mult).then_inc(normed, 1)
                for n in range(LEAD):
                    split(n)
                dve.wait_ge(small_in, 16 * 5)
                tt(gg, gq, gk, ALU.mult).then_inc(lat_gain, 1)
                for s in range(8):
                    dve.wait_ge(tr_a, s + 1)
                    for i in range(2):
                        k = 2 * s + i
                        last = v.scalar_tensor_tensor(htl[:, k, :], B[s % 4][:, i * 256:(i + 1) * 256], ng[:, k:k + 1],
                                                      hth[:, k, :].bitcast(F32), ALU.mult, ALU.subtract)
                    last.then_inc(tr_d, 1)
                dense_to(AT_LORA)
                dve.wait_ge(mu_in, 16)
                for s in wk_shift:
                    dve.wait_ge(s, 16)
                lat = WK[:, :, 64:192]
                link(tt(PW, PW, lat, ALU.subtract))
                link(tt(PW, PW, over_halves(MU[:, 1536:1664]), ALU.mult))
                tt(lat, lat, PW, ALU.add).then_inc(lora_dve, 1)
                for i in range(3):
                    dense_to(AT_MIX[i])
                    for s in r_shift[2 * i:2 * i + 2]:
                        dve.wait_ge(s, 16)
                    c = slice(i * 512, (i + 1) * 512)
                    link(tt(PV[:, :, c], PV[:, :, c], R[:, :, c], ALU.subtract))
                    link(tt(PV[:, :, c], PV[:, :, c], over_halves(MU[:, c]), ALU.mult))
                    tt(R[:, :, c], R[:, :, c], PV[:, :, c], ALU.add).then_inc(mixed, 1)
                dense_to(AT_KK)
                dve.wait_ge(mixed, 3)
                rr, rk, rv = (R[:, :, i * 512:(i + 1) * 512] for i in range(3))
                k_k, k_a, r_k = (over_halves(ROWS[:, i * 512:(i + 1) * 512]) for i in range(3))
                gn_g, gn_b = k_k, k_a
                dve.wait_ge(rows_in, 16 * 5)
                link(tt(KK, rk, k_k, ALU.mult))
                link(tt(S1, KK, KK, ALU.mult))
                dense_to(AT_KK + 1)
                link(head_sums(kss, S1))
                v.tensor_scalar(kss, kss, 1e-24, None, ALU.max).then_inc(kk_ss, 1)
                dve.wait_ge(lora_act, 2)
                for h in range(HALVES):
                    last = v.scalar_tensor_tensor(S1[:, h, :], AA[:, h, :], -1.0, ROWS[:, 512:1024], ALU.add, ALU.mult)
                link(last)
                dense_to(AT_KK + 2)
                for h in range(HALVES):
                    last = v.scalar_tensor_tensor(R[:, h, 512:1024], S1[:, h, :], 1.0, R[:, h, 512:1024], ALU.add, ALU.mult)
                link(last)
                dve.wait_ge(kk_rs, 1)
                dense_to(AT_KK + 3)
                link(per_head(KK, KK, kss))
                dense_to(AT_KK + 4)
                link(tt(AA, AA, KK, ALU.mult))
                dense_to(AT_KK + 5)
                link(tt(S1, rr, rk, ALU.mult))
                dense_to(AT_KK + 6)
                link(tt(S1, S1, r_k, ALU.mult))
                dense_to(AT_KK + 7)
                head_sums(bon, S1).then_inc(ops_done, 1)
                link(tt(KR, WK[:, :, 0:64], over_halves(GR[:, 64:128]), ALU.mult))
                dst = QS[:, 640:768].rearrange("p (h n c) -> p h n c", h=2, n=1)
                rope(KR.unsqueeze(2), dst, QS[:, 512:640], 1)
                link(v.tensor_copy(KR, dst[:, :, 0, :]))
                dense_to(END["ckv"] + 1)
                dve.wait_ge(lat_act, 1)
                for i, t in enumerate((CQ, CKV)):
                    for h in range(HALVES):
                        last = v.tensor_scalar(t[:, h, :], t[:, h, :], css[:, 2 * i + h:2 * i + h + 1], None, ALU.mult)
                last.then_inc(lat_dve, 1)
                dense_to(AT_LATENTS)
                for i, (hi, lo, g) in enumerate(((cqh, cql, cqg), (ckh, ckl, ckg))):
                    dve.wait_ge(lat_hi, 4 * i + 4)
                    for k in range(4):
                        v.scalar_tensor_tensor(lo[:, k, :], B[2 * i + k // 2][:, k % 2 * 256:(k % 2 + 1) * 256],
                                               g[:, k:k + 1], hi[:, k, :].bitcast(F32), ALU.mult, ALU.subtract
                                               ).then_inc(lat_out, 2)
                dense_to(AT_DECAY)
                dve.wait_ge(cum_act, 1)
                tt(rr, rr, S2, ALU.mult)
                tt(rk, rk, S1, ALU.mult)
                dense_to(AT_DECAY + 1)
                tt(AA, AA, S1, ALU.mult)
                for h in range(HALVES):
                    last = v.scalar_tensor_tensor(KK[:, h, :], KK[:, h, :], -1.0, S3[:, h, :], ALU.mult, ALU.mult)
                last.then_inc(cum_dve, 2)
                dve.wait_ge(cum_dve, 2)
                dve.wait_ge(cum_act, 2)
                dve.wait_ge(preset, 6)
                dense_to(AT_PAIRS)
                for p in range(4):
                    rw_pair(p)
                dve.wait_ge(rw_dve, 4 * RW_DVE)
                link(head_sums(mean, S2))
                link(v.tensor_scalar(mean, mean, 1.0 / 64, None, ALU.mult))
                beat()
                link(per_head(S2, S2, mean, ALU.subtract))
                beat()
                link(tt(S1, S2, S2, ALU.mult))
                beat()
                head_sums(var, S1).then_inc(gn_var, 1)
                dve.wait_ge(gn_var, 1)
                beat()
                per_head(S1, rv, bon)
                beat()
                dve.wait_ge(gn_rs, 1)
                link(per_head(S2, S2, var))
                beat()
                dve.wait_ge(gn_in, 32)
                link(tt(S2, S2, gn_g, ALU.mult))
                beat()
                link(tt(S2, S2, gn_b, ALU.add))
                tt(S2, S2, S1, ALU.add).then_inc(gn_done, 1)
                dve.wait_ge(gn_done, 1)
                beat()
                for p in range(4):
                    mla_pair(p)
                dense_to(END["sv"])
                for h in range(SBH):
                    sb_head(h)
                dve.wait_ge(sb_dve, 2 * SBH)
                dve.wait_ge(ml_dve, 3 * MLH)
                dense_to(END["mg1"])
                for s in range(8):
                    dve.wait_ge(tr_a, 8 + s + 1)
                    tt(htl[:, 2 * s:2 * s + 2, :], B[s % 4][:].rearrange("p (k t) -> p k t", k=2),
                       hth[:, 2 * s:2 * s + 2, :].bitcast(F32), ALU.subtract).then_inc(tr_d, 1)
                for j in range(4):
                    dense_to(merged_at(j))
                    for s in range(2):
                        dve.wait_ge(mt_act, 2 * j + s + 1)
                        k = slice(4 * j + 2 * s, 4 * j + 2 * s + 2)
                        tt(mtl[:, k, :], B[s][:].rearrange("p (k t) -> p k t", k=2), mth[:, k, :].bitcast(F32),
                           ALU.subtract).then_inc(mt_dve, 1)
                dense_to(END["o3"])
                layer_end(dve, l)


NAMES = ["x", "norm_g", "w_in", "mla_q_norm_g", "mla_kv_norm_g", "mla_w_uq", "mla_w_ukv", "mla_qn_g", "mla_kn_g",
         "rw_mu", "rw_w0", "rw_w_up", "rw_a0", "rw_a_up", "rw_k_k", "rw_k_a", "rw_r_k", "rw_gn_g", "rw_gn_b",
         "w_br_sb", "w_br_mla", "w_br_rw", "w_out"]


def kernel(**inputs):
    import concourse.bacc as bacc
    from concourse.bass_utils import run_bass_kernel_spmd

    nc = bacc.Bacc("TRN2", target_bir_lowering=False, num_devices=1)
    arrays, args = {}, []
    for name in NAMES:
        a = np.ascontiguousarray(inputs[name])
        arrays["in_" + name] = a
        args.append(nc.dram_tensor("in_" + name, a.shape, mybir.dt.from_np(a.dtype), kind="ExternalInput").ap())
    arrays["in_consts"] = constants()
    args.append(nc.dram_tensor("in_consts", (P, K_END), F32, kind="ExternalInput").ap())
    args.append(nc.dram_tensor("out_x", (1, SEQ, DM), F32, kind="ExternalOutput").ap())
    args.append(nc.dram_tensor("gate_spill", (12, SEQ, 512), F32, kind="Internal").ap())
    program(nc, *args)
    r = run_bass_kernel_spmd(nc, [arrays], core_ids=[0])
    return r.results[0]["out_x"]
```

```python
import numpy as np
import concourse.bass as bass
from concourse import mybir
from contextlib import ExitStack

F32 = mybir.dt.float32
U32 = mybir.dt.uint32
F32R = mybir.dt.float32r
ALU = mybir.AluOpType
ACT = mybir.ActivationFunctionType
X = mybir.AxisListType.X

DEPTH, SEQ, DM = 2, 256, 2048
P = 128
HALVES = SEQ // P
KD = DM // P
SBH, MLH = 4, 8
NOPE, ROPE, VD = 128, 64, 128
QK = NOPE + ROPE
LORA = 512
RWW = 512
EPS = 1e-6
C_SB = 0
C_CQ = 2048
C_CKV = C_CQ + LORA
C_KR = C_CKV + LORA
C_MG = C_KR + ROPE
C_RW = C_MG + MLH * VD
C_WD = C_RW + 3 * RWW
C_RG = C_WD + 128
C_GATE = C_RG + RWW
DECAY = float(np.exp(-0.5))
MID = P // 2 - 1
LEVELS = 6
KC = 2
RING = 4
HALF_RING = 4
LEAD = HALF_RING - 1
ARENA = 18700
SB_SCALE = 128.0 ** -0.5
ML_SCALE = QK ** -0.5
MASKED = -1e30

K_ID, K_INC, K_NTRI, K_NONE, K_RWM, K_LEV = 0, 128, 256, 384, 512, 1024
K_COS = K_LEV + (LEVELS + 1) * 128
K_SIN = K_COS + 64
K_COL = K_SIN + 64
K_MASK = K_COL + 2
K_END = K_MASK + 4 * P


def constants():
    c = np.zeros((P, K_END), np.float32)
    i = np.arange(P)
    row, col = i[:, None], i[None, :]
    c[:, K_ID:K_ID + P] = row == col
    past_mid = (row <= MID).astype(np.float32)
    c[:, K_INC:K_INC + P] = -DECAY * ((row <= col).astype(np.float32) - past_mid)
    c[:, K_NTRI:K_NTRI + P] = -(row >= col).astype(np.float32)
    c[:, K_NONE:K_NONE + P] = -1.0
    strict, incl = (row < col), (row <= col)
    c[:, K_RWM:K_RWM + 512] = np.concatenate([strict, incl, strict, incl], 1)
    for n in range(LEVELS + 1):
        b = 2 ** n
        c[:, K_LEV + n * P:K_LEV + (n + 1) * P] = (row // (2 * b) == col // (2 * b)) & (row // b < col // b)
    half = ROPE // 2
    freqs = (np.float32(10000.0) ** (-np.arange(half, dtype=np.float32) / np.float32(half))).astype(np.float32)
    ang = np.arange(SEQ, dtype=np.float32)[:, None] * freqs[None, :]
    for h in range(HALVES):
        c[:, K_COS + h * half:K_COS + (h + 1) * half] = np.cos(ang[h * P:(h + 1) * P])
        c[:, K_SIN + h * half:K_SIN + (h + 1) * half] = np.sin(ang[h * P:(h + 1) * P])
    c[:, K_COL] = -DECAY * (i > MID)
    c[:, K_COL + 1] = -DECAY * (i <= MID)
    for h in range(HALVES):
        c[ROPE + h, K_MASK + h * P:K_MASK + h * P + 64] = MASKED
        c[ROPE + h, K_MASK + (2 + h) * P + 64:K_MASK + (3 + h) * P] = 1.0
    return c


def groups():
    def wide(name, c0):
        return [(name, "w_in", c0, 512, KD)]

    def pair(p):
        return [(f"uq{p}", "uq", p * 2 * QK, 2 * QK, 4), (f"ukv{p}", "ukv", p * 512, 512, 4)]

    gates = [wide(f"gate{n}", C_GATE + n * 512)[0] for n in range(12)]
    g = [("wk", "w_in", C_KR, 256, KD)]
    g += wide("rr", C_RW) + wide("rk", C_RW + 512) + wide("rv", C_RW + 1024)
    g += gates[:1] + wide("cq", C_CQ) + wide("ckv", C_CKV)
    g += gates[1:9] + pair(0) + pair(1) + gates[9:11] + wide("sq", C_SB) + pair(2)
    g += wide("sk", C_SB + 512) + wide("sv", C_SB + 1024) + pair(3)
    g += [("rg", "w_in", C_RG + 64, 448, KD)] + gates[11:]
    g += wide("mg0", C_MG) + wide("mg1", C_MG + 512) + wide("sg", C_SB + 1536)
    for j in range(4):
        g += [(f"br{j}", "br", j * 512, 512, 4), (f"bm{j}", "bm", j * 512, 512, 8), (f"bs{j}", "bs", j * 512, 512, 4)]
    g += [(f"o{j}", "w_out", j * 512, 512, KD) for j in range(4)]
    return g


GROUPS = groups()
CHUNKS = [(gi, c) for gi, g in enumerate(GROUPS) for c in range(g[4] // KC)]
GI = {g[0]: i for i, g in enumerate(GROUPS)}
NEXT = [(0, c) for c in range(LEAD)]
assert LEAD <= min(RING, 4)
assert len(CHUNKS) % RING == 0 and len(CHUNKS) % HALF_RING == 0
assert DEPTH & (DEPTH - 1) == 0
END = {g[0]: sum(x[4] // KC for x in GROUPS[:i + 1]) for i, g in enumerate(GROUPS)}

AT_MIX = [END[n] + 2 for n in ("rr", "rk", "rv")]
AT_LORA = END["wk"] + 8
AT_Z = END["rv"] + 2
AT_KK = AT_Z + 1
AT_DECAY = AT_KK + 9
AT_PAIRS = AT_DECAY + 5
RW_STEPS = [1, 2] + [0.75, 0.75, 0.65] * LEVELS + [1] * 6
LATENT_STEPS = [2, 2.5]
GN_STEPS = [1] * 8
ML_STEPS = [2.2, 2.2, 2.4] + [1, 1.3, 1, 1] * 2
SB_STEPS = [1.5, 3, 2, 2]
RW_BEATS, GN_BEATS, ML_BEATS, SB_BEATS = len(RW_STEPS), len(GN_STEPS), len(ML_STEPS), len(SB_STEPS)
STEPS = RW_STEPS + LATENT_STEPS + 3 * RW_STEPS + GN_STEPS + 4 * ML_STEPS + SBH // 2 * SB_STEPS
AT_STEP = [sum(STEPS[:n]) for n in range(len(STEPS) + 1)]


def beat_at(n):
    return AT_PAIRS + int(AT_STEP[n] / AT_STEP[-1] * (END["mg1"] - AT_PAIRS) * KC) / KC


assert END["ckv"] < beat_at(RW_BEATS)
ML_AT = [beat_at(4 * RW_BEATS + len(LATENT_STEPS) + GN_BEATS + p * ML_BEATS) for p in range(5)]
assert ML_AT[0] < END["sq"]
for p in (2, 3):
    assert ML_AT[p - 1] < END[f"uq{p}"] <= END[f"ukv{p}"] <= ML_AT[p]
assert END["sv"] <= ML_AT[4] < END["mg0"]


def merged_at(j):
    return END[f"br{j + 1}"] + 1 if j < 3 else END["bs3"] + 4


def renewed_at(j):
    return END[f"o{j}"] + (2 if j < 3 else 0)


AT_RW, AT_ML1, AT_SB = END["mg1"] + 2, END["mg1"] + 4, END["br0"]

RW_PE, RW_ACT, RW_DVE = 8 + 3 * LEVELS, 5 + 2 * LEVELS, 5 + LEVELS


def program(nc, x, norm_g, w_in, mla_q_norm_g, mla_kv_norm_g, mla_w_uq, mla_w_ukv, mla_qn_g, mla_kn_g,
            rw_mu, rw_w0, rw_w_up, rw_a0, rw_a_up, rw_k_k, rw_k_a, rw_r_k, rw_gn_g, rw_gn_b,
            w_br_sb, w_br_mla, w_br_rw, w_out, consts, out, spill):
    weights = dict(w_in=w_in, uq=mla_w_uq, ukv=mla_w_ukv, bs=w_br_sb, bm=w_br_mla, br=w_br_rw, w_out=w_out)
    with ExitStack() as ctx:
        def sb(name, shape):
            return ctx.enter_context(nc.sbuf_tensor(name, shape, F32))

        def sbr(name, shape):
            return ctx.enter_context(nc.sbuf_tensor(name, shape, F32R))

        sems = []

        def sem(name):
            s = ctx.enter_context(nc.semaphore(name))
            sems.append(s)
            return s

        con = sb("con", [P, K_END])
        xy = sb("xy", [P, HALVES, DM])
        hth, htl = sbr("ht_hi", [P, KD, SEQ]), sbr("ht_lo", [P, KD, SEQ])
        ring = sb("ring", [P, RING, KC, 512])
        wh, wl = sbr("w_hi", [P, HALF_RING, KC, 512]), sbr("w_lo", [P, HALF_RING, KC, 512])
        cqh, cql = sbr("cq_hi", [P, 4, SEQ]), sbr("cq_lo", [P, 4, SEQ])
        ckh, ckl = sbr("ckv_hi", [P, 4, SEQ]), sbr("ckv_lo", [P, 4, SEQ])
        small = sb("small", [P, 172])
        gev = sb("gev", [P, 2, HALVES, 512])
        with nc.sbuf_tensor("arena", [P, ARENA], F32) as arena:
            pass
        mth, mtl = sbr("mt_hi", [P, KD, SEQ]), sbr("mt_lo", [P, KD, SEQ])
        used = [0]

        def take(n):
            a = arena[:, used[0]:used[0] + n]
            used[0] += n
            assert used[0] <= ARENA, used[0]
            return a

        def halved(n):
            return take(n).rearrange("p (h c) -> p h c", h=HALVES)

        def units(n, u):
            return take(n).rearrange("p (u c) -> p u c", u=u)

        def again(tile_start, *makers):
            end, used[0] = used[0], tile_start
            made = [m() for m in makers]
            used[0] = end
            return made

        R = halved(3072)
        SQKV = R
        PV = halved(3072)
        S1, SIG, AA = (PV[:, :, n * 512:(n + 1) * 512] for n in range(3))
        WK = halved(384)
        PW = halved(256)
        ROWS = take(3 * 512)
        KK, S2 = xy[:, :, 0:512], xy[:, :, 1536:2048]
        at_tt = used[0]
        TT = units(1024, 2)
        XB = units(512, 4)
        LW, LA, WT, AT = again(at_tt, lambda: take(512), lambda: take(512), lambda: take(256), lambda: take(256))
        at_am = used[0]
        AM = units(2048, 4)
        MU, = again(at_am, lambda: take(1664))
        QKN, QKR, PP, PT, KRH = again(at_am, *[lambda n=n: take(n) for n in (512, 512, 384, 384, 256)])
        KRH = KRH.rearrange("p (h n c) -> p h n c", h=2, n=2)
        at_tb = used[0]
        TB = units(1024, 4)
        LM = units(512, 4)
        sb_tiles = [again(at_tb, *[lambda n=n: take(n) for n in (512, 384, 384)])]
        YU = take(256)
        ST = take(128)
        QS = take(768)
        at_mq = used[0]
        MQ = take(1536).rearrange("p (b h n c) -> p b h n c", b=2, h=2, n=2)
        S3, = again(at_mq, lambda: halved(1024))
        sb_tiles.append(again(at_mq, *[lambda n=n: take(n) for n in (512, 384, 384)]))
        QKT, AZ, LF = ([t[i] for t in sb_tiles] for i in range(3))
        at_mkv = used[0]
        MKV = take(2048).rearrange("p (b h n c) -> p b h n c", b=2, h=2, n=2)
        CQ, CKV = again(at_mkv, lambda: halved(1024), lambda: halved(1024))
        KR = halved(128)
        RG0 = halved(128)
        GR = take(128)
        used[0] = 2 * KD * SEQ
        GT = take(3072).rearrange("p (n h c) -> p n h c", n=3, h=2)
        MJ = take(2048).rearrange("p (n h c) -> p n h c", n=2, h=2)
        MG = halved(1024)

        cell = [0]

        def cells(n):
            cell[0] += n
            return small[:, cell[0] - n:cell[0]]

        ng, cqg, ckg, gq, gk, gg = cells(16), cells(4), cells(4), cells(1), cells(1), cells(1)
        ss, sums, rs, rs_q = cells(2), cells(8), cells(2), cells(2)
        kss, bon, mean, var = cells(16), cells(16), cells(16), cells(16)
        scv, css, qss, nss, krs = cells(4), cells(4), cells(4), cells(4), cells(2)
        mx, nb, den, rden = cells(2), cells(2), cells(2), cells(2)
        eps, eps_gn, bias_kk = cells(1), cells(1), cells(1)

        ident = con[:, K_ID:K_ID + P]
        level = [con[:, K_LEV + n * P:K_LEV + (n + 1) * P] for n in range(LEVELS + 1)]
        ntri, none = con[:, K_NTRI:K_NTRI + P], con[:, K_NONE:K_NONE + P]
        cosx = con[:, K_COS:K_COS + 64].rearrange("p (h c) -> p h c", h=2)
        sinx = con[:, K_SIN:K_SIN + 64].rearrange("p (h c) -> p h c", h=2)

        def psum(name):
            return ctx.enter_context(nc.psum_tensor(name, [P, 512], F32))

        D = [psum(f"D{i}") for i in range(4)]
        B = [psum(f"B{i}") for i in range(4)]

        def own(bank):
            return bank[:, 0:384].rearrange("p (a c) -> p a c", a=2)[:, :, 0:64]

        def as_pair(a):
            return a.rearrange("p (a c) -> p a c", a=2)

        full = [sem(f"ring_full{i}") for i in range(RING)]
        split_hi, split_lo = sem("weights_hi"), sem("weights_lo")
        freed = sem("ring_freed")
        dense_ev = sem("dense_out")
        small_in, rows_in, lora_in, gn_in = (sem(n + "_in") for n in ("gains", "rows", "lora", "gn"))
        mu_in = [sem("mu_latents_in"), sem("mu_in")]
        wk_shift = [sem(f"latents_shifted{i}") for i in range(2)]
        r_shift = [sem(f"rkv_shifted{i}") for i in range(6)]
        preset = sem("preset")
        act_seq, dve_seq = sem("act_order"), sem("dve_order")
        br_pe, br_act, br_dve = sem("branch_transposed"), sem("branch_hi"), sem("branch_lo")
        xt_pe, xt_act, xt_dve = sem("x_transposed"), sem("x_hi"), sem("x_lo")
        x_sq, x_sum = sem("x_squares"), sem("x_sums")
        lora_dve, lora_pe, lora_act = sem("lora_mixed"), sem("lora_pe"), sem("lora_act")
        mixed = sem("rkv_mixed")
        kk_ss, kk_rs = sem("kk_squares"), sem("kk_rstd")
        ops_done = sem("rw_operands")
        cum_pe, cum_act = sem("decay_sums"), sem("decay_exps")
        cum_dve = sem("decayed")
        rw_pe, rw_act, rw_dve, rw_pool = sem("rw_pe"), sem("rw_act"), sem("rw_dve"), sem("rw_levels")
        gn_var, gn_rs, gn_done = sem("gn_var"), sem("gn_rstd"), sem("gn_done")
        lat_act, lat_dve, lat_pe, lat_gain, lat_hi, lat_out = (sem("latents_" + n) for n in (
            "rstd", "normed", "transposed", "gain", "hi", "lo"))
        ml_sq, ml_ss, ml_rs, ml_qk = (sem("ml_" + n) for n in ("squares", "sums", "rstd", "qk"))
        ml_pe, ml_act, ml_dve = sem("ml_pe"), sem("ml_act"), sem("ml_dve")
        sb_pe, sb_act, sb_dve, sb_pool = sem("sb_pe"), sem("sb_act"), sem("sb_dve"), sem("sb_pool")
        spilled = [sem(f"gates_spilled{i}") for i in range(2)]
        silu_sig, silu_dve = sem("silu_sigmoid"), sem("silu_gated")
        gate_in = [sem(f"gate_in{i}") for i in range(3)]
        gate_sig, gate_used = sem("gate_sigmoid"), sem("gate_used")
        merged, mt_pe, mt_act, mt_dve = (sem("merged" + n) for n in ("", "_transposed", "_hi", "_lo"))
        x_in, x_new = sem("x_back"), sem("x_new")
        x_settled = sem("x_settled")
        s_done = sem("engines_done")
        s_go = ctx.enter_context(nc.semaphore("next_layer"))
        con_in = ctx.enter_context(nc.semaphore("constants_in"))
        id_in = ctx.enter_context(nc.semaphore("identity_in"))
        x_moved = [ctx.enter_context(nc.semaphore(f"x_moved{j}")) for j in range(4)]
        x_copy = ctx.enter_context(nc.semaphore("x_to_out"))
        first_w = [ctx.enter_context(nc.semaphore(f"first_weights{c}")) for c in range(LEAD)]
        first_gain, first_hi, first_lo, first_pe, first_xh, first_xl, first_sq, first_sum = (
            ctx.enter_context(nc.semaphore("first_" + n)) for n in (
                "gains", "weights_hi", "weights_lo", "x_transposed", "x_hi", "x_lo", "squares", "sums"))
        resumed = ctx.enter_context(nc.semaphore("resumed"))
        once = ctx.enter_context(nc.semaphore("set_once"))
        numbers = sorted(s.num for s in sems)
        assert numbers == list(range(numbers[0], numbers[-1] + 1))
        block = ctx.enter_context(nc.Block())

        def layer_end(eng, l):
            eng.drain().then_inc(s_done, 1)
            eng.wait_ge(s_go, l + 1)
            eng.sem_inc(resumed, 1)

        def chunk(n):
            return (CHUNKS + NEXT)[n]

        def filled(n):
            return 16 * sum(2 if chunk(m)[0] == 0 else 1 for m in range(LEAD, n + 1) if m % RING == n % RING)

        def pieces(gi, c, l):
            name, w, c0, cols, _ = GROUPS[gi]
            rows = slice(c * KC * P, (c + 1) * KC * P)
            cut = ((0, C_KR, ROPE), (ROPE, C_WD, 192)) if name == "wk" else ((0, c0, cols),)
            return [(d0, m, weights[w][l, rows, s0:s0 + m].rearrange("(k p) n -> p k n", p=P)) for d0, s0, m in cut]

        def columns(gain):
            return gain.rearrange("(k p) -> p k", p=P)

        @block.sync
        def _(sp):
            for j in range(4):
                c = slice(j * 512, (j + 1) * 512)
                if j == 0:
                    sp.dma_start(con[:, 0:P], consts[:, 0:P]).then_inc(id_in, 16)
                sp.dma_start(xy[:, :, c], x[0, :, c].rearrange("(h p) d -> p h d", p=P)).then_inc(x_moved[j], 16)
                if j == 0:
                    with nc.allow_non_contiguous_dma("gains as columns"):
                        sp.dma_start(ng, columns(norm_g[0])).then_inc(first_gain, 16)
                if j < LEAD:
                    for d0, m, src in pieces(0, j, 0):
                        sp.dma_start(ring[:, j, :, d0:d0 + m], src).then_inc(first_w[j], 16)
            with sp.Fori(0, DEPTH) as l:
                def store(j):
                    sp.wait_ge(x_new, j + 1)
                    sp.dma_start(out[0, :, j * 512:(j + 1) * 512].rearrange("(h p) d -> p h d", p=P),
                                 xy[:, :, j * 512:(j + 1) * 512]).then_inc(x_moved[j], 16)

                def row(dst, src, s):
                    sp.dma_start(dst, src.rearrange("(a n) -> a n", a=1).to_broadcast([P, dst.shape[-1]])
                                 ).then_inc(s, 16)

                following = (l + 1) & (DEPTH - 1)

                for n in range(LEAD, len(CHUNKS) + LEAD):
                    slot = n % RING
                    if n == RING:
                        sp.wait_ge(first_lo, LEAD)
                        sp.wait_ge(first_sq, 4)
                        sp.wait_ge(first_xl, 8)
                    if n == 2 * RING + 2:
                        for j in range(4):
                            sp.wait_ge(x_moved[j], 16 * (l + 1))
                            sp.sem_inc(x_settled, 1)
                    if n == 2 * RING:
                        row(MU[:, 1536:1664], rw_mu[l, 1536:1664], mu_in[0])
                    if n == 3 * RING - 1:
                        row(MU[:, 0:1536], rw_mu[l, 0:1536], mu_in[1])
                    if n == 3 * RING:
                        row(GR[:, 0:64], mla_qn_g[l, P:QK], rows_in)
                        row(GR[:, 64:128], mla_kn_g[l, P:QK], rows_in)
                        for dst, up, bias in ((LW, rw_w_up, rw_w0), (LA, rw_a_up, rw_a0)):
                            sp.dma_start(dst[0:64, :], up[l]).then_inc(lora_in, 16)
                            sp.dma_start(dst[64:65, :], bias[l].rearrange("(a n) -> a n", a=1)).then_inc(lora_in, 16)
                    for i, src in enumerate((rw_k_k[l], rw_k_a[l], rw_r_k[l].rearrange("h n -> (h n)"))):
                        if n == (4 + i) * RING:
                            row(ROWS[:, i * 512:(i + 1) * 512], src, rows_in)
                    if n == 7 * RING:
                        with nc.allow_non_contiguous_dma("gains as columns"):
                            for dst, src in ((cqg, mla_q_norm_g[l]), (ckg, mla_kv_norm_g[l]), (gq, mla_qn_g[l, 0:P]),
                                             (gk, mla_kn_g[l, 0:P]), (ng, norm_g[following])):
                                sp.dma_start(dst, columns(src)).then_inc(small_in, 16)
                    if n == AT_PAIRS + LEAD + RING:
                        sp.wait_ge(ops_done, 1)
                        row(ROWS[:, 0:512], rw_gn_g[l], gn_in)
                        row(ROWS[:, 512:1024], rw_gn_b[l], gn_in)
                    if n >= RING + LEAD:
                        sp.wait_ge(split_lo, n - RING + 1 - LEAD)
                    for d0, m, src in pieces(*chunk(n), l if n < len(CHUNKS) else following):
                        sp.dma_start(ring[:, slot, :, d0:d0 + m], src).then_inc(full[slot], 16)
                    for j in range(3):
                        if n == END[f"o{j}"] + RING:
                            store(j)
                store(3)
                layer_end(sp, l)
            for j in range(4):
                sp.wait_ge(x_moved[j], 16 * (DEPTH + 1))

        @block.gpsimd
        def _(pool):
            nc.gpsimd.memset(eps, EPS).then_inc(once, 1)
            pool.wait_ge(once, 1)
            nc.gpsimd.memset(eps_gn, 64e-5).then_inc(once, 1)
            pool.wait_ge(once, 2)
            nc.gpsimd.memset(bias_kk, float(10 * np.log(2.0))).then_inc(once, 1)
            pool.wait_ge(once, 3)
            pool.wait_ge(first_sq, 4)
            pool.wait_ge(split_lo, 2)
            pool.dma_start(con[:, P:K_END], consts[:, P:K_END]).then_inc(con_in, 16)
            pool.wait_ge(split_lo, 6)
            pool.dma_start(out[0], x[0]).then_inc(x_copy, 16)
            with pool.Fori(0, DEPTH) as l:
                for n, (t, value) in enumerate(((PV[0:1, 0, :], 0.0), (PW[0:1, 0, :], 0.0), (WT[64:65, :], 1.0),
                                                (AT[64:65, :], 1.0), (ST, 0.0))):
                    nc.gpsimd.memset(t, value).then_inc(preset, 1)
                    pool.wait_ge(preset, n + 1)
                def shift(dst, src, s):
                    pool.dma_start(dst[1:P, :, :], src[0:P - 1, :, :]).then_inc(s[0], 16)
                    pool.dma_start(dst[0:1, 1, :], src[P - 1:P, 0, :]).then_inc(s[1], 16)

                pool.wait_ge(dense_ev, GI["wk"] + 1)
                shift(PW, WK[:, :, 64:192], wk_shift)
                for i in range(3):
                    pool.wait_ge(dense_ev, GI["rr"] + i + 1)
                    shift(PV[:, :, i * 512:(i + 1) * 512], R[:, :, i * 512:(i + 1) * 512], r_shift[2 * i:2 * i + 2])

                pool.wait_ge(con_in, 16)
                pool.wait_ge(mixed, 3)
                nc.gpsimd.memset(AM, 0.0).then_inc(preset, 1)
                gate, beats = [0], [0]

                def dense_to(end):
                    while gate[0] < 12 and END[f"gate{gate[0]}"] <= end:
                        n = gate[0]
                        pool.wait_ge(dense_ev, GI[f"gate{n}"] + 1)
                        pool.dma_start(spill[n].rearrange("(h p) c -> p h c", p=P), gev[:, n % 2, :, :]
                                       ).then_inc(spilled[n % 2], 16)
                        gate[0] += 1

                def beat(count=1):
                    beats[0] += count
                    dense_to(int(beat_at(beats[0])))

                def rw_level(p, n):
                    nc.gpsimd.tensor_tensor(LM, AM[:, :, 0:P], level[n].unsqueeze(1).to_broadcast([P, 4, P]),
                                            ALU.mult).then_inc(rw_pool, 1)

                for p in range(4):
                    if p == 1:
                        beat(len(LATENT_STEPS))
                    beat()
                    pool.wait_ge(rw_dve, RW_DVE * p + 2)
                    rw_level(p, 1)
                    beat()
                    for n in range(1, LEVELS + 1):
                        beat()
                        if n < LEVELS:
                            pool.wait_ge(rw_pe, RW_PE * p + 1 + 3 * n)
                            rw_level(p, n + 1)
                        beat(2)
                    beat(6)
                beat(GN_BEATS + 4 * ML_BEATS)
                dense_to(END["sv"])
                for q in range(SBH // 2):
                    beat(2)
                    for e in range(2):
                        pool.wait_ge(sb_act, 6 * q + 5 + e)
                        for c0 in (0, 256):
                            part = AZ[e][:, c0:c0 + P]
                            last = nc.gpsimd.affine_select(out=part, in_=part, compare_op=ALU.is_gt, fill=0.0,
                                                           base=0, pattern=[[1, P]], channel_multiplier=-1)
                        last.then_inc(sb_pool, 1)
                    beat(2)
                dense_to(END["gate11"])
                for i in range(2):
                    pool.wait_ge(spilled[i], 16 * 6)
                pool.wait_ge(silu_dve, 8)
                for n in range(12):
                    if n >= 3:
                        pool.wait_ge(gate_used, n - 2)
                    gate = spill[(2 - n % 3) * 4 + n // 3].rearrange("(h p) c -> p h c", p=P)
                    pool.dma_start(GT[:, n % 3, :, :], gate
                                   ).then_inc(gate_in[n % 3], 16)
                    if n == 2:
                        pool.wait_ge(br_pe, 8)
                        pool.wait_ge(x_copy, 16)
                        pool.wait_ge(x_settled, 4)
                        pool.dma_start(xy[:], out[0].rearrange("(h p) d -> p h d", p=P)).then_inc(x_in, 16)
                pool.wait_ge(s_done, 4)
                pool.dma_reset(range(numbers[0], numbers[-1] + 1))
                pool.sem_clear(range(numbers[0], numbers[-1] + 1))
                pool.drain().then_inc(s_go, 1)

        @block.tensor
        def _(pe):
            at, beats = [0], [0]

            def mm(o, a, b, start, stop):
                return nc.tensor.matmul(o, a, b, start=start, stop=stop, skip_group_check=True)

            def stationary(name, c):
                kind = name.rstrip("0123456789")
                if kind == "bm":
                    return (ckh, ckl, 0) if c < 2 else (hth, htl, 0)
                return {"uq": (cqh, cql, 0), "ukv": (ckh, ckl, 0), "bs": (hth, htl, 0), "br": (cqh, cql, 0),
                        "o": (mth, mtl, 0)}.get(kind, (hth, htl, 0))

            def dense_to(end):
                while at[0] < end:
                    n, kk = int(at[0]), round(at[0] % 1 * KC)
                    gi, c = CHUNKS[n]
                    name, _, _, cols, blocks = GROUPS[gi]
                    if kk == 0:
                        if c == 0 and gi >= 2:
                            pe.wait_ge(dense_ev, gi - 1)
                        if c == 0 and name == "uq0":
                            pe.wait_ge(lat_out, 16)
                        if name in ("br0", "bm0", "bs0"):
                            pe.wait_ge(br_dve, n - END["sg"] + 1)
                        if name == "o0":
                            pe.wait_ge(mt_dve, c + 1)
                        if n >= LEAD:
                            pe.wait_ge(split_lo, n + 1 - LEAD)
                    sh, sl, first = stationary(name, c)
                    w = n % HALF_RING
                    k = c * KC + kk
                    for h in range(HALVES):
                        o, t = D[gi % 2 * 2 + h][:, 0:cols], slice(h * P, (h + 1) * P)
                        mm(o, sh[:, first + k, t], wh[:, w, kk, 0:cols], k == 0, False)
                        mm(o, sh[:, first + k, t], wl[:, w, kk, 0:cols], False, False)
                        last = mm(o, sl[:, first + k, t], wh[:, w, kk, 0:cols], False, k == blocks - 1)
                    if kk == KC - 1:
                        last.then_inc(freed, 1)
                    at[0] += 1 / KC

            def beat(count=1):
                for _ in range(count):
                    beats[0] += 1
                    dense_to(beat_at(beats[0]))

            def transposes(steps, col, done):
                for i, s in enumerate(steps):
                    for k in range(2):
                        for h in range(HALVES):
                            c0 = col + (2 * i + k) * P
                            last = nc.tensor.transpose(B[s % 4][:, k * 256 + h * P:k * 256 + (h + 1) * P],
                                                       xy[:, h, c0:c0 + P], ident)
                    last.then_inc(done, 1)

            def rw_pair(p):
                d0, a0 = RW_DVE * p, RW_ACT * p
                c = slice(p * P, (p + 1) * P)
                if p == 0:
                    pe.wait_ge(cum_dve, 2)
                else:
                    pe.wait_ge(rw_dve, d0)
                if p == 1:
                    pe.wait_ge(lat_out, 16)
                for h in range(HALVES):
                    for i, s in enumerate((KK, R[:, :, 0:512], AA, R[:, :, 512:1024])):
                        last = nc.tensor.transpose(B[2 + h][:, i * P:(i + 1) * P], s[:, h, c], ident)
                last.then_inc(rw_pe, 1)
                beat()
                pe.wait_ge(rw_act, a0 + 1)
                pe.wait_ge(rw_dve, d0 + 1)
                for u in range(4):
                    a, h = u // 2, u % 2
                    r = slice(64 * a, 64 * a + 64)
                    mm(B[u][:, 0:256], TT[r, h, 256:384], TT[r, h, 0:256], True, True)
                    last = mm(B[u][:, 256:512], TT[r, h, 384:512], TT[r, h, 0:256], False, True)
                last.then_inc(rw_pe, 1)
                beat()
                for n in range(1, LEVELS + 1):
                    pe.wait_ge(rw_dve, d0 + 2 + n)
                    for u in range(4):
                        last = nc.tensor.transpose(B[0][:, u * P:(u + 1) * P], TB[:, u, P:2 * P], ident)
                    last.then_inc(rw_pe, 1)
                    beat()
                    pe.wait_ge(rw_act, a0 + 2 * n)
                    pe.wait_ge(rw_pool, LEVELS * p + n)
                    for u in range(4):
                        last = mm(B[1][:, u * P:(u + 1) * P], LM[:, u, :], TB[:, u, 0:P], True, True)
                    last.then_inc(rw_pe, 1)
                    beat()
                    pe.wait_ge(rw_act, a0 + 2 * n + 1)
                    for u in range(4):
                        last = mm(B[2][:, u * P:(u + 1) * P], XB[:, u, :], TB[:, u, P:2 * P], True, True)
                    last.then_inc(rw_pe, 1)
                    beat()
                for h in range(HALVES):
                    v = R[:, h, 1024 + p * P:1024 + (p + 1) * P]
                    pe.wait_ge(rw_dve, d0 + 9 + h)
                    for a in range(2):
                        last = mm(B[0][:, a * P:(a + 1) * P], AM[:, 2 * a + h, 256:384], v, True, h == 0)
                        if h:
                            last = mm(B[0][:, a * P:(a + 1) * P], TT[:, 1, 0:P], ST, False, True)
                    last.then_inc(rw_pe, 1)
                    beat()
                    pe.wait_ge(rw_act, a0 + 14 + 2 * h)
                    for a in range(2):
                        last = mm(B[1][:, a * P:(a + 1) * P], TB[:, 2 * a + h, P:2 * P], YU[:, 0:P], True, True)
                    last.then_inc(rw_pe, 1)
                    beat()
                    pe.wait_ge(rw_act, a0 + 15 + 2 * h)
                    u = YU[:, P:2 * P]
                    if h == 0:
                        mm(B[0][:, 0:P], AA[:, 0, c], u, True, False)
                        mm(B[0][:, 0:P], R[:, 0, 512 + p * P:512 + (p + 1) * P], v, False, True)
                    for a in range(2):
                        o = B[2 + h][:, a * P:(a + 1) * P]
                        mm(o, AM[:, 2 * a + h, 128:256], u, True, False)
                        last = mm(o, AM[:, 2 * a + h, 384:512], v, False, h == 0)
                        if h:
                            last = mm(o, TT[:, 1, P:2 * P], ST, False, True)
                    last.then_inc(rw_pe, 1)
                    beat()

            def latents():
                beat()
                pe.wait_ge(rw_dve, RW_DVE)
                pe.wait_ge(lat_dve, 1)
                for i, s in enumerate((CQ, CKV)):
                    for k in range(4):
                        for h in range(HALVES):
                            o = B[2 * i + k // 2][:, k % 2 * 256 + h * P:k % 2 * 256 + (h + 1) * P]
                            last = nc.tensor.transpose(o, s[:, h, k * P:(k + 1) * P], ident)
                    last.then_inc(lat_pe, 1)
                beat()

            def mla_head(m):
                b, i = m // 2 % 2, m % 2
                if i == 0:
                    pe.wait_ge(ml_qk, m // 2 + 1)
                if m:
                    pe.wait_ge(ml_dve, 3 * m)
                for h in range(HALVES):
                    nc.tensor.transpose(B[0][:, h * P:(h + 1) * P], MQ[:, b, h, i, 0:NOPE], ident)
                    nc.tensor.transpose(B[0][:, 256 + h * P:256 + (h + 1) * P], MKV[:, b, h, i, 0:NOPE], ident)
                    nc.tensor.transpose(B[1][0:64, h * P:(h + 1) * P], MQ[:, b, h, i, NOPE:QK], ident)
                    last = nc.tensor.transpose(B[1][0:64, 256 + h * P:256 + (h + 1) * P], KRH[:, h, i, :], ident)
                last.then_inc(ml_pe, 1)
                beat()
                pe.wait_ge(ml_act, 3 * m + 1)
                pe.wait_ge(ml_dve, 3 * m + 1)
                mm(B[2][:, 0:128], QKN[:, 0:128], QKN[:, 256:384], True, False)
                mm(B[2][:, 0:128], QKR[0:66, 0:128], QKR[0:66, 256:384], False, True)
                mm(B[2][:, 128:384], QKN[:, 128:256], QKN[:, 256:512], True, False)
                mm(B[2][:, 128:384], QKR[0:66, 128:256], QKR[0:66, 256:512], False, True).then_inc(ml_pe, 1)
                beat()
                pe.wait_ge(ml_act, 3 * m + 2)
                for n in range(3):
                    last = nc.tensor.transpose(B[3][:, n * P:(n + 1) * P], PP[:, n * P:(n + 1) * P], ident)
                last.then_inc(ml_pe, 1)
                beat()
                pe.wait_ge(ml_act, 3 * m + 3)
                v = [MKV[:, b, h, i, NOPE:NOPE + VD] for h in range(2)]
                mm(B[0][:, 0:128], PT[:, 0:128], v[0], True, True)
                mm(B[0][:, 128:256], PT[:, 128:256], v[0], True, False)
                mm(B[0][:, 128:256], PT[:, 256:384], v[1], False, True).then_inc(ml_pe, 1)
                beat()

            def sb_pair(q):
                if q == 0:
                    pe.wait_ge(ml_dve, 24)
                    pe.wait_ge(dense_ev, GI["sv"] + 1)
                for e in range(2):
                    h = 2 * q + e
                    if q:
                        pe.wait_ge(sb_dve, 3 + e)
                    for i in range(2):
                        for t in range(HALVES):
                            last = nc.tensor.transpose(B[2 * e][:, i * 256 + t * P:i * 256 + (t + 1) * P],
                                                       SQKV[:, t, i * 512 + h * P:i * 512 + (h + 1) * P], ident)
                    last.then_inc(sb_pe, 1)
                beat()
                for e in range(2):
                    qk, o = QKT[e], B[2 * e + 1]
                    pe.wait_ge(sb_act, 6 * q + e + 1)
                    mm(o[:, 0:256], qk[:, 256:384], qk[:, 0:256], True, True)
                    mm(o[:, 256:384], qk[:, 384:512], qk[:, 128:256], False, True).then_inc(sb_pe, 1)
                beat()
                for e in range(2):
                    lf, o = LF[e], B[2 * e + 1]
                    pe.wait_ge(sb_dve, 4 * q + e + 1)
                    mm(o[:, 0:256], ntri, lf[:, 0:256], False, True)
                    mm(o[:, 128:256], none, lf[:, 256:384], False, True)
                    mm(o[:, 256:384], ntri, lf[:, 256:384], False, True).then_inc(sb_pe, 1)
                beat()
                for e in range(2):
                    az, o, h = AZ[e], B[2 * e], 2 * q + e
                    pe.wait_ge(sb_pool, 2 * q + e + 1)
                    v = [SQKV[:, t, 1024 + h * P:1024 + (h + 1) * P] for t in range(HALVES)]
                    mm(o[:, 0:128], az[:, 0:128], v[0], True, True)
                    mm(o[:, 128:256], az[:, 128:256], v[0], True, False)
                    mm(o[:, 128:256], az[:, 256:384], v[1], False, True).then_inc(sb_pe, 1)
                beat()

            pe.wait_ge(id_in, 16)
            for j in range(4):
                pe.wait_ge(x_moved[j], 16)
                if j >= 2:
                    pe.wait_ge(first_xl, 2 * j - 2)
                transposes((2 * j, 2 * j + 1), j * 512, first_pe)
            pe.wait_ge(first_xl, 8)
            pe.wait_ge(first_lo, LEAD)
            with pe.Fori(0, DEPTH) as l:
                at[0] = beats[0] = 0
                dense_to(AT_LORA)
                pe.wait_ge(lora_dve, 1)
                for i in range(2):
                    for h in range(HALVES):
                        last = nc.tensor.transpose(B[i][0:64, h * P:(h + 1) * P],
                                                   WK[:, h, 64 + i * 64:128 + i * 64], ident)
                last.then_inc(lora_pe, 1)
                dense_to(AT_Z)
                pe.wait_ge(lora_act, 1)
                pe.wait_ge(lora_in, 64)
                for i, (lat, up) in enumerate(((WT, LW), (AT, LA))):
                    for h in range(HALVES):
                        last = mm(B[2 * i + h][:], lat[0:65, h * P:(h + 1) * P], up[0:65, :], True, True)
                last.then_inc(lora_pe, 1)
                dense_to(AT_DECAY)
                pe.wait_ge(lora_act, 2)
                pe.wait_ge(con_in, 16)
                for h in range(HALVES):
                    mm(B[h][:], con[:, K_INC:K_INC + P], SIG[:, h, :], True, True)
                for p in range(4):
                    for h in range(HALVES):
                        last = mm(B[2][:, p:p + 1], SIG[:, h, p * P:(p + 1) * P],
                                  con[:, K_COL + h:K_COL + h + 1], h == 0, h == 1)
                last.then_inc(cum_pe, 1)
                dense_to(AT_PAIRS)
                pe.wait_ge(cum_act, 1)
                for p in range(4):
                    if p == 1:
                        latents()
                    rw_pair(p)
                pe.wait_ge(rw_dve, 4 * RW_DVE)
                beat(GN_BEATS)
                for m in range(MLH):
                    if m % 2 == 0:
                        dense_to(END[f"ukv{m // 2}"])
                        beat(3)
                    mla_head(m)
                dense_to(END["sv"])
                for q in range(SBH // 2):
                    sb_pair(q)
                dense_to(AT_RW)
                pe.wait_ge(sb_dve, 8)
                pe.wait_ge(silu_dve, 6)
                transposes((0, 1), 1536, br_pe)
                transposes((2, 3), 512, br_pe)
                dense_to(AT_ML1)
                pe.wait_ge(br_dve, 2)
                transposes((4, 5), 1024, br_pe)
                dense_to(AT_SB)
                pe.wait_ge(br_dve, 4)
                pe.wait_ge(silu_dve, 8)
                transposes((6, 7), 0, br_pe)
                for j in range(4):
                    dense_to(merged_at(j))
                    pe.wait_ge(merged, j + 1)
                    for s in range(2):
                        if j:
                            pe.wait_ge(mt_dve, 2 * j - 1 + s)
                        for k in range(2):
                            for h in range(HALVES):
                                kk = 2 * s + k
                                last = nc.tensor.transpose(B[s][:, k * 256 + h * P:k * 256 + (h + 1) * P],
                                                           MJ[:, j % 2, h, kk * P:(kk + 1) * P], ident)
                        last.then_inc(mt_pe, 1)
                for j in range(4):
                    dense_to(renewed_at(j))
                    pe.wait_ge(x_new, j + 1)
                    if j < 2:
                        pe.wait_ge(mt_dve, 8)
                    else:
                        pe.wait_ge(xt_dve, 2 * j - 2)
                    transposes((2 * j, 2 * j + 1), j * 512, xt_pe)
                layer_end(pe, l)

        @block.scalar
        def _(act):
            at, group, beats, order = [0], [0], [0], [0]

            def f(o, i, fn=ACT.Copy, **kw):
                return nc.scalar.activation(o, i, fn, **kw)

            def link(ins):
                order[0] += 1
                ins.then_inc(act_seq, 1)
                act.wait_ge(act_seq, order[0])

            def split(n):
                cols = GROUPS[chunk(n)[0]][3]
                act.wait_ge(full[n % RING], filled(n))
                if n >= HALF_RING:
                    act.wait_ge(freed, n - HALF_RING + 1)
                f(wh[:, n % HALF_RING, :, 0:cols], ring[:, n % RING, :, 0:cols]).then_inc(split_hi, 1)

            def dense_to(end):
                while at[0] < end:
                    at[0] += 1
                    split(at[0] + LEAD - 1)
                    take_out(at[0])

            def take_out(end):
                while group[0] < len(GROUPS) and END[GROUPS[group[0]][0]] <= end:
                    gi = group[0]
                    name, _, _, cols, blocks = GROUPS[gi]
                    group[0] += 1
                    kind, no = name.rstrip("0123456789"), int(name[-1]) if name[-1].isdigit() else 0
                    if name.startswith("gate"):
                        no = int(name[4:])
                    if kind in ("bs", "bm", "br"):
                        n = 3 * no + ("br", "bm", "bs").index(kind)
                        act.wait_ge(gate_in[n % 3], 16 * (n // 3 + 1))
                        f(GT[:, n % 3, :, :], GT[:, n % 3, :, :], ACT.Sigmoid).then_inc(gate_sig, 1)
                        continue
                    if kind == "o":
                        continue
                    act.wait_ge(freed, END[name])
                    bank = [D[gi % 2 * 2 + h][:, 0:cols] for h in range(HALVES)]
                    scale = [rs[:, h:h + 1] for h in range(HALVES)]
                    if kind in ("rg", "sg", "mg"):
                        n = ("rg", "mg0", "mg1", "sg").index(name)
                        if n < 2:
                            act.wait_ge(spilled[n], 16 * 6)
                        else:
                            act.wait_ge(silu_dve, 2 * (n - 1))
                        skip = 512 - cols
                        for h in range(HALVES):
                            if skip:
                                f(gev[:, n % 2, h, 0:skip], RG0[:, h, :], ACT.Sigmoid, scale=scale[h])
                            last = f(gev[:, n % 2, h, skip:512], bank[h], ACT.Sigmoid, scale=scale[h])
                        last.then_inc(silu_sig, 1)
                        continue
                    if kind == "gate":
                        if no >= 2:
                            act.wait_ge(spilled[no % 2], 16 * (no // 2))
                        if gi > GI["rg"]:
                            act.wait_ge(silu_dve, 2)
                        dst = [gev[:, no % 2, h, :] for h in range(HALVES)]
                    elif kind == "wk":
                        for h in range(HALVES):
                            f(RG0[:, h, :], bank[h][:, 192:256])
                        bank = [b[:, 0:192] for b in bank]
                        dst = [WK[:, h, :] for h in range(HALVES)]
                    elif name in ("rr", "rk", "rv"):
                        i = ("rr", "rk", "rv").index(name)
                        dst = [R[:, h, i * 512:(i + 1) * 512] for h in range(HALVES)]
                    elif name in ("sq", "sk", "sv"):
                        i = ("sq", "sk", "sv").index(name)
                        if i == 0:
                            scale = [rs_q[:, h:h + 1] for h in range(HALVES)]
                            act.wait_ge(gn_done, 1)
                        dst = [SQKV[:, h, i * 512:(i + 1) * 512] for h in range(HALVES)]
                    elif name in ("cq", "ckv"):
                        dst = [(CQ if name == "cq" else CKV)[:, h, :] for h in range(HALVES)]
                    else:
                        scale = [1.0, 1.0]
                        act.wait_ge(lat_out, 16)
                        act.wait_ge(cum_dve, 1)
                        if no >= 2:
                            act.wait_ge(ml_dve, 6 * (no - 1))
                        t = MQ if kind == "uq" else MKV
                        dst = [t[:, no % 2, h, :, :] for h in range(HALVES)]
                        bank = [b.rearrange("p (n c) -> p n c", n=2) for b in bank]
                    for h in range(HALVES):
                        last = f(dst[h], bank[h], scale=scale[h])
                    last.then_inc(dense_ev, 1)

            def beat(count=1):
                for _ in range(count):
                    beats[0] += 1
                    dense_to(int(beat_at(beats[0])))

            def rw_pair(p):
                e = RW_PE * p
                act.wait_ge(rw_pe, e + 1)
                f(TT[:, 0, :], B[2][:]).then_inc(rw_act, 1)
                beat()
                beat()
                for n in range(1, LEVELS + 1):
                    act.wait_ge(rw_pe, e + 3 * n)
                    f(TB[:, :, 0:P], B[0][:].rearrange("p (u c) -> p u c", u=4)).then_inc(rw_act, 1)
                    beat()
                    act.wait_ge(rw_pe, e + 3 * n + 1)
                    f(XB, B[1][:].rearrange("p (u c) -> p u c", u=4)).then_inc(rw_act, 1)
                    beat()
                    beat()
                for h in range(HALVES):
                    for k in range(2):
                        act.wait_ge(rw_pe, e + 21 + 3 * h + k)
                        f(as_pair(YU[:, k * P:(k + 1) * P]), own(B[k])).then_inc(rw_act, 1)
                        beat()
                    beat()

            def latents():
                act.wait_ge(dense_ev, GI["ckv"] + 1)
                for i, t in enumerate((CQ, CKV)):
                    for h in range(HALVES):
                        link(f(QS[:, 0:512], t[:, h, :], ACT.Square, accum_out=css[:, 2 * i + h:2 * i + h + 1]))
                for h in range(HALVES):
                    link(f(QS[:, 0:64], WK[:, h, 0:64], ACT.Square, accum_out=krs[:, h:h + 1]))
                link(f(css, css, ACT.Ln, scale=1.0 / LORA, bias=eps))
                f(css, css, ACT.Exp, scale=-0.5).then_inc(lat_act, 1)
                beat()
                for i, (t, g) in enumerate(((cqh, cqg), (ckh, ckg))):
                    act.wait_ge(lat_pe, i + 1)
                    act.wait_ge(small_in, 16 * 5)
                    for k in range(4):
                        f(t[:, k, :], B[2 * i + k // 2][:, k % 2 * 256:(k % 2 + 1) * 256], scale=g[:, k:k + 1]
                          ).then_inc(lat_hi, 1)
                beat()

            def mla_pair(p):
                b = p % 2
                dense_to(END[f"ukv{p}"])
                act.wait_ge(dense_ev, GI[f"ukv{p}"] + 1)
                if p:
                    act.wait_ge(ml_ss, 2 * p)
                q2 = QS.rearrange("p (h n c) -> p h n c", h=2, n=2)
                f(q2, MQ[:, b, :, :, :], ACT.Square).then_inc(ml_sq, 1)
                act.wait_ge(ml_ss, 2 * p + 1)
                f(q2[:, :, :, 0:NOPE], MKV[:, b, :, :, 0:NOPE], ACT.Square).then_inc(ml_sq, 1)
                act.wait_ge(ml_ss, 2 * p + 2)
                link(f(qss, qss, ACT.Ln, scale=1.0 / QK, bias=eps))
                link(f(nss, nss, ACT.Ln, scale=1.0 / QK, bias=eps))
                f(qss, qss, ACT.Exp, scale=-0.5)
                f(nss, nss, ACT.Exp, scale=-0.5).then_inc(ml_rs, 1)
                beat(3)
                for m in (2 * p, 2 * p + 1):
                    act.wait_ge(ml_pe, 4 * m + 1)
                    f(QKN[:, 0:256], B[0][:, 0:256], scale=gg)
                    f(QKN[:, 256:512], B[0][:, 256:512]).then_inc(ml_act, 1)
                    beat()
                    act.wait_ge(ml_dve, 3 * m + 2)
                    f(PP[:, 0:128], B[2][:, 0:128], ACT.Exp, scale=ML_SCALE, bias=nb[:, 0:1], accum_out=den[:, 0:1])
                    f(PP[:, 128:384], B[2][:, 128:384], ACT.Exp, scale=ML_SCALE, bias=nb[:, 1:2],
                      accum_out=den[:, 1:2]).then_inc(ml_act, 1)
                    beat()
                    act.wait_ge(ml_pe, 4 * m + 3)
                    f(PT, B[3][:, 0:384]).then_inc(ml_act, 1)
                    beat()
                    beat()

            def sb_pair(q):
                for e in range(2):
                    act.wait_ge(sb_pe, 8 * q + e + 1)
                    f(QKT[e], B[2 * e][:]).then_inc(sb_act, 1)
                beat()
                for e in range(2):
                    act.wait_ge(sb_pe, 8 * q + 3 + e)
                    link(f(AZ[e], B[2 * e + 1][:, 0:384], ACT.Abs))
                    link(f(AZ[e], AZ[e], ACT.Exp, scale=-1.0))
                    f(LF[e], AZ[e], ACT.Ln, bias=1.0).then_inc(sb_act, 1)
                beat()
                for e in range(2):
                    act.wait_ge(sb_pe, 8 * q + 5 + e)
                    act.wait_ge(sb_act, 6 * q + 3 + e)
                    f(AZ[e], B[2 * e + 1][:, 0:384], ACT.Exp).then_inc(sb_act, 1)
                beat()
                beat()

            def columns_hi(j, ready, done):
                for s in (2 * j, 2 * j + 1):
                    act.wait_ge(ready, s + 1)
                    for i in range(2):
                        k = 2 * s + i
                        last = f(hth[:, k, :], B[s % 4][:, i * 256:(i + 1) * 256], scale=ng[:, k:k + 1])
                    last.then_inc(done, 1)

            def squares(j, done):
                for h in range(HALVES):
                    last = f(MG[:, h, :], xy[:, h, j * 512:(j + 1) * 512], ACT.Square,
                             accum_out=sums[:, 4 * h + j:4 * h + j + 1])
                last.then_inc(done, 1)
                act.wait_ge(done, j + 1)

            act.wait_ge(once, 3)
            act.preload_act_table_set("natural_log_exp_and_others")
            act.wait_ge(first_gain, 16)
            for j in range(4):
                act.wait_ge(x_moved[j], 16)
                columns_hi(j, first_pe, first_xh)
                squares(j, first_sq)
                if j < LEAD:
                    act.wait_ge(first_w[j], 32)
                    f(wh[:, j, :, 0:256], ring[:, j, :, 0:256]).then_inc(first_hi, 1)
            act.wait_ge(first_sum, 1)
            with act.Fori(0, DEPTH) as l:
                at[0] = group[0] = beats[0] = order[0] = 0
                act.preload_act_table_set("natural_log_exp_and_others")
                link(f(ss, ss, ACT.Ln, scale=1.0 / DM, bias=eps))
                link(f(rs, ss, ACT.Exp, scale=-0.5))
                link(f(rs_q, rs, scale=SB_SCALE))
                dense_to(AT_LORA)
                act.wait_ge(lora_pe, 1)
                act.wait_ge(preset, 5)
                f(WT[0:64, :], B[0][0:64, 0:256], ACT.Tanh)
                f(AT[0:64, :], B[1][0:64, 0:256]).then_inc(lora_act, 1)
                dense_to(AT_Z)
                act.preload_act_table_set("sigmoid_and_others")
                act.wait_ge(lora_pe, 2)
                act.wait_ge(mixed, 3)
                for i, t in enumerate((SIG, AA)):
                    for h in range(HALVES):
                        last = f(t[:, h, :], B[2 * i + h][:], ACT.Sigmoid)
                last.then_inc(lora_act, 1)
                act.preload_act_table_set("natural_log_exp_and_others")
                dense_to(AT_KK + 1)
                act.wait_ge(kk_ss, 1)
                link(f(kss, kss, ACT.Ln, scale=2.0 ** 20))
                f(kss, kss, ACT.Exp, scale=-0.5, bias=bias_kk).then_inc(kk_rs, 1)
                dense_to(AT_DECAY)
                act.wait_ge(cum_pe, 1)
                act.wait_ge(ops_done, 1)
                for h in range(HALVES):
                    f(S1[:, h, :], B[h][:], ACT.Exp, scale=-1.0)
                    f(S2[:, h, :], B[h][:], ACT.Exp)
                    f(S3[:, h, :], SIG[:, h, :], ACT.Exp, scale=DECAY)
                f(scv, B[2][:, 0:4], ACT.Exp).then_inc(cum_act, 1)
                dense_to(AT_PAIRS)
                for p in range(4):
                    if p == 1:
                        latents()
                    rw_pair(p)
                beat(4)
                act.wait_ge(gn_var, 1)
                link(f(var, var, ACT.Ln, scale=1.0 / 64, bias=eps_gn))
                f(var, var, ACT.Exp, scale=-0.5).then_inc(gn_rs, 1)
                beat(GN_BEATS - 4)
                for p in range(4):
                    mla_pair(p)
                dense_to(END["sv"])
                for q in range(SBH // 2):
                    sb_pair(q)

                def branch_hi(first, t, k0):
                    for i in range(2):
                        act.wait_ge(br_pe, first + i + 1)
                        f(t[:, k0 + 2 * i:k0 + 2 * i + 2, :],
                          B[(first + i) % 4][:].rearrange("p (k t) -> p k t", k=2)).then_inc(br_act, 1)

                dense_to(AT_RW)
                branch_hi(0, cqh, 0)
                branch_hi(2, ckh, 0)
                dense_to(END["sg"])
                branch_hi(4, hth, 4)
                dense_to(AT_SB)
                branch_hi(6, hth, 0)
                for j in range(4):
                    dense_to(merged_at(j))
                    for s in range(2):
                        act.wait_ge(mt_pe, 2 * j + s + 1)
                        f(mth[:, 4 * j + 2 * s:4 * j + 2 * s + 2, :],
                          B[s][:].rearrange("p (k t) -> p k t", k=2)).then_inc(mt_act, 1)
                for j in range(4):
                    dense_to(renewed_at(j))
                    if j == 0:
                        act.preload_act_table_set("natural_log_exp_and_others")
                    act.wait_ge(x_new, j + 1)
                    squares(j, x_sq)
                    columns_hi(j, xt_pe, xt_act)
                layer_end(act, l)

        @block.vector
        def _(dve):
            v = nc.vector
            at, group, beats, order = [0], [GI["rg"]], [0], [0]

            def link(ins):
                order[0] += 1
                ins.then_inc(dve_seq, 1)
                dve.wait_ge(dve_seq, order[0])

            def tt(o, a, b, op):
                return v.tensor_tensor(o, a, b, op)

            def split(n):
                cols, slot = GROUPS[chunk(n)[0]][3], n % HALF_RING
                dve.wait_ge(split_hi, n + 1 - LEAD)
                tt(wl[:, slot, :, 0:cols], ring[:, n % RING, :, 0:cols], wh[:, slot, :, 0:cols].bitcast(F32),
                   ALU.subtract).then_inc(split_lo, 1)

            def dense_to(end):
                while at[0] < end:
                    at[0] += 1
                    split(at[0] + LEAD - 1)
                    while group[0] < len(GROUPS) and END[GROUPS[group[0]][0]] <= at[0]:
                        take_out(group[0])
                        group[0] += 1

            def beat(count=1):
                for _ in range(count):
                    beats[0] += 1
                    dense_to(int(beat_at(beats[0])))

            def take_out(gi):
                name = GROUPS[gi][0]
                kind, j = name.rstrip("0123456789"), int(name[-1]) if name[-1].isdigit() else 0
                if kind == "gate":
                    return
                bank = [D[gi % 2 * 2 + h][:] for h in range(HALVES)]
                if kind in ("rg", "sg", "mg"):
                    n = ("rg", "mg0", "mg1", "sg").index(name)
                    dve.wait_ge(silu_sig, n + 1)
                    skip = 512 - GROUPS[gi][3]
                    for h in range(HALVES):
                        parts = [(slice(skip, 512), bank[h][:, 0:512 - skip])]
                        parts += [(slice(0, skip), RG0[:, h, :])] if skip else []
                        for c, z in parts:
                            last = v.scalar_tensor_tensor(gev[:, n % 2, h, c], z, rs[:, h:h + 1], gev[:, n % 2, h, c],
                                                          ALU.mult, ALU.mult)
                    last.then_inc(dense_ev, 1)
                    dve.wait_ge(dense_ev, gi + 1)
                    c0 = (1536, 512, 1024, 0)[n]
                    y = xy[:, :, c0:c0 + 512]
                    tt(y, y, gev[:, n % 2, :, :], ALU.mult).then_inc(silu_dve, 2)
                elif kind in ("bs", "bm", "br"):
                    b = ("br", "bm", "bs").index(kind)
                    dve.wait_ge(gate_sig, 3 * j + b + 1)
                    dve.wait_ge(freed, END[name])
                    if b == 0 and j >= 2:
                        dve.wait_ge(mt_pe, 2 * (j - 1))
                    o = MJ[:, j % 2, :, :] if b == 0 else MG
                    for h in range(HALVES):
                        last = tt(o[:, h, :], GT[:, b, h, :], bank[h], ALU.mult)
                    last.then_inc(dense_ev, 1)
                    dve.wait_ge(dense_ev, gi + 1)
                    if b:
                        link(tt(MJ[:, j % 2, :, :], MJ[:, j % 2, :, :], MG, ALU.add))
                    v.sem_inc(gate_used, 1)
                    if b == 2:
                        v.sem_inc(merged, 1)
                else:
                    if j == 0:
                        dve.wait_ge(x_in, 16)
                    dve.wait_ge(freed, END[name])
                    for h in range(HALVES):
                        t = xy[:, h, j * 512:(j + 1) * 512]
                        last = tt(t, t, bank[h], ALU.add)
                    last.then_inc(x_new, 1)
                    dve.wait_ge(x_new, j + 1)
                    v.sem_inc(dense_ev, 1)

            def over_halves(row):
                return row.unsqueeze(1).to_broadcast([P, HALVES, row.shape[-1]])

            def rope(src, dst, tmp, n):
                x1, x2 = src[:, :, :, 0:32], src[:, :, :, 32:64]
                t1, t2 = (tmp[:, i * 64 * n:(i + 1) * 64 * n].rearrange("p (h n c) -> p h n c", h=2, n=n)
                          for i in range(2))
                cs, sn = (t.unsqueeze(2).to_broadcast([P, HALVES, n, 32]) for t in (cosx, sinx))
                tt(t1, x1, cs, ALU.mult)
                link(tt(t2, x2, sn, ALU.mult))
                link(tt(dst[:, :, :, 0:32], t1, t2, ALU.subtract))
                tt(t1, x1, sn, ALU.mult)
                link(tt(t2, x2, cs, ALU.mult))
                link(tt(dst[:, :, :, 32:64], t1, t2, ALU.add))

            def split_heads(t, h):
                return t[:, h, :].rearrange("p (n c) -> p n c", c=64)

            def per_head(o, t, s, op=ALU.mult):
                for h in range(HALVES):
                    last = tt(split_heads(o, h), split_heads(t, h),
                              s[:, 8 * h:8 * h + 8].unsqueeze(2).to_broadcast([P, 8, 64]), op)
                return last

            def head_sums(o, t):
                for h in range(HALVES):
                    last = v.tensor_reduce(o[:, 8 * h:8 * h + 8], split_heads(t, h), axis=X, op=ALU.add)
                return last

            def rw_pair(p):
                e = RW_PE * p
                c = slice(p * P, (p + 1) * P)
                dve.wait_ge(rw_pe, e + 1)
                v.tensor_copy(TT[:, 1, :], B[3][:]).then_inc(rw_dve, 1)
                beat()
                dve.wait_ge(rw_pe, e + 2)
                if p:
                    dve.wait_ge(rw_pool, LEVELS * p)
                for u in range(4):
                    last = v.copy_predicated(AM[:, u, :], con[:, K_RWM:K_RWM + 512].bitcast(U32), B[u][:])
                last.then_inc(rw_dve, 1)
                dve.wait_ge(rw_dve, RW_DVE * p + 2)
                link(tt(TB[:, :, P:2 * P], AM[:, :, 0:P], level[0].unsqueeze(1).to_broadcast([P, 4, P]), ALU.mult))
                tt(TB[:, :, P:2 * P], TB[:, :, P:2 * P], ident.unsqueeze(1).to_broadcast([P, 4, P]), ALU.add
                   ).then_inc(rw_dve, 1)
                beat()
                for n in range(1, LEVELS + 1):
                    beat(2)
                    dve.wait_ge(rw_pe, e + 3 * n + 2)
                    t = TB[:, :, P:2 * P]
                    tt(t, t, B[2][:].rearrange("p (u c) -> p u c", u=4), ALU.add).then_inc(rw_dve, 1)
                    beat()
                for h in range(HALVES):
                    beat(2)
                    dve.wait_ge(rw_pe, e + 23 + 3 * h)
                    if h == 0:
                        for a in range(2):
                            d = slice(64 * a, 64 * a + 64)
                            v.tensor_scalar(ST[d, d], B[0][d, d], scv[d, p:p + 1], None, ALU.mult)
                    v.tensor_copy(as_pair(S2[:, h, c]), own(B[2 + h])).then_inc(rw_dve, 1)
                    beat()

            def mla_pair(p):
                b = p % 2
                dense_to(END[f"ukv{p}"])
                dve.wait_ge(ml_sq, 2 * p + 1)
                q2 = QS.rearrange("p (a c) -> p a c", a=4)
                v.tensor_reduce(qss, q2, axis=X, op=ALU.add).then_inc(ml_ss, 1)
                dve.wait_ge(ml_sq, 2 * p + 2)
                link(v.tensor_reduce(nss, q2[:, :, 0:NOPE], axis=X, op=ALU.add))
                nss2 = nss.rearrange("p (h n) -> p h n", h=2)
                tt(nss2, nss2, krs.unsqueeze(2).to_broadcast([P, 2, 2]), ALU.add).then_inc(ml_ss, 1)
                beat()
                dve.wait_ge(ml_rs, p + 1)
                mq, mk = MQ[:, b, :, :, :], MKV[:, b, :, :, :]
                for h in range(HALVES):
                    for i in range(2):
                        k = 2 * h + i
                        v.tensor_scalar(mq[:, h, i, :], mq[:, h, i, :], qss[:, k:k + 1], None, ALU.mult)
                        v.tensor_scalar(mk[:, h, i, 0:NOPE], mk[:, h, i, 0:NOPE], nss[:, k:k + 1], None, ALU.mult)
                        last = v.tensor_scalar(KRH[:, h, i, :], KR[:, h, :], nss[:, k:k + 1], None, ALU.mult)
                link(last)
                beat()
                for h in range(HALVES):
                    last = tt(mq[:, h, :, NOPE:QK], mq[:, h, :, NOPE:QK],
                              GR[:, 0:64].unsqueeze(1).to_broadcast([P, 2, 64]), ALU.mult)
                link(last)
                rope(mq[:, :, :, NOPE:QK], QS[:, 0:256].rearrange("p (h n c) -> p h n c", h=2, n=2), QS[:, 256:512], 2)
                if p == 0:
                    v.tensor_copy(QKR[64:66, :], con[64:66, K_MASK:K_MASK + 512])
                v.tensor_copy(mq[:, :, :, NOPE:QK], QS[:, 0:256].rearrange("p (h n c) -> p h n c", h=2, n=2)
                              ).then_inc(ml_qk, 1)
                beat()
                for m in (2 * p, 2 * p + 1):
                    dve.wait_ge(ml_pe, 4 * m + 1)
                    v.tensor_copy(QKR[0:64, :], B[1][0:64, :]).then_inc(ml_dve, 1)
                    beat()
                    dve.wait_ge(ml_pe, 4 * m + 2)
                    v.reduce_max(mx[:, 0:1], B[2][:, 0:128], axis=X)
                    link(v.reduce_max(mx[:, 1:2], B[2][:, 128:384], axis=X))
                    v.tensor_scalar(nb, mx, -ML_SCALE, None, ALU.mult).then_inc(ml_dve, 1)
                    beat()
                    dve.wait_ge(ml_act, 3 * m + 2)
                    link(v.reciprocal(rden, den))
                    beat()
                    dve.wait_ge(ml_pe, 4 * m + 4)
                    c0 = 512 + m * VD
                    for h in range(HALVES):
                        last = v.tensor_scalar(xy[:, h, c0:c0 + VD], B[0][:, h * P:(h + 1) * P], rden[:, h:h + 1],
                                               None, ALU.mult)
                    last.then_inc(ml_dve, 1)
                    beat()

            def latents():
                dve.wait_ge(small_in, 16 * 5)
                tt(gg, gq, gk, ALU.mult).then_inc(lat_gain, 1)
                dve.wait_ge(lat_act, 1)
                for i, t in enumerate((CQ, CKV)):
                    for h in range(HALVES):
                        last = v.tensor_scalar(t[:, h, :], t[:, h, :], css[:, 2 * i + h:2 * i + h + 1], None, ALU.mult)
                last.then_inc(lat_dve, 1)
                beat()
                for i, (hi, lo, g) in enumerate(((cqh, cql, cqg), (ckh, ckl, ckg))):
                    dve.wait_ge(lat_hi, 4 * i + 4)
                    for k in range(4):
                        v.scalar_tensor_tensor(lo[:, k, :], B[2 * i + k // 2][:, k % 2 * 256:(k % 2 + 1) * 256],
                                               g[:, k:k + 1], hi[:, k, :].bitcast(F32), ALU.mult, ALU.subtract
                                               ).then_inc(lat_out, 2)
                beat()

            def sb_pair(q):
                beat()
                for e in range(2):
                    dve.wait_ge(sb_act, 6 * q + 3 + e)
                    link(v.scalar_tensor_tensor(LF[e], B[2 * e + 1][:, 0:384], 0.0, LF[e], ALU.max, ALU.add))
                    for c0 in (0, 256):
                        last = tt(LF[e][:, c0:c0 + P], LF[e][:, c0:c0 + P], con[:, K_RWM:K_RWM + P], ALU.mult)
                    last.then_inc(sb_dve, 1)
                beat(2)
                for e in range(2):
                    h = 2 * q + e
                    dve.wait_ge(sb_pe, 8 * q + 7 + e)
                    v.tensor_copy(xy[:, :, h * P:(h + 1) * P], B[2 * e][:, 0:256].rearrange("p (h c) -> p h c", h=2)
                                  ).then_inc(sb_dve, 1)
                beat()

            def columns_lo(j, hi, done):
                for s in (2 * j, 2 * j + 1):
                    dve.wait_ge(hi, s + 1)
                    for i in range(2):
                        k = 2 * s + i
                        last = v.scalar_tensor_tensor(htl[:, k, :], B[s % 4][:, i * 256:(i + 1) * 256], ng[:, k:k + 1],
                                                      hth[:, k, :].bitcast(F32), ALU.mult, ALU.subtract)
                    last.then_inc(done, 1)

            def sum_squares(squared, done):
                dve.wait_ge(squared, 4)
                v.tensor_reduce(ss, sums.rearrange("p (h j) -> p h j", h=2), axis=X, op=ALU.add).then_inc(done, 1)

            dve.wait_ge(first_gain, 16)
            for j in range(4):
                columns_lo(j, first_xh, first_xl)
                if j < LEAD:
                    dve.wait_ge(first_hi, j + 1)
                    tt(wl[:, j, :, 0:256], ring[:, j, :, 0:256], wh[:, j, :, 0:256].bitcast(F32), ALU.subtract
                       ).then_inc(first_lo, 1)
            sum_squares(first_sq, first_sum)
            with dve.Fori(0, DEPTH) as l:
                at[0] = beats[0] = order[0] = 0
                group[0] = GI["rg"]
                dense_to(AT_LORA)
                dve.wait_ge(mu_in[0], 16)
                for s in wk_shift:
                    dve.wait_ge(s, 16)
                lat = WK[:, :, 64:192]
                link(tt(PW, PW, lat, ALU.subtract))
                link(tt(PW, PW, over_halves(MU[:, 1536:1664]), ALU.mult))
                tt(lat, lat, PW, ALU.add).then_inc(lora_dve, 1)
                for i in range(3):
                    dense_to(AT_MIX[i])
                    dve.wait_ge(mu_in[1], 16)
                    for s in r_shift[2 * i:2 * i + 2]:
                        dve.wait_ge(s, 16)
                    c = slice(i * 512, (i + 1) * 512)
                    link(tt(PV[:, :, c], PV[:, :, c], R[:, :, c], ALU.subtract))
                    link(tt(PV[:, :, c], PV[:, :, c], over_halves(MU[:, c]), ALU.mult))
                    tt(R[:, :, c], R[:, :, c], PV[:, :, c], ALU.add).then_inc(mixed, 1)
                dense_to(AT_KK)
                dve.wait_ge(mixed, 3)
                rr, rk, rv = (R[:, :, i * 512:(i + 1) * 512] for i in range(3))
                k_k, k_a, r_k = (over_halves(ROWS[:, i * 512:(i + 1) * 512]) for i in range(3))
                gn_g, gn_b = k_k, k_a
                dve.wait_ge(rows_in, 16 * 5)
                dve.wait_ge(x_settled, 4)
                link(tt(KK, rk, k_k, ALU.mult))
                link(tt(S1, KK, KK, ALU.mult))
                dense_to(AT_KK + 1)
                link(head_sums(kss, S1))
                v.tensor_scalar(kss, kss, 1e-24, None, ALU.max).then_inc(kk_ss, 1)
                dve.wait_ge(lora_act, 2)
                for h in range(HALVES):
                    last = v.scalar_tensor_tensor(S1[:, h, :], AA[:, h, :], -1.0, ROWS[:, 512:1024], ALU.add, ALU.mult)
                link(last)
                dense_to(AT_KK + 2)
                for h in range(HALVES):
                    last = v.scalar_tensor_tensor(R[:, h, 512:1024], S1[:, h, :], 1.0, R[:, h, 512:1024],
                                                  ALU.add, ALU.mult)
                link(last)
                dve.wait_ge(kk_rs, 1)
                dense_to(AT_KK + 3)
                link(per_head(KK, KK, kss))
                dense_to(AT_KK + 4)
                link(tt(AA, AA, KK, ALU.mult))
                dense_to(AT_KK + 5)
                link(tt(S1, rr, rk, ALU.mult))
                dense_to(AT_KK + 6)
                link(tt(S1, S1, r_k, ALU.mult))
                dense_to(AT_KK + 7)
                head_sums(bon, S1).then_inc(ops_done, 1)
                dve.wait_ge(con_in, 16)
                link(tt(KR, WK[:, :, 0:64], over_halves(GR[:, 64:128]), ALU.mult))
                dst = QS[:, 640:768].rearrange("p (h n c) -> p h n c", h=2, n=1)
                rope(KR.unsqueeze(2), dst, QS[:, 512:640], 1)
                link(v.tensor_copy(KR, dst[:, :, 0, :]))
                dense_to(AT_DECAY)
                dve.wait_ge(cum_act, 1)
                for h in range(HALVES):
                    last = v.scalar_tensor_tensor(KK[:, h, :], KK[:, h, :], -1.0, S3[:, h, :], ALU.mult, ALU.mult)
                link(last)
                dense_to(AT_DECAY + 1)
                tt(rr, rr, S2, ALU.mult)
                tt(rk, rk, S1, ALU.mult)
                dense_to(AT_DECAY + 2)
                tt(AA, AA, S1, ALU.mult)
                tt(KK, KK, S2, ALU.mult).then_inc(cum_dve, 2)
                dve.wait_ge(cum_dve, 2)
                dve.wait_ge(preset, 6)
                dense_to(AT_PAIRS)
                for p in range(4):
                    if p == 1:
                        latents()
                    rw_pair(p)
                dve.wait_ge(rw_dve, 4 * RW_DVE)
                link(head_sums(mean, S2))
                link(v.tensor_scalar(mean, mean, 1.0 / 64, None, ALU.mult))
                beat()
                link(per_head(S2, S2, mean, ALU.subtract))
                beat()
                link(tt(S1, S2, S2, ALU.mult))
                beat()
                head_sums(var, S1).then_inc(gn_var, 1)
                dve.wait_ge(gn_var, 1)
                beat()
                per_head(S1, rv, bon)
                beat()
                dve.wait_ge(gn_rs, 1)
                link(per_head(S2, S2, var))
                beat()
                dve.wait_ge(gn_in, 32)
                link(tt(S2, S2, gn_g, ALU.mult))
                beat()
                link(tt(S2, S2, gn_b, ALU.add))
                tt(S2, S2, S1, ALU.add).then_inc(gn_done, 1)
                dve.wait_ge(gn_done, 1)
                beat()
                for p in range(4):
                    mla_pair(p)
                dve.wait_ge(ml_dve, 3 * MLH)
                dense_to(END["sv"])
                for q in range(SBH // 2):
                    sb_pair(q)
                dve.wait_ge(sb_dve, 2 * SBH)

                def branch_lo(first, hi, lo, k0):
                    for i in range(2):
                        dve.wait_ge(br_act, first + i + 1)
                        k = slice(k0 + 2 * i, k0 + 2 * i + 2)
                        tt(lo[:, k, :], B[(first + i) % 4][:].rearrange("p (k t) -> p k t", k=2),
                           hi[:, k, :].bitcast(F32), ALU.subtract).then_inc(br_dve, 1)

                dense_to(AT_RW)
                branch_lo(0, cqh, cql, 0)
                branch_lo(2, ckh, ckl, 0)
                dense_to(END["sg"])
                branch_lo(4, hth, htl, 4)
                dense_to(AT_SB)
                branch_lo(6, hth, htl, 0)
                for j in range(4):
                    dense_to(merged_at(j))
                    for s in range(2):
                        dve.wait_ge(mt_act, 2 * j + s + 1)
                        k = slice(4 * j + 2 * s, 4 * j + 2 * s + 2)
                        tt(mtl[:, k, :], B[s][:].rearrange("p (k t) -> p k t", k=2), mth[:, k, :].bitcast(F32),
                           ALU.subtract).then_inc(mt_dve, 1)
                for j in range(4):
                    dense_to(renewed_at(j))
                    columns_lo(j, xt_act, xt_dve)
                sum_squares(x_sq, x_sum)
                layer_end(dve, l)


NAMES = ["x", "norm_g", "w_in", "mla_q_norm_g", "mla_kv_norm_g", "mla_w_uq", "mla_w_ukv", "mla_qn_g", "mla_kn_g",
         "rw_mu", "rw_w0", "rw_w_up", "rw_a0", "rw_a_up", "rw_k_k", "rw_k_a", "rw_r_k", "rw_gn_g", "rw_gn_b",
         "w_br_sb", "w_br_mla", "w_br_rw", "w_out"]


def kernel(**inputs):
    import concourse.bacc as bacc
    from concourse.bass_utils import run_bass_kernel_spmd

    nc = bacc.Bacc("TRN2", target_bir_lowering=False, num_devices=1)
    arrays, args = {}, []
    for name in NAMES:
        a = np.ascontiguousarray(inputs[name])
        arrays["in_" + name] = a
        args.append(nc.dram_tensor("in_" + name, a.shape, mybir.dt.from_np(a.dtype), kind="ExternalInput").ap())
    arrays["in_consts"] = constants()
    args.append(nc.dram_tensor("in_consts", (P, K_END), F32, kind="ExternalInput").ap())
    args.append(nc.dram_tensor("out_x", (1, SEQ, DM), F32, kind="ExternalOutput").ap())
    args.append(nc.dram_tensor("gate_spill", (12, SEQ, 512), F32, kind="Internal").ap())
    program(nc, *args)
    r = run_bass_kernel_spmd(nc, [arrays], core_ids=[0])
    return r.results[0]["out_x"]
```
